# Optimizing a Trainium2 kernel written in Bass

```python
import math
import jax, jax.numpy as jnp
from jax import lax
import numpy as np

D_MODEL = 1024
BATCH = 1
SEQ = 1024
DEPTH = 1

CHUNK = 64
HEAD_DIM = 64
HEAD_UNIT = D_MODEL // (4 * HEAD_DIM)
SB_HEADS = HEAD_UNIT
DIFF_HEADS = HEAD_UNIT
CA_HEADS = HEAD_UNIT
SB_WIDTH = SB_HEADS * HEAD_DIM
DIFF_WIDTH = DIFF_HEADS * 2 * HEAD_DIM
CA_WIDTH = CA_HEADS * HEAD_DIM
MIX_WIDTH = SB_WIDTH + DIFF_WIDTH + CA_WIDTH
QKV_WIDTH = 3 * MIX_WIDTH
Q_BLOCK = 128
CA_LEFT_CHUNKS = 8
CA_BAND = (CA_LEFT_CHUNKS + 1) * CHUNK
CA_REL_CLIP = 128
T5_BUCKETS = 32
T5_MAX_DIST = 256
N_GROUPS = 4
EXPERTS_PER_GROUP = 8
N_EXPERTS = N_GROUPS * EXPERTS_PER_GROUP
TOP_K_INNER = 2
D_EXPERT = 512
MOE_BLOCK = 128
EPS = 1e-6

kernel_name = "hybrid_sb_diff_chunk_hmoe"

def rmsnorm(x, gain):
    x32 = x.astype(jnp.float32)
    y = x32 * lax.rsqrt(jnp.mean(x32 * x32, axis=-1, keepdims=True) + EPS)
    return (y * gain.astype(jnp.float32)).astype(x.dtype)

def split_heads(t, n_heads):
    b, s, _ = t.shape
    return t.reshape(b, s, n_heads, -1).transpose(0, 2, 1, 3)

def merge_heads(t):
    b, n, s, d = t.shape
    return t.transpose(0, 2, 1, 3).reshape(b, s, n * d)

def to_query_blocks(q):
    s, d = q.shape[-2], q.shape[-1]
    q = q.reshape(q.shape[:-2] + (s // Q_BLOCK, Q_BLOCK, d))
    return jnp.moveaxis(q, -3, 0)

def from_query_blocks(y):
    y = jnp.moveaxis(y, 0, -3)
    return y.reshape(y.shape[:-3] + (y.shape[-3] * y.shape[-2], y.shape[-1]))

def t5_bucket(rel):
    nb = T5_BUCKETS // 2
    max_exact = nb // 2
    ret = jnp.where(rel > 0, nb, 0)
    n = jnp.abs(rel)
    large = max_exact + (jnp.log(jnp.maximum(n, 1).astype(jnp.float32) / max_exact)
                         / math.log(T5_MAX_DIST / max_exact) * (nb - max_exact)).astype(jnp.int32)
    large = jnp.minimum(large, nb - 1)
    return ret + jnp.where(n < max_exact, n, large)

def stick_breaking_attention(q, k, v):
    s_len = q.shape[-2]
    scale = HEAD_DIM ** -0.5
    key_pos = jnp.arange(s_len)
    v32 = v.astype(jnp.float32)

    def block(args):
        qb, bi = args
        qpos = bi * Q_BLOCK + jnp.arange(Q_BLOCK)
        z = jnp.einsum('bhqd,bhkd->bhqk', qb, k, preferred_element_type=jnp.float32) * scale
        earlier = key_pos[None, :] < qpos[:, None]
        log_keep = jnp.where(earlier, jax.nn.log_sigmoid(-z), 0.0)
        between = lax.cumsum(log_keep, axis=3, reverse=True) - log_keep
        w = jnp.where(earlier, jnp.exp(jax.nn.log_sigmoid(z) + between), 0.0)
        return jnp.einsum('bhqk,bhkd->bhqd', w, v32)

    y = lax.map(block, (to_query_blocks(q), jnp.arange(s_len // Q_BLOCK)))
    return from_query_blocks(y)

def differential_attention(q, k, v, t5_bias, lam):
    s_len = q.shape[-2]
    scale = HEAD_DIM ** -0.5
    key_pos = jnp.arange(s_len)
    key_chunk = key_pos // CHUNK
    v32 = v.astype(jnp.float32)

    def block(args):
        qb, bi = args
        qpos = bi * Q_BLOCK + jnp.arange(Q_BLOCK)
        bias = t5_bias[t5_bucket(key_pos[None, :] - qpos[:, None])]
        bias = jnp.transpose(bias, (2, 0, 1)).astype(jnp.float32)
        allowed = key_chunk[None, :] <= (qpos // CHUNK)[:, None]
        logits = jnp.einsum('bhmqd,bhmkd->bhmqk', qb, k,
                            preferred_element_type=jnp.float32) * scale + bias[None, :, None]
        logits = jnp.where(allowed, logits, -jnp.inf)
        p = jax.nn.softmax(logits, axis=-1)
        w = p[:, :, 0] - lam * p[:, :, 1]
        return jnp.einsum('bhqk,bhkd->bhqd', w, v32)

    y = lax.map(block, (to_query_blocks(q), jnp.arange(s_len // Q_BLOCK)))
    return from_query_blocks(y)

def chunked_rel_attention(q, k, v, rel_bias):
    b, h, s_len, d = q.shape
    n_chunks = s_len // CHUNK
    scale = HEAD_DIM ** -0.5
    qc = q.reshape(b, h, n_chunks, CHUNK, d)
    pad = ((0, 0), (0, 0), (CA_LEFT_CHUNKS, 0), (0, 0), (0, 0))
    kp = jnp.pad(k.reshape(b, h, n_chunks, CHUNK, d), pad)
    vp = jnp.pad(v.reshape(b, h, n_chunks, CHUNK, d), pad)
    kb = jnp.concatenate([kp[:, :, j:j + n_chunks] for j in range(CA_LEFT_CHUNKS + 1)], axis=3)
    vb = jnp.concatenate([vp[:, :, j:j + n_chunks] for j in range(CA_LEFT_CHUNKS + 1)], axis=3)
    key_off = jnp.arange(CA_BAND) - CA_LEFT_CHUNKS * CHUNK
    rel = key_off[None, :] - jnp.arange(CHUNK)[:, None]
    bias = rel_bias[jnp.clip(rel, -CA_REL_CLIP, CA_REL_CLIP) + CA_REL_CLIP]
    bias = jnp.transpose(bias, (2, 0, 1)).astype(jnp.float32)
    band_chunk = jnp.arange(CA_BAND) // CHUNK
    valid = (jnp.arange(n_chunks)[:, None] - CA_LEFT_CHUNKS + band_chunk[None, :]) >= 0
    logits = jnp.einsum('bhnqd,bhnkd->bhnqk', qc, kb,
                        preferred_element_type=jnp.float32) * scale + bias[None, :, None]
    logits = jnp.where(valid[None, None, :, None, :], logits, -jnp.inf)
    p = jax.nn.softmax(logits, axis=-1)
    y = jnp.einsum('bhnqk,bhnkd->bhnqd', p, vb.astype(jnp.float32))
    return y.reshape(b, h, s_len, d)

def hybrid_mixer(a, w_in, w_out, t5_bias, diff_qk_norm, diff_lambda, diff_subln,
                 ca_qk_norm, ca_rel_bias, lam_init):
    b, s_len, _ = a.shape
    proj = a @ w_in
    sb, df, ca = jnp.split(proj, [3 * SB_WIDTH, 3 * SB_WIDTH + 3 * DIFF_WIDTH], axis=-1)

    qa, ka, va = [split_heads(t, SB_HEADS) for t in jnp.split(sb, 3, axis=-1)]
    ya = stick_breaking_attention(qa, ka, va)

    qd, kd, vd = jnp.split(df, 3, axis=-1)
    qd = rmsnorm(qd.reshape(b, s_len, DIFF_HEADS, 2, HEAD_DIM), diff_qk_norm[0]).transpose(0, 2, 3, 1, 4)
    kd = rmsnorm(kd.reshape(b, s_len, DIFF_HEADS, 2, HEAD_DIM), diff_qk_norm[1]).transpose(0, 2, 3, 1, 4)
    vd = split_heads(vd, DIFF_HEADS)
    lmb = diff_lambda.astype(jnp.float32)
    lam = jnp.exp(jnp.sum(lmb[0] * lmb[1])) - jnp.exp(jnp.sum(lmb[2] * lmb[3])) + lam_init
    yd = differential_attention(qd, kd, vd, t5_bias, lam)
    yd = rmsnorm(yd, diff_subln) * (1.0 - lam_init)

    qc, kc, vc = [split_heads(t, CA_HEADS) for t in jnp.split(ca, 3, axis=-1)]
    qc = rmsnorm(qc, ca_qk_norm[0])
    kc = rmsnorm(kc, ca_qk_norm[1])
    yc = chunked_rel_attention(qc, kc, vc, ca_rel_bias)

    merged = jnp.concatenate([merge_heads(ya), merge_heads(yd), merge_heads(yc)], axis=-1).astype(a.dtype)
    return merged @ w_out

def hierarchical_moe(f, wg_r, bg_r, we_r, be_r, w_gate, w_up, w_down):
    b, s_len, d = f.shape
    n_tok = b * s_len
    xt = f.reshape(n_tok, d)
    tok_idx = jnp.arange(n_tok)
    g_logits = (xt @ wg_r + bg_r).astype(jnp.float32)
    g_sel = jnp.argmax(g_logits, axis=-1)
    g_w = jax.nn.softmax(g_logits, axis=-1)[tok_idx, g_sel]
    e_logits = (xt @ we_r + be_r).astype(jnp.float32).reshape(n_tok, N_GROUPS, EXPERTS_PER_GROUP)
    e_prob = jax.nn.softmax(e_logits[tok_idx, g_sel], axis=-1)
    top_p, top_i = lax.top_k(e_prob, TOP_K_INNER)
    top_p = top_p / jnp.sum(top_p, axis=-1, keepdims=True)
    eid = (g_sel[:, None] * EXPERTS_PER_GROUP + top_i).reshape(-1)
    gate = (g_w[:, None] * top_p).reshape(-1)
    tok = jnp.repeat(tok_idx, TOP_K_INNER)
    n_asg = n_tok * TOP_K_INNER
    order = jnp.argsort(eid)
    eid_s, tok_s, gate_s = eid[order], tok[order], gate[order]
    counts = jnp.zeros((N_EXPERTS,), jnp.int32).at[eid].add(1)
    padded = (counts + MOE_BLOCK - 1) // MOE_BLOCK * MOE_BLOCK
    start = jnp.cumsum(counts) - counts
    pend = jnp.cumsum(padded)
    pstart = pend - padded
    dest = pstart[eid_s] + (jnp.arange(n_asg) - start[eid_s])
    n_rows = n_asg + N_EXPERTS * MOE_BLOCK
    n_blocks = n_rows // MOE_BLOCK
    row_tok = jnp.zeros((n_rows,), jnp.int32).at[dest].set(tok_s)
    row_gate = jnp.zeros((n_rows,), jnp.float32).at[dest].set(gate_s)
    blk_expert = jnp.minimum(jnp.searchsorted(pend, jnp.arange(n_blocks) * MOE_BLOCK, side='right'),
                             N_EXPERTS - 1)

    def expert_block(args):
        toks, gts, e = args
        xb = xt[toks]
        hid = jax.nn.silu(xb @ w_gate[e]) * (xb @ w_up[e])
        y = hid @ w_down[e]
        return y * gts[:, None].astype(y.dtype)

    y = lax.map(expert_block, (row_tok.reshape(n_blocks, MOE_BLOCK),
                               row_gate.reshape(n_blocks, MOE_BLOCK), blk_expert))
    y = y.reshape(n_rows, d)
    out = jnp.zeros((n_tok, d), y.dtype).at[row_tok].add(y)
    return out.reshape(b, s_len, d).astype(f.dtype)

def setup_inputs(seed: int = 0) -> dict:
    key = jax.random.key(seed)
    ks = jax.random.split(key, 20)
    f32 = jnp.float32

    def nrm(k, shape, scale):
        return jax.random.normal(k, shape, f32) * scale

    return {
        'x': nrm(ks[0], (BATCH, SEQ, D_MODEL), 1.0),
        't5_bias': nrm(ks[1], (T5_BUCKETS, DIFF_HEADS), 0.1),
        'attn_norm': 1.0 + nrm(ks[2], (DEPTH, D_MODEL), 0.02),
        'w_in': nrm(ks[3], (DEPTH, D_MODEL, QKV_WIDTH), D_MODEL ** -0.5),
        'diff_qk_norm': 1.0 + nrm(ks[4], (DEPTH, 2, HEAD_DIM), 0.02),
        'diff_lambda': nrm(ks[5], (DEPTH, 4, HEAD_DIM), 0.1),
        'diff_subln': 1.0 + nrm(ks[6], (DEPTH, 2 * HEAD_DIM), 0.02),
        'ca_qk_norm': 1.0 + nrm(ks[7], (DEPTH, 2, HEAD_DIM), 0.02),
        'ca_rel_bias': nrm(ks[8], (DEPTH, 2 * CA_REL_CLIP + 1, CA_HEADS), 0.1),
        'w_out': nrm(ks[9], (DEPTH, MIX_WIDTH, D_MODEL), MIX_WIDTH ** -0.5),
        'ffn_norm': 1.0 + nrm(ks[10], (DEPTH, D_MODEL), 0.02),
        'router_group_w': nrm(ks[11], (DEPTH, D_MODEL, N_GROUPS), D_MODEL ** -0.5),
        'router_group_b': nrm(ks[12], (DEPTH, N_GROUPS), 0.01),
        'router_expert_w': nrm(ks[13], (DEPTH, D_MODEL, N_EXPERTS), D_MODEL ** -0.5),
        'router_expert_b': nrm(ks[14], (DEPTH, N_EXPERTS), 0.01),
        'expert_w_gate': nrm(ks[15], (DEPTH, N_EXPERTS, D_MODEL, D_EXPERT), D_MODEL ** -0.5),
        'expert_w_up': nrm(ks[16], (DEPTH, N_EXPERTS, D_MODEL, D_EXPERT), D_MODEL ** -0.5),
        'expert_w_down': nrm(ks[17], (DEPTH, N_EXPERTS, D_EXPERT, D_MODEL), D_EXPERT ** -0.5),
    }

def reference(x, t5_bias, attn_norm, w_in, diff_qk_norm, diff_lambda, diff_subln, ca_qk_norm,
              ca_rel_bias, w_out, ffn_norm, router_group_w, router_group_b, router_expert_w,
              router_expert_b, expert_w_gate, expert_w_up, expert_w_down):
    h = x
    for l in range(DEPTH):
        lam_init = 0.8 - 0.6 * math.exp(-0.3 * l)
        a = rmsnorm(h, attn_norm[l])
        h = h + hybrid_mixer(a, w_in[l], w_out[l], t5_bias, diff_qk_norm[l], diff_lambda[l],
                             diff_subln[l], ca_qk_norm[l], ca_rel_bias[l], lam_init)
        f = rmsnorm(h, ffn_norm[l])
        h = h + hierarchical_moe(f, router_group_w[l], router_group_b[l], router_expert_w[l],
                                 router_expert_b[l], expert_w_gate[l], expert_w_up[l], expert_w_down[l])
    return h


_drawn_inputs = setup_inputs


def setup_inputs(seed=0):
    import zlib

    import numpy as np

    out = dict(_drawn_inputs(seed))
    spreads = {}
    factors = {'ca_qk_norm': 8.0,
     'ca_rel_bias': 20.58,
     'router_group_b': 12.213,
     'router_expert_b': 15.423,
     'diff_subln': 3.133,
     'ffn_norm': 3.533}
    for name, (base, spread) in spreads.items():
        noise = np.random.default_rng([zlib.crc32(name.encode()), seed]).standard_normal(out[name].shape)
        drawn = base * np.exp(spread * noise) if base else spread * noise
        out[name] = __import__('jax').numpy.asarray(drawn.astype(out[name].dtype))
    for name, factor in factors.items():
        out[name] = (out[name] * factor).astype(out[name].dtype)
    return out
```

```python
import math
from contextlib import ExitStack

import numpy as np

import concourse.bass as bass
from concourse import mybir

ALU = mybir.AluOpType
ACT = mybir.ActivationFunctionType
AX = mybir.AxisListType
F32 = mybir.dt.float32
BF16 = mybir.dt.bfloat16
I32 = mybir.dt.int32
U32 = mybir.dt.uint32

P = 128
BANK = 512
EPS = 1e-6
MASKED = -1e30
LOWEST = -3e38
LAM_INIT = 0.8 - 0.6 * math.exp(-0.3 * 0)
HEAD = 64
SCALE = HEAD ** -0.5
T5_BUCKETS, T5_MAX_DIST = 32, 256
CLIP = 128
BAND = 4
TOP = 2


def t5_runs(lo, hi):
    half = T5_BUCKETS // 2
    exact = half // 2
    runs = []
    for rel in range(lo, hi):
        n = abs(rel)
        if n < exact:
            b = n
        else:
            b = exact + int(np.float32(np.log(np.float32(n / exact))) / np.float32(math.log(T5_MAX_DIST / exact))
                            * np.float32(half - exact))
            b = min(b, half - 1)
        b += half if rel > 0 else 0
        if runs and runs[-1][2] == b:
            runs[-1][1] = rel + 1
        else:
            runs.append([rel, rel + 1, b])
    return runs


def hybrid_block(nc, x, t5_bias, attn_norm, w_in, diff_qk_norm, diff_lambda, diff_subln, ca_qk_norm,
                 ca_rel_bias, w_out, ffn_norm, group_w, group_b, expert_w, expert_b, w_gate, w_up, w_down, out):
    _, S, D = x.shape
    QKV = w_in.shape[2]
    NE, _, DE = w_gate.shape[1:]
    NG = group_w.shape[2]
    EG = NE // NG
    T = S // P
    KD = D // P
    KE = DE // P
    CH = QKV // BANK
    NR = NG + NE
    NB = NE + TOP * S // P
    SBW = D // 4
    SB_Q, SB_K, SB_V = 0, SBW, 2 * SBW
    DF_Q, DF_K, DF_V = 3 * SBW, 5 * SBW, 7 * SBW
    CA_Q, CA_K, CA_V = 9 * SBW, 10 * SBW, 11 * SBW
    SB_O, DF_O, CA_O = 0, SBW, 3 * SBW
    SB_PAIRS, DF_PAIRS, CA_PAIRS = SBW // P, 2 * SBW // P, SBW // P
    NH = ca_rel_bias.shape[2]

    T5_LINE = S + P - 1
    CA_W = (BAND + 1) * P
    CA_LINE = CA_W + P - 1

    x_rows = x[0]
    t5_line = nc.dram_tensor("t5_line", [NH, T5_LINE + 1], F32).ap()
    ca_line = nc.dram_tensor("ca_line", [NH, CA_LINE + 1], F32).ap()
    f_rows = nc.dram_tensor("f_rows", [S, D], F32).ap()
    y_rows = nc.dram_tensor("y_rows", [TOP * S, D], F32).ap()

    with ExitStack() as ctx:
        def sb(name, shape, dt=F32):
            return ctx.enter_context(nc.sbuf_tensor(name, shape, dt))

        def sem(name):
            return ctx.enter_context(nc.semaphore(name))

        arena = sb("arena", [P, 49152])

        def part(first, *dims, dt=F32):
            n = int(np.prod(dims)) * (2 if dt == BF16 else 4) // 4
            v = arena[:, first:first + n]
            if dt != F32:
                v = v.bitcast(dt)
            if len(dims) == 1:
                return v
            names = "abcd"[:len(dims)]
            sizes = {c: d for c, d in zip(names[1:], dims[1:])}
            return v.rearrange(f"p ({' '.join(names)}) -> p {' '.join(names)}", **sizes)

        proj = part(0, T, QKV)
        x_all = part(16384, T, D)
        aT = part(24576, KD, S)
        merged = part(24576, T, D)
        w_in_ring = part(32768, 2, KD, BANK)
        a_buf = part(40960, 2, D)
        norm_junk = part(43008, D)
        t5_sb = part(44032, T5_LINE + 1)[0:NH]
        ca_sb = part(45440, CA_LINE + 1)[0:NH]
        lam_in = part(46208, 4 * HEAD)
        lam_junk = part(46464, HEAD)
        lines_in = part(46592, T5_BUCKETS + 2 * CLIP + 1)[0:NH]
        q_stage, k_stage = part(32768, T, P), part(33792, T, P)
        qT, kT = part(34816, S), part(35840, S)
        bias_tiles = part(36864, 2, S)
        pt_sb = part(38912, 2, BANK)
        work = part(40960, 6, S)
        squares = part(47104, 2, T, P)
        w_out_sb = part(0, KD, D)
        h2 = part(32768, T, D)
        m_stage = part(22528, 2, D)
        mT = part(40960, 2, KD, P)
        f_buf = part(43008, 2, D)
        fT = part(45056, KD, P)
        out_junk = part(46080, D)
        gu_ring = part(0, 2, KD, 2 * DE)
        gu_first = part(8192, KD, 2 * DE)
        dn_ring = part(2 * KD * 2 * DE, 3, KE, D)
        xg = part(40960, D)
        xT = part(41984, KD, P)
        silu = part(43008, DE)
        hid = part(43520, DE)
        hT = part(44032, KE, P)
        y_sb = part(44544, D)
        pos_hot = part(28672, TOP, T, P, dt=BF16)
        blk_hot = part(29696, TOP, T, NB)
        blk_vals = part(30464, TOP, T, 3 * NB, dt=BF16).rearrange("p c t (a b) -> p c t a b", a=3)
        hot = part(31616, TOP, T, NE)
        picked = part(32128, TOP, T, NE)
        be_cmp = part(45568, NB, NE)[0:1]
        e_all = part(47104, T, NG, EG)
        row_f = part(47488, 2, NB)
        logits = part(47616, T, NR)
        y_tiles = part(0, T, TOP, D)

        ident = sb("ident", [P, P])
        attn_gain = sb("attn_gain", [P, D])
        subln = sb("subln", [P, 2 * HEAD])
        qk_gain = sb("qk_gain", [P, 4])
        lam_sum = sb("lam_sum", [P, 2])
        lam_exp = sb("lam_exp", [P, 2])
        neg_lam = sb("neg_lam", [P, 1])
        ones = sb("ones", [P, 1])
        mhalf = sb("mhalf", [P, 2 * T * 2])
        ss = sb("ss", [P, T])
        ms = sb("ms", [P, T])
        rstd = sb("rstd", [P, T])
        qk_ss = sb("qk_ss", [P, 2, 2 * T])
        qk_ms = sb("qk_ms", [P, 2, 2 * T])
        qk_rstd = sb("qk_rstd", [P, 2, 2 * T])
        low = sb("low", [P, 4, 2])
        total = sb("total", [P, 4, 2])
        inv = sb("inv", [P, 4, 2])
        mix = sb("mix", [P, 4])
        yd = sb("yd", [P, 2, 2 * HEAD])
        yd_junk = sb("yd_junk", [P, 2 * HEAD])
        yd_ss = sb("yd_ss", [P, 2])
        yd_ms = sb("yd_ms", [P, 2])
        yd_rstd = sb("yd_rstd", [P, 2])
        w_r = sb("w_r", [P, KD, NR])
        b_r = sb("b_r", [P, NR])
        g8 = sb("g8", [P, T, 8])
        g_top = sb("g_top", [P, T, 8])
        g_idx = sb("g_idx", [P, T, 8], U32)
        e_top = sb("e_top", [P, T, 8])
        e_idx = sb("e_idx", [P, T, 8], U32)
        g_sel = sb("g_sel", [P, T])
        g_exp = sb("g_exp", [P, T, NG])
        g_sum = sb("g_sum", [P, T])
        g_w = sb("g_w", [P, T])
        g_hot = sb("g_hot", [P, T, NG])
        e8 = sb("e8", [P, T, EG])
        e_gap = sb("e_gap", [P, T])
        e_sec = sb("e_sec", [P, T])
        e_den = sb("e_den", [P, T])
        e_inv = sb("e_inv", [P, T])
        gates = sb("gates", [P, T, TOP])
        e_idf = sb("e_idf", [P, T, TOP])
        eid = sb("eid", [P, T, TOP])
        hot_sum = sb("hot_sum", [P, T, NE], BF16)
        iota_f = sb("iota_f", [P, P])
        part_id = sb("part_id", [P, 1])
        tri = sb("tri", [P, P], BF16)
        ones_b = sb("ones_b", [P, P], BF16)
        tile_id = sb("tile_id", [P, T])
        cnt_i = sb("cnt_i", [P, NE], I32)
        nblk = sb("nblk", [P, NE])
        blk_end = sb("blk_end", [P, NE])
        blk_start = sb("blk_start", [P, NE])
        rank = sb("rank", [P, TOP, T])
        rank_i = sb("rank_i", [P, TOP, T], I32)
        hi_i = sb("hi_i", [P, TOP, T], I32)
        lo_i = sb("lo_i", [P, TOP, T], I32)
        hi_f = sb("hi_f", [P, TOP, T])
        lo_f = sb("lo_f", [P, TOP, T])
        first_blk = sb("first_blk", [P, TOP, T])
        blk = sb("blk", [P, TOP, T])
        empty = sb("empty", [P, NB])
        row_i = sb("row_i", [P, 2, NB], I32)
        be_f = sb("be_f", [1, NB])
        be_i = sb("be_i", [1, NB], I32)
        last_i = sb("last_i", [1, 1], I32)
        tok_col = sb("tok_col", [P, 1], I32)
        row_col = sb("row_col", [P, 1], I32)

        psum = ctx.enter_context(nc.psum_tensor("psum", [P, 8, BANK], F32))

        def banks(first, n):
            return psum[:, first:first + n, :].rearrange("p a b -> p (a b)")

        s_const = sem("s_const")
        s_ident = sem("s_ident")
        s_waits_met = sem("s_waits_met")
        s_pool_const = sem("s_pool_const")
        s_lines_in = sem("s_lines_in")
        s_lines = sem("s_lines")
        s_lines_out = sem("s_lines_out")
        s_dve_const = sem("s_dve_const")
        s_lam_sum = sem("s_lam_sum")
        s_lam_exp = sem("s_lam_exp")
        s_lam = sem("s_lam")
        s_x = [sem(f"s_x{i}") for i in range(4)]
        n_sq = sem("n_sq"); n_ms = sem("n_ms"); n_rstd = sem("n_rstd"); n_a = sem("n_a")
        n_tp = sem("n_tp"); n_aT_act = sem("n_aT_act"); n_aT_dve = sem("n_aT_dve")
        w_landed = [sem(f"w_landed{i}") for i in range(2)]
        acc_ready = sem("acc_ready"); acc_act = sem("acc_act"); acc_dve = sem("acc_dve")

        def attention_sems(kind):
            names = ["squared", "qk_ms_ready", "qk_rstd_ready", "staged", "q_tp", "k_tp", "qT_ready",
                     "kT_ready", "z_ready", "z_read", "p_ready", "pt0", "pt1", "pt_sb0", "pt_sb1",
                     "o_ready", "o_read", "bias_landed", "bias_ready", "abs_done", "exp_done", "lp_ready",
                     "sp_ready", "sp_masked", "scanned", "w_exp", "summed", "inverse", "mixed", "yd_ready",
                     "yd_ss_ready", "yd_ms_ready", "yd_rstd_ready", "merged_ready"]
            used = {"sb": set(names) - {"squared", "qk_ms_ready", "qk_rstd_ready", "bias_landed", "bias_ready",
                                        "summed", "inverse", "mixed", "yd_ready", "yd_ss_ready", "yd_ms_ready",
                                        "yd_rstd_ready", "merged_ready"},
                    "df": set(names) - {"abs_done", "exp_done", "lp_ready", "sp_ready", "sp_masked", "scanned",
                                        "w_exp"},
                    "ca": set(names) - {"abs_done", "exp_done", "lp_ready", "sp_ready", "sp_masked", "scanned",
                                        "w_exp", "mixed", "yd_ready", "yd_ss_ready", "yd_ms_ready",
                                        "yd_rstd_ready", "merged_ready"}}[kind]
            return {n: sem(f"{kind}_{n}") for n in names if n in used}

        SBS, DFS, CAS = attention_sems("sb"), attention_sems("df"), attention_sems("ca")

        s_wout = sem("s_wout"); s_x_again = sem("s_x_again")
        c_stage = sem("c_stage"); c_tp = sem("c_tp"); c_mT_act = sem("c_mT_act"); c_mT_dve = sem("c_mT_dve")
        c_acc = sem("c_acc"); c_h2 = sem("c_h2"); c_sq = sem("c_sq"); c_ms = sem("c_ms"); c_rstd = sem("c_rstd")
        c_f = sem("c_f"); c_fsaved = sem("c_fsaved"); c_ftp = sem("c_ftp")
        c_fT_act = sem("c_fT_act"); c_fT_dve = sem("c_fT_dve"); c_lg = sem("c_lg"); c_logits = sem("c_logits")
        r_dve = sem("r_dve"); r_gexp_in = sem("r_gexp_in"); r_gexp = sem("r_gexp"); r_esec_in = sem("r_esec_in")
        r_esec = sem("r_esec"); r_hot = sem("r_hot"); r_counted = sem("r_counted"); r_vals = sem("r_vals")
        r_rows = sem("r_rows"); r_table = sem("r_table"); r_idx = sem("r_idx"); s_gain = sem("s_gain")
        gate_landed = sem("gate_landed"); up_landed = sem("up_landed"); down_landed = sem("down_landed")
        tok_ready = sem("tok_ready"); row_ready = sem("row_ready"); xg_zero = sem("xg_zero"); xg_landed = sem("xg_landed")
        x_tp = sem("x_tp"); xT_act = sem("xT_act"); xT_dve = sem("xT_dve")
        g_ready = sem("g_ready"); u_ready = sem("u_ready"); silu_ready = sem("silu_ready")
        h_ready = sem("h_ready"); h_tp = sem("h_tp"); hT_ready = sem("hT_ready")
        y_ready = sem("y_ready"); y_act = sem("y_act"); y_dve = sem("y_dve"); y_stored = sem("y_stored")
        s_y = s_x
        f_part = sem("f_part"); f_out = sem("f_out"); out_stored = sem("out_stored")

        class Plan:

            def __init__(self, kind, s, q, k, v, o, pairs):
                self.kind, self.s, self.q, self.k, self.v, self.o, self.pairs = kind, s, q, k, v, o, pairs
                self.units = 2 * T
                self.results = T if kind == "df" else 2 * T

            def tile(self, r):
                return r if self.kind == "df" else r // 2

            def keys(self, t):
                first = max(0, t - BAND) if self.kind == "ca" else 0
                return first, t + 1 - first

            def groups(self, r):
                n = self.keys(self.tile(r))[1]
                return [list(range(g, min(g + 4, n))) for g in range(0, n, 4)]

            def group_no(self, g, r):
                has = [len(self.groups(i)) > g for i in range(self.results)]
                return sum(has[:r]), sum(has)

        SB = Plan("sb", SBS, SB_Q, SB_K, SB_V, SB_O, SB_PAIRS)
        DF = Plan("df", DFS, DF_Q, DF_K, DF_V, DF_O, DF_PAIRS)
        CA = Plan("ca", CAS, CA_Q, CA_K, CA_V, CA_O, CA_PAIRS)

        def cols(first, p, width=P, step=P):
            return bass.ds(p * step + first, width)

        def wait_alone(eng, semaphore, value):
            eng.wait_ge(semaphore, value)
            eng.sem_inc(s_waits_met, 1)

        def wait_slot(eng, a, p, r, slots):
            back = r - slots if r >= slots else max(i for i in range(a.results) if i % slots == r % slots)
            g = len(a.groups(back)) - 1
            before, per = a.group_no(g, back)
            eng.wait_ge(a.s[f"pt{g}"], p * per + (before + 1 + (per if r >= slots else 0)))

        block = ctx.enter_context(nc.Block())

        @block.sync
        def _(sp):
            for i in range(4):
                sp.dma_start(x_all[:, i, :], x_rows[i * P:(i + 1) * P, :]).then_inc(s_x[i], 16)
            sp.dma_start(attn_gain[:, :], attn_norm.to_broadcast([P, D])).then_inc(s_gain, 16)
            for i in range(4):
                sp.wait_ge(s_x[i], 16)
                sp.dma_start(x_all[:, 4 + i, :], x_rows[(4 + i) * P:(5 + i) * P, :]).then_inc(s_x[i], 16)
            w_in_tiles = w_in[0].rearrange("(k p) n -> p k n", p=P)
            for j in range(2):
                sp.dma_start(w_in_ring[:, j, :, :], w_in_tiles[:, :, j * BANK:(j + 1) * BANK]).then_inc(w_landed[j], 16)
            with sp.Fori(1, CH // 2) as i:
                for j in range(2):
                    sp.wait_ge(acc_ready, i * 2 * T + (j - 1) * T)
                    sp.dma_start(w_in_ring[:, j, :, :], w_in_tiles[:, :, bass.ds(i * 2 * BANK + j * BANK, BANK)]) \
                        .then_inc(w_landed[j], 16)

            def bias_loads(a, line, width, tiles):
                with sp.Fori(0, a.pairs) as p:
                    sp.wait_ge(a.s["z_read"], p * a.units + 2)
                    for m in range(tiles):
                        src = bass.AP(line.tensor, (p * tiles + m) * line.shape[1], [[1, P], [1, width]])
                        sp.dma_start(bias_tiles[:, m, 0:width], src).then_inc(a.s["bias_landed"], 16)

            sp.wait_ge(n_a, T)
            sp.dma_start(attn_gain[:, :], ffn_norm.to_broadcast([P, D])).then_inc(s_gain, 16)
            sp.wait_ge(s_lines_out, 32)
            sp.wait_ge(acc_act, 2 + CH * T // 2)
            sp.wait_ge(acc_dve, 2 + CH * T // 2)
            bias_loads(DF, t5_line, S, 1)
            sp.wait_ge(DFS["merged_ready"], DF_PAIRS * DF.results)
            bias_loads(CA, ca_line, CA_W, 2)

            sp.wait_ge(CAS["o_read"], 2 + CA.pairs * CA.results)
            sp.wait_ge(CAS["staged"], 2 * (CA.pairs + 1))
            sp.dma_start(w_out_sb, w_out[0].rearrange("(k p) n -> p k n", p=P)).then_inc(s_wout, 16)
            for j in range(2):
                half = T // 2 * P
                sp.dma_start(h2[:, j * (T // 2):(j + 1) * (T // 2), :],
                             x_rows[j * half:(j + 1) * half, :].rearrange("(t p) d -> p t d", p=P)).then_inc(s_x_again, 16)
            sp.dma_start(gu_first[:, :, 0:DE], w_gate[0, 0].rearrange("(k p) n -> p k n", p=P)).then_inc(gate_landed, 16)
            sp.dma_start(gu_first[:, :, DE:2 * DE], w_up[0, 0].rearrange("(k p) n -> p k n", p=P)).then_inc(up_landed, 16)
            sp.dma_start(dn_ring[:, 0, :, :], w_down[0, 0].rearrange("(k p) n -> p k n", p=P)).then_inc(down_landed, 16)

            sp.wait_ge(r_idx, 1)
            sp.wait_ge(c_acc, 2 * T)
            last_b = sp.value_load(last_i[0:1, 0:1], min_val=NE - 1, max_val=NB - 2)
            with sp.Fori(1, last_b + 1) as b:
                e = sp.value_load(be_i[0:1, bass.ds(b, 1)], min_val=0, max_val=NE - 1)
                slot = (b + 1) % 2
                sp.wait_ge(xg_landed, b * 16 + 16)
                wait_alone(sp, u_ready, b)
                sp.wait_ge(gate_landed, b * 16)
                sp.dma_start(gu_ring[:, slot, :, 0:DE], w_gate[0, e, :, :].rearrange("(k p) n -> p k n", p=P)) \
                    .then_inc(gate_landed, 16)
                sp.wait_ge(up_landed, b * 16)
                sp.dma_start(gu_ring[:, slot, :, DE:2 * DE], w_up[0, e, :, :].rearrange("(k p) n -> p k n", p=P)) \
                    .then_inc(up_landed, 16)
                sp.wait_ge(y_ready, b * 2)
                sp.wait_ge(down_landed, b * 16)
                sp.dma_start(dn_ring[:, b % 3, :, :], w_down[0, e, :, :].rearrange("(k p) n -> p k n", p=P)) \
                    .then_inc(down_landed, 16)

            sp.wait_ge(y_stored, last_b * 16 + 16)
            sp.wait_ge(y_ready, last_b * 2 + 6)
            y_t = y_rows.rearrange("(t c p) d -> p t c d", p=P, c=TOP)
            for i in range(4):
                sp.dma_start(y_tiles[:, i, :, :], y_t[:, i, :, :]).then_inc(s_y[i], 16)
            for i in range(4):
                sp.wait_ge(s_y[i], 48)
                sp.dma_start(y_tiles[:, 4 + i, :, :], y_t[:, 4 + i, :, :]).then_inc(s_y[i], 16)
            out_t = out[0].rearrange("(t p) d -> t p d", p=P)
            for t in range(T):
                sp.wait_ge(f_out, t + 1)
                sp.dma_start(out_t[t], h2[:, t, :]).then_inc(out_stored, 16)
            sp.wait_ge(out_stored, 16 * T)

        @block.tensor
        def _(pe):
            for a in (SB, DF, CA):
                for g in range(2):
                    pe.sem_inc(a.s[f"pt{g}"], a.group_no(g, 0)[1])
            pe.sem_inc(u_ready, 1)
            pe.sem_inc(y_ready, 4)
            pe.wait_ge(s_ident, 2)

            def transpose_tile(src, first_bank):
                for k in range(KD):
                    last = pe.transpose(psum[:, first_bank + k // 4, (k % 4) * P:(k % 4 + 1) * P],
                                        src[:, k * P:(k + 1) * P], ident[:, :])
                return last

            with pe.Fori(0, T // 2) as i:
                for j in range(2):
                    pe.wait_ge(n_a, i * 2 + (j + 1))
                    pe.wait_ge(n_aT_act, i * 2 + (j + 1))
                    pe.wait_ge(n_aT_dve, i * 2 + (j + 1))
                    transpose_tile(a_buf[:, j, :], 2 * j).then_inc(n_tp, 1)

            with pe.Fori(0, CH // 2) as i:
                for j in range(2):
                    pe.wait_ge(w_landed[j], i * 16 + 16)
                    for t in range(T):
                        pe.wait_ge(n_aT_act, 2 + t + 1)
                        pe.wait_ge(n_aT_dve, 2 + t + 1)
                        pe.wait_ge(acc_act if t % 2 == 0 else acc_dve, i * T + (j * T // 2 + t // 2 + 1))
                        for k in range(KD):
                            last = pe.matmul(psum[:, 4 + t % 4, :], aT[:, k, t * P:(t + 1) * P], w_in_ring[:, j, k, :],
                                             start=(k == 0), stop=(k == KD - 1))
                        last.then_inc(acc_ready, 1)

            def transpose_qk(a, p):
                pe.wait_ge(a.s["staged"], p * 2 + 2)
                pe.wait_ge(a.s["z_read"], p * a.units + 2)
                for stage, first, done in ((q_stage, 0, "q_tp"), (k_stage, 2, "k_tp")):
                    for t in range(T):
                        last = pe.transpose(psum[:, first + t // 4, (t % 4) * P:(t % 4 + 1) * P], stage[:, t, :],
                                            ident[:, :])
                    last.then_inc(a.s[done], 1)
                pe.wait_ge(a.s["qT_ready"], p * 2 + 2)
                pe.wait_ge(a.s["kT_ready"], p * 2 + 2)

            def logits_of(a, p, u):
                t, m = u // 2, u % 2
                first, n = a.keys(t)
                pe.wait_ge(a.s["z_read"], p * a.units + (u + 1))
                rows = slice(HEAD * m, HEAD * (m + 1))
                for c in range(0, n * P, BANK):
                    w = min(BANK, n * P - c)
                    last = pe.matmul(psum[:, 2 * m + c // BANK, 0:w], qT[rows, t * P:(t + 1) * P],
                                     kT[rows, first * P + c:first * P + c + w], start=True, stop=True)
                last.then_inc(a.s["z_ready"], 1)

            def transpose_weights(a, p, r, weights):
                pe.wait_ge(a.s["p_ready"], p * a.results + (r + 1))
                groups = a.groups(r)
                for g, tiles in enumerate(groups):
                    before, per = a.group_no(g, r)
                    pe.wait_ge(a.s[f"pt_sb{g}"], p * per + (before + 1))
                    for c in tiles:
                        last = pe.transpose(psum[:, 4 + g, (c % 4) * P:(c % 4 + 1) * P], weights[:, c * P:(c + 1) * P],
                                            ident[:, :])
                    last.then_inc(a.s[f"pt{g}"], 1)

            def result_of(a, p, r):
                first, n = a.keys(a.tile(r))
                width = 2 * HEAD if a.kind == "df" else HEAD
                head = 0 if a.kind == "df" else HEAD * (r % 2)
                groups = a.groups(r)
                pe.wait_ge(a.s["o_read"], p * a.results + (r + 1))
                for g, tiles in enumerate(groups):
                    before, per = a.group_no(g, r)
                    pe.wait_ge(a.s[f"pt_sb{g}"], p * per + (before + 2))
                    for c in tiles:
                        last = pe.matmul(psum[:, 6 + r % 2, 0:width], pt_sb[:, g, (c % 4) * P:(c % 4 + 1) * P],
                                         proj[:, first + c, cols(a.v + head, p, width)], start=(c == 0), stop=(c == n - 1))
                last.then_inc(a.s["o_ready"], 1)

            pe.wait_ge(acc_act, 2 + CH * T // 2)
            pe.wait_ge(acc_dve, 2 + CH * T // 2)
            with pe.Fori(0, SB.pairs) as p:
                transpose_qk(SB, p)
                for s in range(SB.units + 2):
                    if s < SB.units:
                        logits_of(SB, p, s)
                    if s >= 2:
                        transpose_weights(SB, p, s - 2, work[:, (s - 2) % 2, :])
                        result_of(SB, p, s - 2)
            pe.wait_ge(SBS["o_read"], 2 + SB.pairs * SB.results)
            with pe.Fori(0, DF.pairs) as p:
                transpose_qk(DF, p)
                for s in range(T + 2):
                    if s >= 2:
                        transpose_weights(DF, p, s - 2, work[:, 2 * ((s - 2) % 3), :])
                    if s < T:
                        logits_of(DF, p, 2 * s)
                        logits_of(DF, p, 2 * s + 1)
                    if s >= 2:
                        result_of(DF, p, s - 2)
            pe.wait_ge(DFS["merged_ready"], DF.pairs * DF.results)
            with pe.Fori(0, CA.pairs) as p:
                transpose_qk(CA, p)
                for s in range(CA.units + 2):
                    if s >= 2:
                        transpose_weights(CA, p, s - 2, work[:, (s - 2) % 4, :])
                    if s < CA.units:
                        logits_of(CA, p, s)
                    if s >= 2:
                        result_of(CA, p, s - 2)
            pe.wait_ge(CAS["o_read"], 2 + CA.pairs * CA.results)

            def merged_tile(i, j):
                pe.wait_ge(c_stage, i * 2 + (j + 1))
                pe.wait_ge(c_mT_act, i * 2 + (j + 1))
                pe.wait_ge(c_mT_dve, i * 2 + (j + 1))
                transpose_tile(m_stage[:, j, :], 0).then_inc(c_tp, 1)

            def out_tile(i, j):
                pe.wait_ge(c_mT_act, i * 2 + (j + 2))
                pe.wait_ge(c_mT_dve, i * 2 + (j + 2))
                for n in range(2):
                    pe.wait_ge(c_h2, i * 4 + (2 * j + n + 1))
                    for k in range(KD):
                        last = pe.matmul(psum[:, 2 + n, :], mT[:, j, k, :], w_out_sb[:, k, n * BANK:(n + 1) * BANK],
                                         start=(k == 0), stop=(k == KD - 1))
                    last.then_inc(c_acc, 1)

            def f_tile(i, j):
                pe.wait_ge(c_f, i * 2 + (j + 1))
                pe.wait_ge(c_logits, i * 2 + (j + 1))
                transpose_tile(f_buf[:, j, :], 4).then_inc(c_ftp, 1)

            def router_tile(i, j):
                pe.wait_ge(c_fT_act, i * 2 + (j + 1))
                pe.wait_ge(c_fT_dve, i * 2 + (j + 1))
                for k in range(KD):
                    last = pe.matmul(psum[:, 6, 0:NR], fT[:, k, :], w_r[:, k, :], start=(k == 0), stop=(k == KD - 1))
                last.then_inc(c_lg, 1)

            pe.wait_ge(s_wout, 16)
            with pe.Fori(0, T // 2) as i:
                for j in range(2):
                    merged_tile(i, j)
                    out_tile(i, j)
                    f_tile(i, j)
                    router_tile(i, j)

            pe.wait_ge(r_hot, 1)
            pe.wait_ge(s_pool_const, 1)
            ranks = psum[:, 0, 0:T * NE].rearrange("p (t e) -> p t e", t=T)
            for t in range(T - 1):
                later = T - 1 - t
                rhs = bass.AP(hot_sum[:, t, :].tensor, t * NE, [[T * NE, P], [0, later], [1, NE]])
                pe.matmul(ranks[:, t + 1:T, :], ones_b[:, :], rhs, start=(t == 0), stop=False, skip_group_check=True)
            pe.matmul(ranks, tri[:, :], hot_sum[:, :, :], start=False, stop=True, skip_group_check=True)
            for t in range(T):
                last = pe.matmul(psum[:, 1, 0:NE], ones_b[:, :], hot_sum[:, t, :], start=(t == 0), stop=(t == T - 1))
            last.then_inc(r_counted, 1)
            pe.wait_ge(r_vals, 1)
            n = 0
            for t in range(T):
                for c in range(TOP):
                    last = pe.matmul(psum[:, 2, 0:3 * NB], pos_hot[:, c, t, :],
                                     blk_vals[:, c, t, :, :].rearrange("p a b -> p (a b)"),
                                     start=(n == 0), stop=(n == TOP * T - 1))
                    n += 1
            last.then_inc(r_rows, 1)

            def gather_tp(b):
                pe.wait_ge(xg_landed, b * 16 + 16)
                for k in range(KD):
                    last = pe.transpose(psum[:, 4 + k // 4, (k % 4) * P:(k % 4 + 1) * P], xg[:, k * P:(k + 1) * P],
                                        ident[:, :])
                last.then_inc(x_tp, 1)

            def gate_up(b, slot):
                pe.wait_ge(xT_act, b + 1)
                pe.wait_ge(xT_dve, b + 1)
                for part_no, landed, ready in ((0, gate_landed, g_ready), (1, up_landed, u_ready)):
                    pe.wait_ge(landed, b * 16 + 16)
                    for k in range(KD):
                        last = pe.matmul(psum[:, part_no, :], xT[:, k, :],
                                         gu_ring[:, slot, k, part_no * DE:(part_no + 1) * DE],
                                         start=(k == 0), stop=(k == KD - 1))
                    last.then_inc(ready, 1)

            def hidden_tp(b):
                pe.wait_ge(h_ready, b + 1)
                for k in range(KE):
                    last = pe.transpose(psum[:, 6, k * P:(k + 1) * P], hid[:, k * P:(k + 1) * P], ident[:, :])
                last.then_inc(h_tp, 1)

            def down(b, slot):
                pe.wait_ge(hT_ready, b + 1)
                pe.wait_ge(down_landed, b * 16 + 16)
                pe.wait_ge(y_act, b + 1)
                pe.wait_ge(y_dve, b + 1)
                for n in range(2):
                    for k in range(KE):
                        last = pe.matmul(psum[:, 2 + n, :], hT[:, k, :], dn_ring[:, slot, k, n * BANK:(n + 1) * BANK],
                                         start=(k == 0), stop=(k == KE - 1))
                    last.then_inc(y_ready, 1)

            pe.wait_ge(r_idx, 1)
            last_b = pe.value_load(last_i[0:1, 0:1], min_val=NE - 1, max_val=NB - 2)
            gather_tp(0)
            gate_up(0, 1)
            gather_tp(1)
            with pe.Fori(1, last_b + 1) as b:
                hidden_tp(b - 1)
                gate_up(b, (b + 1) % 2)
                gather_tp(b + 1)
                down(b - 1, (b + 2) % 3)
            hidden_tp(last_b)
            down(last_b, last_b % 3)

        @block.scalar
        def _(act):
            act.sem_inc(n_aT_act, 2)
            act.sem_inc(n_sq, 1)
            act.sem_inc(c_sq, 1)
            act.sem_inc(acc_act, 2)
            for a in (SB, DF, CA):
                act.sem_inc(a.s["pt_sb0"], 1)
            act.sem_inc(SBS["o_read"], 2)
            act.sem_inc(c_mT_act, 1)
            act.sem_inc(y_act, 1)
            act.dma_start(lines_in[:, 0:T5_BUCKETS], t5_bias.rearrange("b h -> h b"), allow_slow_non_contiguous=True) \
                .then_inc(s_lines_in, 16)
            act.dma_start(lines_in[:, T5_BUCKETS:], ca_rel_bias[0].rearrange("b h -> h b"),
                          allow_slow_non_contiguous=True).then_inc(s_lines_in, 16)
            act.dma_start(subln[:, :], diff_subln.to_broadcast([P, 2 * HEAD])).then_inc(s_const, 16)
            act.dma_start(lam_in[:, :], diff_lambda[0].rearrange("(o a) b -> o (a b)", o=1).to_broadcast([P, 4 * HEAD])) \
                .then_inc(s_const, 16)
            for half in range(2):
                for n, gain in enumerate((diff_qk_norm, ca_qk_norm)):
                    act.dma_start(qk_gain[HEAD * half:HEAD * (half + 1), 2 * n:2 * n + 2],
                                  gain[0].rearrange("a b -> b a"), allow_slow_non_contiguous=True).then_inc(s_const, 16)
            act.dma_start(w_r[:, :, 0:NG], group_w[0].rearrange("(k p) n -> p k n", p=P),
                          allow_slow_non_contiguous=True).then_inc(s_const, 16)
            act.dma_start(w_r[:, :, NG:NR], expert_w[0].rearrange("(k p) n -> p k n", p=P)).then_inc(s_const, 16)
            act.dma_start(b_r[:, 0:NG], group_b.to_broadcast([P, NG])).then_inc(s_const, 16)
            act.dma_start(b_r[:, NG:NR], expert_b.to_broadcast([P, NE])).then_inc(s_const, 16)

            def copy_half(dst, src, done):
                act.copy(dst, src).then_inc(done, 1)

            with act.Fori(0, T // 4) as i:
                for j in range(4):
                    act.wait_ge(s_x[j], i * 16 + 16)
                    act.wait_ge(n_sq, i * 4 + (j + 1))
                    act.activation(norm_junk, x_all[:, bass.ds(i * 4 + j, 1), :].rearrange("p a b -> p (a b)"), ACT.Square,
                                   accum_out=ss[:, bass.ds(i * 4 + j, 1)]).then_inc(n_sq, 1)
            with act.Fori(0, T // 2) as i:
                for j in range(2):
                    act.wait_ge(n_tp, i * 2 + (j + 1))
                    act.copy(aT[:, 0:4, bass.ds(i * 2 * P + j * P, P)],
                             psum[:, 2 * j, :].rearrange("p (a b) -> p a b", a=4)).then_inc(n_aT_act, 1)
            act.wait_ge(s_lam_sum, 2)
            act.activation(lam_exp[:, :], lam_sum[:, :], ACT.Exp).then_inc(s_lam_exp, 1)
            act.wait_ge(s_lines, 2)
            act.dma_start(t5_line[:, 0:T5_LINE], t5_sb[:, 0:T5_LINE]).then_inc(s_lines_out, 16)
            act.dma_start(ca_line[:, 0:CA_LINE], ca_sb[:, 0:CA_LINE]).then_inc(s_lines_out, 16)
            with act.Fori(0, CH) as i:
                for t in range(0, T, 2):
                    act.wait_ge(acc_ready, i * T + (t + 1))
                    act.copy(proj[:, t, bass.ds(i * BANK, BANK)], psum[:, 4 + t % 4, :]).then_inc(acc_act, 1)

            def copy_kT(a, p, gain):
                act.wait_ge(a.s["k_tp"], p + 1)
                for c in range(2):
                    act.activation(kT[:, c * BANK:(c + 1) * BANK], psum[:, 2 + c, :], ACT.Copy, scale=gain) \
                        .then_inc(a.s["kT_ready"], 1)

            def copy_pt0(a, p, r):
                before, per = a.group_no(0, r)
                w = len(a.groups(r)[0]) * P
                act.wait_ge(a.s["pt0"], p * per + (before + 1 + per))
                act.copy(pt_sb[:, 0, 0:w], psum[:, 4, 0:w]).then_inc(a.s["pt_sb0"], 1)

            def squares_of(a, p):
                for n, first in enumerate((a.q, a.k)):
                    act.wait_ge(a.s["qk_ms_ready"], p * 2 + 1)
                    act.activation(squares[:, n, :, :], proj[:, :, cols(first, p)], ACT.Square) \
                        .then_inc(a.s["squared"], 1)

            def exp_rows(a, p, u, slot, stat, m):
                t = u // 2
                w = a.keys(t)[1] * P
                act.wait_ge(a.s["z_read"], p * a.units + (u + 3))
                act.activation(work[:, slot, 0:w], work[:, slot, 0:w], ACT.Exp, bias=low[:, stat, m:m + 1], scale=-1.0,
                               accum_out=total[:, stat, m:m + 1]).then_inc(a.s["summed" if a.kind == "df" else "p_ready"], 1)

            def sb_softplus_tail(p, u):
                w, buf = SB.keys(u // 2)[1] * P, 2 + u % 2
                act.wait_ge(SBS["z_ready"], p * SB.units + (u + 1))
                act.wait_ge(SBS["z_read"], p * SB.units + (u + 1))
                act.activation(work[:, buf, 0:w], banks(2 * (u % 2), 2)[:, 0:w], ACT.Abs).then_inc(SBS["abs_done"], 1)
                act.wait_ge(SBS["abs_done"], p * SB.units + (u + 1))
                act.activation(work[:, buf, 0:w], work[:, buf, 0:w], ACT.Exp, scale=-1.0).then_inc(SBS["exp_done"], 1)
                act.wait_ge(SBS["exp_done"], p * SB.units + (u + 1))
                act.activation(work[:, buf, 0:w], work[:, buf, 0:w], ACT.Ln, bias=1.0).then_inc(SBS["lp_ready"], 1)

            def sb_weights(p, u):
                w, buf = SB.keys(u // 2)[1] * P, u % 2
                act.wait_ge(SBS["z_read"], p * SB.units + (u + 3))
                wait_slot(act, SB, p, u, 2)
                act.activation(work[:, buf, 0:w], work[:, 4 + buf, 0:w], ACT.Exp).then_inc(SBS["w_exp"], 1)

            def sb_merge(p, r):
                act.wait_ge(SBS["o_ready"], p * SB.results + (r + 1))
                act.copy(merged[:, r // 2, cols(SB_O + HEAD * (r % 2), p, HEAD)], psum[:, 6 + r % 2, 0:HEAD]) \
                    .then_inc(SBS["o_read"], 1)

            act.wait_ge(s_lines_out, 32)
            act.preload_act_table_set("natural_log_exp_and_others")
            with act.Fori(0, SB.pairs) as p:
                copy_kT(SB, p, 1.0)
                for s in range(SB.units + 3):
                    if s < SB.units:
                        sb_softplus_tail(p, s)
                    if 2 <= s < SB.units + 2:
                        copy_pt0(SB, p, s - 2)
                    if 1 <= s <= SB.units:
                        sb_weights(p, s - 1)
                    if s >= 3:
                        sb_merge(p, s - 3)
            act.wait_ge(SBS["o_read"], 2 + SB.pairs * SB.results)
            act.preload_act_table_set("exp_and_others")
            squares_of(DF, 0)
            with act.Fori(0, DF.pairs) as p:
                copy_kT(DF, p, qk_gain[:, 1:2])
                for s in range(T + 2):
                    if s >= 2:
                        copy_pt0(DF, p, s - 2)
                    if s < T:
                        for m in range(2):
                            exp_rows(DF, p, 2 * s + m, 2 * (s % 3) + m, s % 4, m)
                    if s == 2:
                        squares_of(DF, p + 1)
            act.wait_ge(DFS["merged_ready"], DF.pairs * DF.results)
            squares_of(CA, 0)
            with act.Fori(0, CA.pairs) as p:
                copy_kT(CA, p, qk_gain[:, 3:4])
                for s in range(CA.units + 2):
                    if s >= 2:
                        copy_pt0(CA, p, s - 2)
                    if s < CA.units:
                        exp_rows(CA, p, s, s % 4, s % 4, 0)
                    if s == 4:
                        squares_of(CA, p + 1)
            act.wait_ge(CAS["o_read"], 2 + CA.pairs * CA.results)

            with act.Fori(0, T // 2) as i:
                for j in range(2):
                    act.wait_ge(c_tp, i * 2 + (j + 1))
                    act.copy(mT[:, j, 0:4, :], psum[:, 0, :].rearrange("p (a b) -> p a b", a=4)).then_inc(c_mT_act, 1)
                    act.wait_ge(c_h2, i * 4 + (2 * j + 4))
                    act.wait_ge(c_sq, i * 2 + (j + 1))
                    act.activation(out_junk, h2[:, bass.ds(i * 2 + j, 1), :].rearrange("p a b -> p (a b)"), ACT.Square,
                                   accum_out=ss[:, bass.ds(i * 2 + j, 1)]).then_inc(c_sq, 1)
                    act.wait_ge(c_f, i * 2 + (j + 1))
                    act.wait_ge(c_fsaved, i * 32 + 16 * (j + 2))
                    act.dma_start(f_rows[bass.ds(i * 2 * P + j * P, P), :], f_buf[:, j, :]).then_inc(c_fsaved, 16)
                    act.wait_ge(c_ftp, i * 2 + (j + 1))
                    act.copy(fT[:, 0:4, :], psum[:, 4, :].rearrange("p (a b) -> p a b", a=4)).then_inc(c_fT_act, 1)

            act.wait_ge(r_gexp_in, 1)
            act.activation(g_exp[:, :, :], g_exp[:, :, :], ACT.Exp).then_inc(r_gexp, 1)
            act.wait_ge(r_esec_in, 1)
            act.activation(e_sec[:, :], e_gap[:, :], ACT.Exp).then_inc(r_esec, 1)

            def copy_xT(b):
                act.wait_ge(x_tp, b + 1)
                act.copy(xT[:, 0:4, :], psum[:, 4, :].rearrange("p (a b) -> p a b", a=4)).then_inc(xT_act, 1)

            def silu_of(b):
                act.wait_ge(g_ready, b + 1)
                act.activation(silu, psum[:, 0, :], ACT.Silu).then_inc(silu_ready, 1)

            def copy_hT(b):
                act.wait_ge(h_tp, b + 1)
                act.copy(hT, psum[:, 6, :].rearrange("p (a b) -> p a b", a=KE)).then_inc(hT_ready, 1)

            def copy_y(b, first=False):
                act.wait_ge(y_ready, b * 2 + 5)
                if not first:
                    act.wait_ge(y_stored, b * 16)
                act.copy(y_sb[:, 0:BANK], psum[:, 2, :]).then_inc(y_act, 1)

            act.wait_ge(r_idx, 1)
            last_b = act.value_load(last_i[0:1, 0:1], min_val=NE - 1, max_val=NB - 2)
            copy_xT(0)
            silu_of(0)
            copy_xT(1)

            def block_of(b, first=False):
                copy_hT(b)
                silu_of(b + 1)
                copy_xT(b + 2)
                copy_y(b, first)

            block_of(0, first=True)
            with act.Fori(1, last_b) as b:
                block_of(b)
            copy_hT(last_b)
            copy_y(last_b)

        @block.vector
        def _(dve):
            dve.sem_inc(n_aT_dve, 2)
            dve.sem_inc(acc_dve, 2)
            for a in (SB, DF, CA):
                dve.sem_inc(a.s["pt_sb1"], 1)
                dve.sem_inc(a.s["z_read"], 2)
            for a in (DF, CA):
                dve.sem_inc(a.s["o_read"], 2)
                dve.sem_inc(a.s["qk_ms_ready"], 2)
            dve.sem_inc(c_mT_dve, 1)
            dve.sem_inc(c_h2, 2)
            dve.sem_inc(c_logits, 1)
            dve.sem_inc(y_dve, 1)
            dve.memset(ones[:, :], 1.0)
            dve.memset(mhalf[:, :], -0.5).then_inc(s_dve_const, 1)

            dve.wait_ge(s_gain, 16)
            for t in range(T):
                dve.wait_ge(n_sq, t + 2)
                dve.tensor_scalar(ms[:, t:t + 1], ss[:, t:t + 1], 1.0 / D, EPS, ALU.mult, ALU.add).then_inc(n_ms, 1)
                dve.wait_ge(n_rstd, t + 1)
                if t >= 2:
                    dve.wait_ge(n_tp, t - 1)
                dve.scalar_tensor_tensor(a_buf[:, t % 2, :], x_all[:, t, :], rstd[:, t:t + 1], attn_gain[:, :],
                                         ALU.mult, ALU.mult).then_inc(n_a, 1)
                if t >= 1:
                    dve.wait_ge(n_tp, t)
                    dve.tensor_copy(aT[:, 4:8, (t - 1) * P:t * P],
                                    psum[:, 2 * ((t - 1) % 2) + 1, :].rearrange("p (a b) -> p a b", a=4)) \
                        .then_inc(n_aT_dve, 1)
            dve.wait_ge(n_tp, T)
            dve.tensor_copy(aT[:, 4:8, (T - 1) * P:T * P],
                            psum[:, 2 * ((T - 1) % 2) + 1, :].rearrange("p (a b) -> p a b", a=4)).then_inc(n_aT_dve, 1)
            dve.wait_ge(s_const, 16 * 10)
            for n in range(2):
                if n:
                    dve.wait_ge(s_lam_sum, n)
                dve.tensor_tensor_reduce(out=lam_junk[:, :], in0=lam_in[:, 2 * n * HEAD:(2 * n + 1) * HEAD],
                                         in1=lam_in[:, (2 * n + 1) * HEAD:(2 * n + 2) * HEAD], scale=1.0, scalar=0.0,
                                         op0=ALU.mult, op1=ALU.add, accum_out=lam_sum[:, n:n + 1]).then_inc(s_lam_sum, 1)
            dve.wait_ge(s_lam_exp, 1)
            dve.tensor_tensor(neg_lam[:, :], lam_exp[:, 1:2], lam_exp[:, 0:1], ALU.subtract).then_inc(s_lam, 1)
            dve.wait_ge(s_lam, 1)
            dve.tensor_scalar(neg_lam[:, :], neg_lam[:, :], LAM_INIT, None, ALU.subtract).then_inc(s_lam, 1)
            for c in (0, 2):
                dve.tensor_scalar(qk_gain[:, c:c + 1], qk_gain[:, c:c + 1], SCALE, None, ALU.mult).then_inc(s_lam, 1)
            dve.tensor_scalar(subln[:, :], subln[:, :], 1.0 - LAM_INIT, None, ALU.mult).then_inc(s_lam, 1)
            with dve.Fori(0, CH) as i:
                for t in range(1, T, 2):
                    dve.wait_ge(acc_ready, i * T + (t + 1))
                    dve.tensor_copy(proj[:, t, bass.ds(i * BANK, BANK)], psum[:, 4 + t % 4, :]).then_inc(acc_dve, 1)
            dve.wait_ge(s_lam, 5)

            def copy_qT(a, p, gain):
                dve.wait_ge(a.s["q_tp"], p + 1)
                for c in range(2):
                    dve.tensor_scalar(qT[:, c * BANK:(c + 1) * BANK], psum[:, c, :], gain, None, ALU.mult) \
                        .then_inc(a.s["qT_ready"], 1)

            def copy_pt1(a, p, r):
                if len(a.groups(r)) < 2:
                    return
                before, per = a.group_no(1, r)
                w = len(a.groups(r)[1]) * P
                dve.wait_ge(a.s["pt1"], p * per + (before + 1 + per))
                dve.tensor_copy(pt_sb[:, 1, 0:w], psum[:, 5, 0:w]).then_inc(a.s["pt_sb1"], 1)

            def mean_squares(a, p):
                dve.wait_ge(a.s["squared"], p * 2 + 2)
                dve.tensor_reduce(qk_ss[:, :, :].rearrange("p n g -> p (n g)"),
                                  squares.rearrange("p n t (h d) -> p (n t h) d", h=2), AX.X, ALU.add) \
                    .then_inc(a.s["qk_ms_ready"], 1)
                dve.wait_ge(a.s["qk_ms_ready"], p * 2 + 3)
                dve.tensor_scalar(qk_ms[:, :, :], qk_ss[:, :, :], 1.0 / HEAD, EPS, ALU.mult, ALU.add) \
                    .then_inc(a.s["qk_ms_ready"], 1)

            def biased(a, p, u, slot, stat, m, tile):
                t = u // 2
                first, n = a.keys(t)
                w = n * P
                wait_alone(dve, a.s["z_ready"], p * a.units + (u + 1))
                dve.tensor_tensor_reduce(out=work[:, slot, 0:w], in0=banks(2 * (u % 2), 2)[:, 0:w],
                                         in1=bias_tiles[:, tile, 0:w][:, ::-1], scale=-1.0, scalar=-LOWEST,
                                         op0=ALU.add, op1=ALU.min, accum_out=low[:, stat, m:m + 1]) \
                    .then_inc(a.s["z_read"], 1)

            def mask_bias(a, p, tiles):
                dve.wait_ge(a.s["bias_landed"], p * 16 * tiles + 16 * tiles)
                for m in range(tiles):
                    last = dve.memset(bias_tiles[0:HEAD, m, 0:HEAD], MASKED)
                    if a.kind == "ca":
                        last = dve.memset(bias_tiles[HEAD:P, m, CA_W - HEAD:CA_W], MASKED)
                last.then_inc(a.s["bias_ready"], 1)

            def sb_softplus(p, u):
                w, buf = SB.keys(u // 2)[1] * P, u % 2
                dve.wait_ge(SBS["lp_ready"], p * SB.units + (u + 1))
                dve.scalar_tensor_tensor(work[:, 2 + buf, 0:w], banks(2 * buf, 2)[:, 0:w], 0.0, work[:, 2 + buf, 0:w],
                                         ALU.max, ALU.add).then_inc(SBS["sp_ready"], 1)

            def sb_exponent(p, u):
                w, buf = SB.keys(u // 2)[1] * P, u % 2
                dve.wait_ge(SBS["sp_masked"], p * SB.units + (u + 1))
                dve.tensor_tensor_scan(work[:, 4 + buf, 0:w][:, ::-1], ones[:, 0:1].to_broadcast([P, w]),
                                       work[:, 2 + buf, 0:w][:, ::-1], 0.0, ALU.mult, ALU.add).then_inc(SBS["scanned"], 1)
                dve.wait_ge(SBS["scanned"], p * SB.units + (u + 1))
                dve.tensor_tensor(work[:, 4 + buf, 0:w], banks(2 * buf, 2)[:, 0:w], work[:, 4 + buf, 0:w],
                                  ALU.subtract).then_inc(SBS["z_read"], 1)

            with dve.Fori(0, SB.pairs) as p:
                copy_qT(SB, p, SCALE)
                for s in range(SB.units + 2):
                    if 1 <= s <= SB.units:
                        sb_exponent(p, s - 1)
                    if s >= 2:
                        copy_pt1(SB, p, s - 2)
                    if s < SB.units:
                        sb_softplus(p, s)

            def df_mix(p, t):
                st = t % 4
                dve.wait_ge(DFS["summed"], p * DF.units + (2 * t + 2))
                dve.reciprocal(inv[:, st, :], total[:, st, :]).then_inc(DFS["inverse"], 1)
                dve.wait_ge(DFS["inverse"], p * 2 * T + (2 * t + 1))
                dve.tensor_scalar(mix[:, st:st + 1], inv[:, st, 1:2], total[:, st, 0:1], neg_lam[:, :], ALU.mult,
                                  ALU.mult).then_inc(DFS["inverse"], 1)
                w, buf = (t + 1) * P, 2 * (t % 3)
                dve.wait_ge(DFS["inverse"], p * 2 * T + (2 * t + 2))
                dve.scalar_tensor_tensor(work[:, buf, 0:w], work[:, buf + 1, 0:w], mix[:, st:st + 1], work[:, buf, 0:w],
                                         ALU.mult, ALU.add).then_inc(DFS["p_ready"], 1)

            def df_result(p, t):
                dve.wait_ge(DFS["o_ready"], p * T + (t + 1))
                dve.tensor_scalar(yd[:, t % 2, :], psum[:, 6 + t % 2, 0:P], inv[:, t % 4, 0:1], None, ALU.mult) \
                    .then_inc(DFS["o_read"], 1)
                dve.wait_ge(DFS["o_read"], p * T + (t + 3))
                dve.tensor_tensor_reduce(out=yd_junk[:, :], in0=yd[:, t % 2, :], in1=yd[:, t % 2, :], scale=1.0,
                                         scalar=0.0, op0=ALU.mult, op1=ALU.add,
                                         accum_out=yd_ss[:, t % 2:t % 2 + 1]).then_inc(DFS["yd_ss_ready"], 1)
                dve.wait_ge(DFS["yd_ss_ready"], p * T + (t + 1))
                dve.tensor_scalar(yd_ms[:, t % 2:t % 2 + 1], yd_ss[:, t % 2:t % 2 + 1], 1.0 / P, EPS, ALU.mult,
                                  ALU.add).then_inc(DFS["yd_ms_ready"], 1)

            def df_merge(p, t):
                dve.wait_ge(DFS["yd_rstd_ready"], p * T + (t + 1))
                dve.scalar_tensor_tensor(merged[:, t, cols(DF_O, p)], yd[:, t % 2, :], yd_rstd[:, t % 2:t % 2 + 1],
                                         subln[:, :], ALU.mult, ALU.mult).then_inc(DFS["merged_ready"], 1)

            dve.wait_ge(SBS["o_read"], 2 + SB.pairs * SB.results)
            mean_squares(DF, 0)
            with dve.Fori(0, DF.pairs) as p:
                copy_qT(DF, p, qk_gain[:, 0:1])
                mask_bias(DF, p, 1)
                dve.wait_ge(DFS["bias_ready"], p + 1)
                for s in range(T + 4):
                    if 2 <= s < T + 2:
                        copy_pt1(DF, p, s - 2)
                    if 1 <= s <= T:
                        df_mix(p, s - 1)
                    if s < T:
                        wait_slot(dve, DF, p, s, 3)
                        for m in range(2):
                            biased(DF, p, 2 * s + m, 2 * (s % 3) + m, s % 4, m, 0)
                    if s == 3:
                        mean_squares(DF, p + 1)
                    if s >= 4:
                        df_merge(p, s - 4)
                    if 3 <= s < T + 3:
                        df_result(p, s - 3)

            dve.wait_ge(DFS["merged_ready"], DF.pairs * DF.results)
            mean_squares(CA, 0)
            with dve.Fori(0, CA.pairs) as p:
                copy_qT(CA, p, qk_gain[:, 2:3])
                mask_bias(CA, p, 2)
                dve.wait_ge(CAS["bias_ready"], p + 1)
                for s in range(CA.units + 3):
                    if 2 <= s < CA.units + 2:
                        copy_pt1(CA, p, s - 2)
                    if s < CA.units:
                        wait_slot(dve, CA, p, s, 4)
                        biased(CA, p, s, s % 4, s % 4, 0, s % 2)
                    if 1 <= s <= CA.units:
                        dve.wait_ge(CAS["p_ready"], p * CA.units + s)
                        dve.reciprocal(inv[:, (s - 1) % 4, 0:1], total[:, (s - 1) % 4, 0:1]).then_inc(CAS["inverse"], 1)
                    if s == 5:
                        mean_squares(CA, p + 1)
                    if s >= 3:
                        r = s - 3
                        dve.wait_ge(CAS["o_ready"], p * CA.results + (r + 1))
                        dve.wait_ge(CAS["inverse"], p * CA.results + (r + 1))
                        dve.tensor_scalar(merged[:, r // 2, cols(CA_O + HEAD * (r % 2), p, HEAD)],
                                          psum[:, 6 + r % 2, 0:HEAD], inv[:, r % 4, 0:1], None, ALU.mult) \
                            .then_inc(CAS["o_read"], 1)

            def row(tensor, i, j):
                return tensor[:, bass.ds(i * 2 + j, 1), :].rearrange("p a b -> p (a b)")

            dve.wait_ge(CAS["o_read"], 2 + CA.pairs * CA.results)
            dve.wait_ge(s_pool_const, 1)
            dve.wait_ge(s_gain, 32)
            dve.wait_ge(s_x_again, 32)
            with dve.Fori(0, T // 2) as i:
                for j in range(2):
                    dve.wait_ge(c_tp, i * 2 + (j + 1))
                    dve.tensor_copy(mT[:, j, 4:8, :], psum[:, 1, :].rearrange("p (a b) -> p a b", a=4)) \
                        .then_inc(c_mT_dve, 1)
                    for n in range(2):
                        half = h2[:, bass.ds(i * 2 + j, 1), n * BANK:(n + 1) * BANK].rearrange("p a b -> p (a b)")
                        dve.wait_ge(c_acc, i * 4 + (2 * j + n + 1))
                        dve.tensor_tensor(half, psum[:, 2 + n, :], half, ALU.add).then_inc(c_h2, 1)
                    dve.wait_ge(c_sq, i * 2 + (j + 2))
                    dve.tensor_scalar(ms[:, bass.ds(i * 2 + j, 1)], ss[:, bass.ds(i * 2 + j, 1)], 1.0 / D, EPS, ALU.mult,
                                      ALU.add).then_inc(c_ms, 1)
                    dve.wait_ge(c_rstd, i * 2 + (j + 1))
                    dve.wait_ge(c_fsaved, i * 32 + 16 * (j + 1))
                    dve.scalar_tensor_tensor(f_buf[:, j, :], row(h2, i, j), rstd[:, bass.ds(i * 2 + j, 1)],
                                             attn_gain[:, :], ALU.mult, ALU.mult).then_inc(c_f, 1)
                    dve.wait_ge(c_ftp, i * 2 + (j + 1))
                    dve.tensor_copy(fT[:, 4:8, :], psum[:, 5, :].rearrange("p (a b) -> p a b", a=4)) \
                        .then_inc(c_fT_dve, 1)
                    dve.wait_ge(c_lg, i * 2 + (j + 1))
                    dve.tensor_tensor(row(logits, i, j), psum[:, 6, 0:NR], b_r[:, :], ALU.add).then_inc(c_logits, 1)

            steps = [0]

            def step(ins, told=None):
                if told is not None:
                    ins.then_inc(told, 1)
                    dve.wait_ge(told, 1)
                else:
                    steps[0] += 1
                    ins.then_inc(r_dve, 1)
                    dve.wait_ge(r_dve, steps[0])

            def over(ap, axis, n):
                dims = [list(d) for d in ap.ap]
                return bass.AP(ap.tensor, ap.offset, dims[:1 + axis] + [[0, n]] + dims[1 + axis:])

            dve.wait_ge(c_logits, T + 1)
            step(dve.memset(g8[:, :, :], LOWEST))
            step(dve.tensor_copy(g8[:, :, 0:NG], logits[:, :, 0:NG]))
            for t in range(T):
                last = dve.max(g_top[:, t, :], g8[:, t, :])
            step(last)
            for t in range(T):
                last = dve.max_index(g_idx[:, t, :], g_top[:, t, :], g8[:, t, :])
            step(last)
            step(dve.tensor_tensor(g_exp[:, :, :], logits[:, :, 0:NG], over(g_top[:, :, 0], 1, NG), ALU.subtract), r_gexp_in)
            step(dve.tensor_copy(g_sel[:, :], g_idx[:, :, 0]))
            step(dve.tensor_tensor(g_hot[:, :, :], over(iota_f[:, 0:NG], 0, T), over(g_sel[:, :], 1, NG), ALU.is_equal))
            step(dve.tensor_tensor(e_all[:, :, :, :], logits[:, :, NG:NR].rearrange("p t (g e) -> p t g e", g=NG),
                                   over(g_hot[:, :, :], 2, EG), ALU.mult))
            step(dve.tensor_reduce(e8[:, :, :], e_all[:, :, :, :].rearrange("p t g e -> p t e g"), AX.X, ALU.add))
            for t in range(T):
                last = dve.max(e_top[:, t, :], e8[:, t, :])
            step(last)
            for t in range(T):
                last = dve.max_index(e_idx[:, t, :], e_top[:, t, :], e8[:, t, :])
            step(last)
            step(dve.tensor_tensor(e_gap[:, :], e_top[:, :, 1], e_top[:, :, 0], ALU.subtract), r_esec_in)
            step(dve.tensor_copy(e_idf[:, :, :], e_idx[:, :, 0:TOP]))
            step(dve.scalar_tensor_tensor(eid[:, :, :], over(g_sel[:, :], 1, TOP), float(EG), e_idf[:, :, :], ALU.mult,
                                          ALU.add))
            for c in range(TOP):
                step(dve.tensor_tensor(hot[:, c, :, :], over(iota_f[:, 0:NE], 0, T), over(eid[:, :, c], 1, NE),
                                       ALU.is_equal))
            step(dve.tensor_tensor(hot_sum[:, :, :], hot[:, 0, :, :], hot[:, 1, :, :], ALU.add), r_hot)
            dve.wait_ge(r_gexp, 1)
            step(dve.tensor_reduce(g_sum[:, :], g_exp[:, :, :], AX.X, ALU.add))
            step(dve.reciprocal(g_w[:, :], g_sum[:, :]))
            dve.wait_ge(r_esec, 1)
            step(dve.tensor_scalar(e_den[:, :], e_sec[:, :], 1.0, None, ALU.add))
            step(dve.reciprocal(e_inv[:, :], e_den[:, :]))
            step(dve.tensor_tensor(gates[:, :, 0], g_w[:, :], e_inv[:, :], ALU.mult))
            step(dve.tensor_tensor(gates[:, :, 1], gates[:, :, 0], e_sec[:, :], ALU.mult))
            dve.wait_ge(r_counted, 1)
            step(dve.tensor_scalar(cnt_i[:, :], psum[:, 1, 0:NE], float(P - 1), None, ALU.add))
            step(dve.tensor_scalar(cnt_i[:, :], cnt_i[:, :], 7, None, ALU.arith_shift_right))
            step(dve.tensor_scalar(nblk[:, :], cnt_i[:, :], 1.0, None, ALU.max))
            step(dve.tensor_tensor_scan(blk_end[:, :], ones[:, 0:1].to_broadcast([P, NE]), nblk[:, :], 0.0, ALU.mult,
                                        ALU.add))
            step(dve.tensor_tensor(blk_start[:, :], blk_end[:, :], nblk[:, :], ALU.subtract))
            ranks = psum[:, 0, 0:T * NE].rearrange("p (t e) -> p t e", t=T)
            for c in range(TOP):
                step(dve.tensor_tensor(picked[:, c, :, :], ranks, hot[:, c, :, :], ALU.mult))
            step(dve.tensor_reduce(rank[:, :, :], picked[:, :, :, :], AX.X, ALU.add))
            for c in range(TOP):
                step(dve.tensor_tensor(picked[:, c, :, :], over(blk_start[:, :], 0, T), hot[:, c, :, :], ALU.mult))
            step(dve.tensor_reduce(first_blk[:, :, :], picked[:, :, :, :], AX.X, ALU.add))
            step(dve.tensor_copy(rank_i[:, :, :], rank[:, :, :]))
            step(dve.tensor_scalar(hi_i[:, :, :], rank_i[:, :, :], 7, None, ALU.arith_shift_right))
            step(dve.tensor_scalar(lo_i[:, :, :], rank_i[:, :, :], P - 1, None, ALU.bitwise_and))
            step(dve.tensor_copy(hi_f[:, :, :], hi_i[:, :, :]))
            step(dve.tensor_copy(lo_f[:, :, :], lo_i[:, :, :]))
            step(dve.tensor_tensor(blk[:, :, :], first_blk[:, :, :], hi_f[:, :, :], ALU.add))
            for c in range(TOP):
                step(dve.tensor_tensor(pos_hot[:, c, :, :], over(iota_f[:, :], 0, T), over(lo_f[:, c, :], 1, P),
                                       ALU.is_equal))
                step(dve.tensor_tensor(blk_hot[:, c, :, :], over(iota_f[:, 0:NB], 0, T), over(blk[:, c, :], 1, NB),
                                       ALU.is_equal))
                step(dve.tensor_scalar(blk_vals[:, c, :, 0, :], blk_hot[:, c, :, :], part_id[:, 0:1], None, ALU.mult))
                step(dve.tensor_tensor(blk_vals[:, c, :, 1, :], blk_hot[:, c, :, :], over(tile_id[:, :], 1, NB), ALU.mult))
                step(dve.tensor_scalar(blk_vals[:, c, :, 2, :], blk_hot[:, c, :, :], float(c), None, ALU.mult))
            step(dve.tensor_scalar(last_i[0:1, 0:1], blk_end[0:1, NE - 1:NE], 1.0, None, ALU.subtract), r_vals)
            step(dve.tensor_tensor(be_cmp[:, :, :], over(blk_end[0:1, :], 0, NB), over(iota_f[0:1, 0:NB], 1, NE), ALU.is_le))
            step(dve.tensor_reduce(be_f[:, :], be_cmp[:, :, :], AX.X, ALU.add))
            step(dve.tensor_scalar(be_i[:, :], be_f[:, :], float(NE - 1), None, ALU.min), r_idx)
            dve.wait_ge(r_rows, 1)
            told = psum[:, 2, 0:3 * NB].rearrange("p (a b) -> p a b", a=3)
            step(dve.tensor_scalar(empty[:, :], told[:, 0, :], 0.0, 65536.0, ALU.is_equal, ALU.mult))
            step(dve.scalar_tensor_tensor(empty[:, :], told[:, 0, :], 1.0, empty[:, :], ALU.subtract, ALU.add))
            step(dve.scalar_tensor_tensor(row_f[:, 0, :], told[:, 1, :], float(P), empty[:, :], ALU.mult, ALU.add))
            step(dve.scalar_tensor_tensor(row_f[:, 1, :], told[:, 1, :], float(P), row_f[:, 0, :], ALU.mult, ALU.add))
            step(dve.scalar_tensor_tensor(row_f[:, 1, :], told[:, 2, :], float(P), row_f[:, 1, :], ALU.mult, ALU.add))
            step(dve.tensor_copy(row_i[:, :, :], row_f[:, :, :]), r_table)

            def copy_xT(b):
                dve.wait_ge(x_tp, b + 1)
                dve.tensor_copy(xT[:, 4:8, :], psum[:, 5, :].rearrange("p (a b) -> p a b", a=4)).then_inc(xT_dve, 1)

            def hidden(b):
                dve.wait_ge(u_ready, b + 2)
                dve.wait_ge(silu_ready, b + 1)
                dve.tensor_tensor(hid, silu, psum[:, 1, :], ALU.mult).then_inc(h_ready, 1)

            def copy_y(b, first=False):
                dve.wait_ge(y_ready, b * 2 + 6)
                if not first:
                    dve.wait_ge(y_stored, b * 16)
                dve.tensor_copy(y_sb[:, BANK:2 * BANK], psum[:, 3, :]).then_inc(y_dve, 1)

            dve.wait_ge(r_idx, 1)
            last_b = dve.value_load(last_i[0:1, 0:1], min_val=NE - 1, max_val=NB - 2)
            copy_xT(0)
            hidden(0)
            copy_xT(1)

            def block_of(b, first=False):
                hidden(b + 1)
                copy_xT(b + 2)
                copy_y(b, first)

            block_of(0, first=True)
            with dve.Fori(1, last_b) as b:
                block_of(b)
            copy_y(last_b)

            for t in range(T):
                dve.wait_ge(s_y[t % 4], 16 * (t // 4 + 3))
                dve.scalar_tensor_tensor(h2[:, t, :], y_tiles[:, t, 0, :], gates[:, t, 0:1], h2[:, t, :], ALU.mult,
                                         ALU.add).then_inc(f_part, 1)
                dve.wait_ge(f_part, t + 1)
                dve.scalar_tensor_tensor(h2[:, t, :], y_tiles[:, t, 1, :], gates[:, t, 1:2], h2[:, t, :], ALU.mult,
                                         ALU.add).then_inc(f_out, 1)

        @block.gpsimd
        def _(pool):
            pool.sem_inc(c_fsaved, 32)
            pool.memset(ident[:, :], 0.0).then_inc(s_ident, 1)
            pool.wait_ge(s_ident, 1)
            pool.affine_select(out=ident[:, :], in_=ident[:, :], compare_op=ALU.not_equal, fill=1.0, base=0,
                               pattern=[[-1, P]], channel_multiplier=1).then_inc(s_ident, 1)
            pool.wait_ge(s_dve_const, 1)
            for t in range(T):
                pool.wait_ge(n_ms, t + 1)
                pool.tensor_tensor(rstd[:, t:t + 1], ms[:, t:t + 1], mhalf[:, 0:1], ALU.pow).then_inc(n_rstd, 1)
            pool.wait_ge(s_lines_in, 32)
            pool.memset(t5_sb[:, :], 0.0)
            pool.memset(ca_sb[:, :], 0.0).then_inc(s_ident, 1)
            pool.wait_ge(s_ident, 3)
            for lo, hi, bucket in t5_runs(-(S - 1), P):
                run = t5_sb[:, P - hi:P - lo]
                last = pool.tensor_scalar(run, run, lines_in[:, bucket:bucket + 1], None, ALU.add)
            last.then_inc(s_lines, 1)
            near = P + CLIP
            pool.tensor_scalar(ca_sb[:, near:CA_LINE], ca_sb[:, near:CA_LINE], lines_in[:, T5_BUCKETS:T5_BUCKETS + 1],
                               None, ALU.add)
            pool.tensor_copy(ca_sb[:, 0:near], lines_in[:, T5_BUCKETS:T5_BUCKETS + near][:, ::-1]) \
                .then_inc(s_lines, 1)
            pool.iota(iota_f[:, :], [[1, P]], base=0, channel_multiplier=0, allow_small_or_imprecise_dtypes=True)
            pool.iota(part_id[:, :], [[1, 1]], base=1, channel_multiplier=1, allow_small_or_imprecise_dtypes=True)
            pool.iota(tile_id[:, :], [[1, T]], base=0, channel_multiplier=0, allow_small_or_imprecise_dtypes=True)
            pool.memset(ones_b[:, :], 1.0).then_inc(s_ident, 1)
            pool.wait_ge(s_ident, 4)
            pool.affine_select(out=tri[:, :], in_=ones_b[:, :], compare_op=ALU.is_gt, fill=0.0, base=0,
                               pattern=[[1, P]], channel_multiplier=-1).then_inc(s_pool_const, 1)

            def stage_plain(a, p):
                for first, stage in ((a.q, q_stage), (a.k, k_stage)):
                    pool.tensor_copy(stage, proj[:, :, cols(first, p)]).then_inc(a.s["staged"], 1)

            def root_mean_squares(a, p):
                pool.wait_ge(a.s["qk_ms_ready"], p * 2 + 4)
                pool.tensor_tensor(qk_rstd[:, :, :], qk_ms[:, :, :], mhalf[:, :].rearrange("p (a b) -> p a b", a=2),
                                   ALU.pow).then_inc(a.s["qk_rstd_ready"], 1)

            def stage_normed(a, p, part_no):
                n, h = part_no // 2, part_no % 2
                first, stage = ((a.q, q_stage), (a.k, k_stage))[n]
                if part_no == 0:
                    pool.wait_ge(a.s["qk_rstd_ready"], p + 1)
                r = qk_rstd[:, n, h:2 * T:2]
                last = pool.tensor_tensor(stage[:, :, h * HEAD:(h + 1) * HEAD], proj[:, :, cols(first + h * HEAD, p, HEAD)],
                                          bass.AP(r.tensor, r.offset, [*[list(d) for d in r.ap], [0, HEAD]]), ALU.mult)
                if h == 1:
                    last.then_inc(a.s["staged"], 1)

            def keep_earlier(buf, t, wait, done, value):
                diag = work[:, buf, t * P:(t + 1) * P]
                wait_alone(pool, wait, value)
                pool.affine_select(out=diag, in_=diag, compare_op=ALU.is_gt, fill=0.0, base=0, pattern=[[-1, P]],
                                   channel_multiplier=1).then_inc(done, 1)

            pool.wait_ge(acc_act, 2 + CH * T // 2)
            pool.wait_ge(acc_dve, 2 + CH * T // 2)
            stage_plain(SB, 0)
            with pool.Fori(0, SB.pairs) as p:
                for s in range(SB.units + 1):
                    if s < SB.units:
                        keep_earlier(2 + s % 2, s // 2, SBS["sp_ready"], SBS["sp_masked"], p * SB.units + (s + 1))
                    if s >= 1:
                        keep_earlier((s - 1) % 2, (s - 1) // 2, SBS["w_exp"], SBS["p_ready"], p * SB.units + s)
                    if s == 4:
                        pool.wait_ge(SBS["k_tp"], p + 1)
                        stage_plain(SB, p + 1)

            pool.wait_ge(SBS["o_read"], 2 + SB.pairs * SB.results)
            root_mean_squares(DF, 0)
            for n in range(4):
                stage_normed(DF, 0, n)
            with pool.Fori(0, DF.pairs) as p:
                for s in range(T + 4):
                    if 3 <= s < T + 3:
                        t = s - 3
                        pool.wait_ge(DFS["yd_ms_ready"], p * T + (t + 1))
                        pool.tensor_tensor(yd_rstd[:, t % 2:t % 2 + 1], yd_ms[:, t % 2:t % 2 + 1], mhalf[:, 0:1],
                                           ALU.pow).then_inc(DFS["yd_rstd_ready"], 1)
                    if s == 3:
                        pool.wait_ge(DFS["k_tp"], p + 1)
                        root_mean_squares(DF, p + 1)
                    if 4 <= s < 8:
                        stage_normed(DF, p + 1, s - 4)
            pool.wait_ge(DFS["merged_ready"], DF.pairs * DF.results)
            root_mean_squares(CA, 0)
            for n in range(4):
                stage_normed(CA, 0, n)
            with pool.Fori(0, CA.pairs) as p:
                pool.wait_ge(CAS["k_tp"], p + 1)
                root_mean_squares(CA, p + 1)
                for n in range(4):
                    stage_normed(CA, p + 1, n)

            pool.wait_ge(CAS["o_read"], 2 + CA.pairs * CA.results)
            with pool.Fori(0, T // 2) as i:
                for j in range(2):
                    pool.wait_ge(c_mT_act, i * 2 + (j + 1))
                    pool.tensor_copy(m_stage[:, j, :], merged[:, bass.ds(i * 2 + j, 1), :].rearrange("p a b -> p (a b)")) \
                        .then_inc(c_stage, 1)
                    pool.wait_ge(c_ms, i * 2 + (j + 1))
                    pool.tensor_tensor(rstd[:, bass.ds(i * 2 + j, 1)], ms[:, bass.ds(i * 2 + j, 1)], mhalf[:, 0:1],
                                       ALU.pow).then_inc(c_rstd, 1)

            pool.wait_ge(c_h2, 2 * T + 2)
            pool.memset(xg, 0.0).then_inc(xg_zero, 1)
            pool.wait_ge(r_table, 1)
            pool.wait_ge(xg_zero, 1)
            pool.wait_ge(c_fsaved, 16 * T + 32)

            def gather(b):
                pool.tensor_copy(tok_col[:, :], row_i[:, 0, bass.ds(b, 1)]).then_inc(tok_ready, 1)
                wait_alone(pool, tok_ready, b + 1)
                pool.indirect_dma_start(out=xg, out_offset=None, in_=f_rows,
                                        in_offset=bass.IndirectOffsetOnAxis(ap=tok_col[:, 0:1], axis=0),
                                        bounds_check=S - 1, oob_is_err=False).then_inc(xg_landed, 16)

            def scatter(b):
                pool.wait_ge(y_act, b + 2)
                pool.wait_ge(y_dve, b + 2)
                pool.tensor_copy(row_col[:, :], row_i[:, 1, bass.ds(b, 1)]).then_inc(row_ready, 1)
                wait_alone(pool, row_ready, b + 1)
                pool.indirect_dma_start(out=y_rows, out_offset=bass.IndirectOffsetOnAxis(ap=row_col[:, 0:1], axis=0),
                                        in_=y_sb, in_offset=None, bounds_check=TOP * S - 1,
                                        oob_is_err=False).then_inc(y_stored, 16)

            last_b = pool.value_load(last_i[0:1, 0:1], min_val=NE - 1, max_val=NB - 2)
            gather(0)
            pool.wait_ge(x_tp, 1)
            gather(1)
            with pool.Fori(1, last_b + 1) as b:
                pool.wait_ge(x_tp, b + 1)
                gather(b + 1)
                scatter(b - 1)
            scatter(last_b)


_INS = ['x', 't5_bias', 'attn_norm', 'w_in', 'diff_qk_norm', 'diff_lambda', 'diff_subln', 'ca_qk_norm',
        'ca_rel_bias', 'w_out', 'ffn_norm', 'router_group_w', 'router_group_b', 'router_expert_w',
        'router_expert_b', 'expert_w_gate', 'expert_w_up', 'expert_w_down']
_OUTS = [((1, 1024, 1024), 'float32')]


def kernel(**inputs):
    import numpy as _np
    import concourse.bacc as _bacc
    from concourse import mybir as _mybir
    from concourse.bass_utils import run_bass_kernel_spmd as _run

    nc = _bacc.Bacc("TRN2", target_bir_lowering=False, num_devices=1)
    arrays, args = {}, []
    for name in _INS:
        a = _np.ascontiguousarray(inputs[name])
        arrays[f"in_{name}_dram"] = a
        args.append(nc.dram_tensor(f"in_{name}_dram", a.shape, _mybir.dt.from_np(a.dtype), kind="ExternalInput").ap())
    for i, (shape, dtype) in enumerate(_OUTS):
        dt = _mybir.dt.from_np(_np.dtype(dtype))
        args.append(nc.dram_tensor(f"out_{i}_dram", shape, dt, kind="ExternalOutput").ap())
    hybrid_block(nc, *args)
    r = _run(nc, [arrays], core_ids=[0])
    got = tuple(r.results[0][f"out_{i}_dram"] for i in range(len(_OUTS)))
    return got[0]
```

```python
import math
from contextlib import ExitStack

import numpy as np

import concourse.bass as bass
from concourse import mybir

ALU = mybir.AluOpType
ACT = mybir.ActivationFunctionType
AX = mybir.AxisListType
F32 = mybir.dt.float32
F32R = mybir.dt.float32r
BF16 = mybir.dt.bfloat16
I32 = mybir.dt.int32
U32 = mybir.dt.uint32

P = 128
BANK = 512
EPS = 1e-6
MASKED = -1e30
LOWEST = -3e38
LAM_INIT = 0.8 - 0.6 * math.exp(-0.3 * 0)
HEAD = 64
SCALE = HEAD ** -0.5
T5_BUCKETS, T5_MAX_DIST = 32, 256
CLIP = 128
BAND = 4
TOP = 2


def t5_runs(lo, hi):
    half = T5_BUCKETS // 2
    exact = half // 2
    runs = []
    for rel in range(lo, hi):
        n = abs(rel)
        if n < exact:
            b = n
        else:
            b = exact + int(np.float32(np.log(np.float32(n / exact))) / np.float32(math.log(T5_MAX_DIST / exact))
                            * np.float32(half - exact))
            b = min(b, half - 1)
        b += half if rel > 0 else 0
        if runs and runs[-1][2] == b:
            runs[-1][1] = rel + 1
        else:
            runs.append([rel, rel + 1, b])
    return runs


def hybrid_block(nc, x, t5_bias, attn_norm, w_in, diff_qk_norm, diff_lambda, diff_subln, ca_qk_norm,
                 ca_rel_bias, w_out, ffn_norm, group_w, group_b, expert_w, expert_b, w_gate, w_up, w_down, out):
    _, S, D = x.shape
    QKV = w_in.shape[2]
    NE, _, DE = w_gate.shape[1:]
    NG = group_w.shape[2]
    EG = NE // NG
    T = S // P
    KD = D // P
    KE = DE // P
    CH = QKV // BANK
    NR = NG + NE
    NB = NE + TOP * S // P
    SBW = D // 4
    SB_Q, SB_K, SB_V = 0, SBW, 2 * SBW
    DF_Q, DF_K, DF_V = 3 * SBW, 5 * SBW, 7 * SBW
    CA_Q, CA_K, CA_V = 9 * SBW, 10 * SBW, 11 * SBW
    SB_O, DF_O, CA_O = 0, SBW, 3 * SBW
    SB_PAIRS, DF_PAIRS, CA_PAIRS = SBW // P, 2 * SBW // P, SBW // P
    NH = ca_rel_bias.shape[2]

    T5_LINE = S + P - 1
    CA_W = (BAND + 1) * P
    CA_LINE = CA_W + P - 1

    x_rows = x[0]
    t5_line = nc.dram_tensor("t5_line", [NH, T5_LINE + 1], F32).ap()
    ca_line = nc.dram_tensor("ca_line", [NH, CA_LINE + 1], F32).ap()
    f_rows = nc.dram_tensor("f_rows", [S, D], F32).ap()
    y_rows = nc.dram_tensor("y_rows", [TOP * S, D], F32).ap()

    with ExitStack() as ctx:
        def sb(name, shape, dt=F32):
            return ctx.enter_context(nc.sbuf_tensor(name, shape, dt))

        def sem(name):
            return ctx.enter_context(nc.semaphore(name))

        ARENA = 49152
        arena = sb("arena", [P, ARENA])
        arena_at = nc.sbuf_base - 4 * ARENA

        def rounded(name, first, *dims):
            return nc.alloc_sbuf_tensor_at(name, [P, *dims], F32R, offset=arena_at + 4 * first)

        def part(first, *dims, dt=F32):
            n = int(np.prod(dims)) * (2 if dt == BF16 else 4) // 4
            v = arena[:, first:first + n]
            if dt != F32:
                v = v.bitcast(dt)
            if len(dims) == 1:
                return v
            names = "abcd"[:len(dims)]
            sizes = {c: d for c, d in zip(names[1:], dims[1:])}
            return v.rearrange(f"p ({' '.join(names)}) -> p {' '.join(names)}", **sizes)

        proj = part(0, T, QKV)
        x_all = part(16384, T, D)
        aT_hi = rounded("aT_hi", 24576, KD, S)
        merged = part(24576, T, D)
        aT_lo = rounded("aT_lo", 32768, KD, S)
        w_in_ring = part(40960, 2, KD // 2, BANK)
        w_in_lo = [rounded(f"w_in_lo{h}", 40960 + h * 2048, KD // 2, BANK) for h in range(2)]
        w_in_hi = [rounded(f"w_in_hi{h}", 45056 + h * 2048, KD // 2, BANK) for h in range(2)]
        a_buf = part(0, 2, D)
        norm_junk = part(2 * D, D)
        t5_sb = part(3 * QKV + 3 * BANK, T5_LINE + 1)[0:NH]
        ca_sb = part(4 * QKV + 3 * BANK, CA_LINE + 1)[0:NH]
        lam_in = part(4 * QKV + 3 * BANK + CA_LINE + 1, 4 * HEAD)
        lam_junk = part(4 * QKV + 3 * BANK + CA_LINE + 1 + 4 * HEAD, HEAD)
        lines_in = part(5 * QKV - 304, T5_BUCKETS + 2 * CLIP + 1)[0:NH]
        q_stage, k_stage = part(32768, T, P), part(33792, T, P)
        squares = part(32768, 2, T, P)
        qT_hi, qT_lo = rounded("qT_hi", 34816, S), rounded("qT_lo", 35840, S)
        kT_hi, kT_lo = rounded("kT_hi", 36864, S), rounded("kT_lo", 37888, S)
        df_bias = part(38912, S)
        ca_bias = [part(39936, CA_W), part(48128, CA_W)]
        work = part(40960, 6, S)
        pt_sb = part(47104, 2, BANK)
        w_out_sb = part(0, KD, D)
        h2 = part(32768, T, D)
        m_stage = part(22528, 2, D)
        mT = part(40960, 2, KD, P)
        f_buf = part(43008, 2, D)
        fT = part(45056, KD, P)
        out_junk = part(46080, D)
        gu_ring = part(0, 2, KD, 2 * DE)
        gu_first = part(8192, KD, 2 * DE)
        dn_ring = part(2 * KD * 2 * DE, 3, KE, D)
        xg = part(40960, D)
        xT = part(41984, KD, P)
        silu = part(43008, DE)
        hid = part(43520, DE)
        hT = part(44032, KE, P)
        y_sb = part(44544, D)
        pos_hot = part(28672, TOP, T, P, dt=BF16)
        blk_hot = part(29696, TOP, T, NB)
        blk_vals = part(30464, TOP, T, 3 * NB, dt=BF16).rearrange("p c t (a b) -> p c t a b", a=3)
        hot = part(31616, TOP, T, NE)
        picked = part(32128, TOP, T, NE)
        be_cmp = part(45568, NB, NE)[0:1]
        e_all = part(47104, T, NG, EG)
        row_f = part(47488, 2, NB)
        logits = part(47616, T, NR)
        y_tiles = part(0, T, TOP, D)

        ident = sb("ident", [P, P])
        attn_gain = sb("attn_gain", [P, D])
        subln = sb("subln", [P, 2 * HEAD])
        qk_gain = sb("qk_gain", [P, 4])
        lam_sum = sb("lam_sum", [P, 2])
        lam_exp = sb("lam_exp", [P, 2])
        neg_lam = sb("neg_lam", [P, 1])
        ones = sb("ones", [P, 1])
        mhalf = sb("mhalf", [P, 2 * T * 2])
        ss = sb("ss", [P, T])
        ms = sb("ms", [P, T])
        rstd = sb("rstd", [P, T])
        qk_ss = sb("qk_ss", [P, 2, 2 * T])
        qk_ms = sb("qk_ms", [P, 2, 2 * T])
        qk_rstd = sb("qk_rstd", [P, 2, 2 * T])
        low = sb("low", [P, 4, 2])
        total = sb("total", [P, 4, 2])
        inv = sb("inv", [P, 4, 2])
        mix = sb("mix", [P, 4])
        yd = sb("yd", [P, 2, 2 * HEAD])
        yd_junk = sb("yd_junk", [P, 2 * HEAD])
        yd_ss = sb("yd_ss", [P, 2])
        yd_ms = sb("yd_ms", [P, 2])
        yd_rstd = sb("yd_rstd", [P, 2])
        w_r = sb("w_r", [P, KD, NR])
        b_r = sb("b_r", [P, NR])
        g8 = sb("g8", [P, T, 8])
        g_top = sb("g_top", [P, T, 8])
        g_idx = sb("g_idx", [P, T, 8], U32)
        e_top = sb("e_top", [P, T, 8])
        e_idx = sb("e_idx", [P, T, 8], U32)
        g_sel = sb("g_sel", [P, T])
        g_exp = sb("g_exp", [P, T, NG])
        g_sum = sb("g_sum", [P, T])
        g_w = sb("g_w", [P, T])
        g_hot = sb("g_hot", [P, T, NG])
        e8 = sb("e8", [P, T, EG])
        e_gap = sb("e_gap", [P, T])
        e_sec = sb("e_sec", [P, T])
        e_den = sb("e_den", [P, T])
        e_inv = sb("e_inv", [P, T])
        gates = sb("gates", [P, T, TOP])
        e_idf = sb("e_idf", [P, T, TOP])
        eid = sb("eid", [P, T, TOP])
        hot_sum = sb("hot_sum", [P, T, NE], BF16)
        iota_f = sb("iota_f", [P, P])
        part_id = sb("part_id", [P, 1])
        tri = sb("tri", [P, P], BF16)
        ones_b = sb("ones_b", [P, P], BF16)
        tile_id = sb("tile_id", [P, T])
        cnt_i = sb("cnt_i", [P, NE], I32)
        nblk = sb("nblk", [P, NE])
        blk_end = sb("blk_end", [P, NE])
        blk_start = sb("blk_start", [P, NE])
        rank = sb("rank", [P, TOP, T])
        rank_i = sb("rank_i", [P, TOP, T], I32)
        hi_i = sb("hi_i", [P, TOP, T], I32)
        lo_i = sb("lo_i", [P, TOP, T], I32)
        hi_f = sb("hi_f", [P, TOP, T])
        lo_f = sb("lo_f", [P, TOP, T])
        first_blk = sb("first_blk", [P, TOP, T])
        blk = sb("blk", [P, TOP, T])
        empty = sb("empty", [P, NB])
        row_i = sb("row_i", [P, 2, NB], I32)
        be_f = sb("be_f", [1, NB])
        be_i = sb("be_i", [1, NB], I32)
        last_i = sb("last_i", [1, 1], I32)
        tok_col = sb("tok_col", [P, 1], I32)
        row_col = sb("row_col", [P, 1], I32)

        psum = ctx.enter_context(nc.psum_tensor("psum", [P, 8, BANK], F32))

        def banks(first, n):
            return psum[:, first:first + n, :].rearrange("p a b -> p (a b)")

        s_const = sem("s_const")
        s_ident = sem("s_ident")
        s_waits_met = sem("s_waits_met")
        s_pool_const = sem("s_pool_const")
        s_lines_in = sem("s_lines_in")
        s_lines = sem("s_lines")
        s_lines_out = sem("s_lines_out")
        s_dve_const = sem("s_dve_const")
        s_lam_sum = sem("s_lam_sum")
        s_lam_exp = sem("s_lam_exp")
        s_lam = sem("s_lam")
        s_x = [sem(f"s_x{i}") for i in range(4)]
        n_sq = sem("n_sq"); n_ms = sem("n_ms"); n_rstd = sem("n_rstd"); n_a = sem("n_a")
        n_tp = sem("n_tp"); n_aT_act = sem("n_aT_act"); n_aT_dve = sem("n_aT_dve")
        n_aT_lo = n_aT_dve
        w_landed = [sem(f"w_landed{i}") for i in range(2)]
        w_hi = sem("w_hi"); w_lo = sem("w_lo"); w_half_used = sem("w_half_used")
        acc_ready = sem("acc_ready"); acc_act = sem("acc_act"); acc_dve = sem("acc_dve")

        def attention_sems(kind):
            names = ["squared", "qk_ms_ready", "qk_rstd_ready", "staged", "q_tp", "k_tp", "qT_ready",
                     "kT_ready", "z_ready", "z_read", "p_ready", "pt0", "pt1", "pt_sb0", "pt_sb1",
                     "o_ready", "o_read", "bias_landed", "bias_ready", "abs_done", "exp_done", "lp_ready",
                     "sp_ready", "sp_masked", "scanned", "w_exp", "summed", "inverse", "mixed", "yd_ready",
                     "yd_ss_ready", "yd_ms_ready", "yd_rstd_ready", "merged_ready"]
            used = {"sb": set(names) - {"squared", "qk_ms_ready", "qk_rstd_ready", "bias_landed", "bias_ready",
                                        "summed", "inverse", "mixed", "yd_ready", "yd_ss_ready", "yd_ms_ready",
                                        "yd_rstd_ready", "merged_ready"},
                    "df": set(names) - {"abs_done", "exp_done", "lp_ready", "sp_ready", "sp_masked", "scanned",
                                        "w_exp"},
                    "ca": set(names) - {"abs_done", "exp_done", "lp_ready", "sp_ready", "sp_masked", "scanned",
                                        "w_exp", "mixed", "yd_ready", "yd_ss_ready", "yd_ms_ready",
                                        "yd_rstd_ready", "merged_ready"}}[kind]
            return {n: sem(f"{kind}_{n}") for n in names if n in used}

        SBS, DFS, CAS = attention_sems("sb"), attention_sems("df"), attention_sems("ca")

        s_wout = sem("s_wout"); s_x_again = sem("s_x_again")
        c_stage = sem("c_stage"); c_tp = sem("c_tp"); c_mT_act = sem("c_mT_act"); c_mT_dve = sem("c_mT_dve")
        c_acc = sem("c_acc"); c_h2 = sem("c_h2"); c_sq = sem("c_sq"); c_ms = sem("c_ms"); c_rstd = sem("c_rstd")
        c_f = sem("c_f"); c_fsaved = sem("c_fsaved"); c_ftp = sem("c_ftp")
        c_fT_act = sem("c_fT_act"); c_fT_dve = sem("c_fT_dve"); c_lg = sem("c_lg"); c_logits = sem("c_logits")
        r_dve = sem("r_dve"); r_gexp_in = sem("r_gexp_in"); r_gexp = sem("r_gexp"); r_esec_in = sem("r_esec_in")
        r_esec = sem("r_esec"); r_hot = sem("r_hot"); r_counted = sem("r_counted"); r_vals = sem("r_vals")
        r_rows = sem("r_rows"); r_table = sem("r_table"); r_idx = sem("r_idx"); s_gain = sem("s_gain")
        gate_landed = sem("gate_landed"); up_landed = sem("up_landed"); down_landed = sem("down_landed")
        tok_ready = sem("tok_ready"); row_ready = sem("row_ready"); xg_zero = sem("xg_zero"); xg_landed = sem("xg_landed")
        x_tp = sem("x_tp"); xT_act = sem("xT_act"); xT_dve = sem("xT_dve")
        g_ready = sem("g_ready"); u_ready = sem("u_ready"); silu_ready = sem("silu_ready")
        h_ready = sem("h_ready"); h_tp = sem("h_tp"); hT_ready = sem("hT_ready")
        y_ready = sem("y_ready"); y_act = sem("y_act"); y_dve = sem("y_dve"); y_stored = sem("y_stored")
        s_y = s_x
        f_part = sem("f_part"); f_out = sem("f_out"); out_stored = sem("out_stored")

        class Plan:

            def __init__(self, kind, s, q, k, v, o, pairs):
                self.kind, self.s, self.q, self.k, self.v, self.o, self.pairs = kind, s, q, k, v, o, pairs
                self.units = 2 * T
                self.results = T if kind == "df" else 2 * T

            def tile(self, r):
                return r if self.kind == "df" else r // 2

            def keys(self, t):
                first = max(0, t - BAND) if self.kind == "ca" else 0
                return first, t + 1 - first

            def groups(self, r):
                n = self.keys(self.tile(r))[1]
                return [list(range(g, min(g + 4, n))) for g in range(0, n, 4)]

            def group_no(self, g, r):
                has = [len(self.groups(i)) > g for i in range(self.results)]
                return sum(has[:r]), sum(has)

        SB = Plan("sb", SBS, SB_Q, SB_K, SB_V, SB_O, SB_PAIRS)
        DF = Plan("df", DFS, DF_Q, DF_K, DF_V, DF_O, DF_PAIRS)
        CA = Plan("ca", CAS, CA_Q, CA_K, CA_V, CA_O, CA_PAIRS)

        def cols(first, p, width=P, step=P):
            return bass.ds(p * step + first, width)

        def wait_alone(eng, semaphore, value):
            eng.wait_ge(semaphore, value)
            eng.sem_inc(s_waits_met, 1)

        def wait_slot(eng, a, p, r, slots):
            back = r - slots if r >= slots else max(i for i in range(a.results) if i % slots == r % slots)
            g = len(a.groups(back)) - 1
            before, per = a.group_no(g, back)
            eng.wait_ge(a.s[f"pt{g}"], p * per + (before + 1 + (per if r >= slots else 0)))

        block = ctx.enter_context(nc.Block())

        @block.sync
        def _(sp):
            for i in range(4):
                sp.dma_start(x_all[:, i, :], x_rows[i * P:(i + 1) * P, :]).then_inc(s_x[i], 16)
            sp.dma_start(attn_gain[:, :], attn_norm.to_broadcast([P, D])).then_inc(s_gain, 16)
            for i in range(4):
                sp.wait_ge(s_x[i], 16)
                sp.dma_start(x_all[:, 4 + i, :], x_rows[(4 + i) * P:(5 + i) * P, :]).then_inc(s_x[i], 16)
            w_in_tiles = w_in[0].rearrange("(h k p) n -> h p k n", p=P, h=2)
            for h in range(2):
                sp.dma_start(w_in_ring[:, h, :, :], w_in_tiles[h, :, :, 0:BANK]).then_inc(w_landed[h], 16)
            with sp.Fori(1, CH) as c:
                for h in range(2):
                    if h == 0:
                        sp.wait_ge(w_half_used, c)
                    else:
                        sp.wait_ge(acc_ready, c * T)
                    sp.dma_start(w_in_ring[:, h, :, :], w_in_tiles[h, :, :, bass.ds(c * BANK, BANK)]).then_inc(w_landed[h], 16)

            def bias_loads(a, line, tiles):
                with sp.Fori(0, a.pairs) as p:
                    sp.wait_ge(a.s["z_read"], p * a.units + 2)
                    for m, tile in enumerate(tiles):
                        src = bass.AP(line.tensor, (p * len(tiles) + m) * line.shape[1], [[1, P], [1, tile.shape[1]]])
                        sp.dma_start(tile, src).then_inc(a.s["bias_landed"], 16)

            sp.wait_ge(n_a, T)
            sp.dma_start(attn_gain[:, :], ffn_norm.to_broadcast([P, D])).then_inc(s_gain, 16)
            sp.wait_ge(s_lines_out, 32)
            sp.wait_ge(acc_act, (CH + 1) * T // 2)
            sp.wait_ge(acc_dve, (CH + 1) * T // 2)
            bias_loads(DF, t5_line, [df_bias])
            bias_loads(CA, ca_line, ca_bias)

            sp.wait_ge(CAS["o_read"], 2 + CA.pairs * CA.results)
            sp.dma_start(w_out_sb, w_out[0].rearrange("(k p) n -> p k n", p=P)).then_inc(s_wout, 16)
            for j in range(2):
                half = T // 2 * P
                sp.dma_start(h2[:, j * (T // 2):(j + 1) * (T // 2), :],
                             x_rows[j * half:(j + 1) * half, :].rearrange("(t p) d -> p t d", p=P)).then_inc(s_x_again, 16)
            sp.dma_start(gu_first[:, :, 0:DE], w_gate[0, 0].rearrange("(k p) n -> p k n", p=P)).then_inc(gate_landed, 16)
            sp.dma_start(gu_first[:, :, DE:2 * DE], w_up[0, 0].rearrange("(k p) n -> p k n", p=P)).then_inc(up_landed, 16)
            sp.dma_start(dn_ring[:, 0, :, :], w_down[0, 0].rearrange("(k p) n -> p k n", p=P)).then_inc(down_landed, 16)

            sp.wait_ge(r_idx, 1)
            sp.wait_ge(c_acc, 4 + 2 * T)
            last_b = sp.value_load(last_i[0:1, 0:1], min_val=NE - 1, max_val=NB - 2)
            with sp.Fori(1, last_b + 1) as b:
                e = sp.value_load(be_i[0:1, bass.ds(b, 1)], min_val=0, max_val=NE - 1)
                slot = (b + 1) % 2
                sp.wait_ge(xg_landed, b * 16 + 16)
                wait_alone(sp, u_ready, b)
                sp.wait_ge(gate_landed, b * 16)
                sp.dma_start(gu_ring[:, slot, :, 0:DE], w_gate[0, e, :, :].rearrange("(k p) n -> p k n", p=P)) \
                    .then_inc(gate_landed, 16)
                sp.wait_ge(up_landed, b * 16)
                sp.dma_start(gu_ring[:, slot, :, DE:2 * DE], w_up[0, e, :, :].rearrange("(k p) n -> p k n", p=P)) \
                    .then_inc(up_landed, 16)
                sp.wait_ge(y_ready, b * 2)
                sp.wait_ge(down_landed, b * 16)
                sp.dma_start(dn_ring[:, b % 3, :, :], w_down[0, e, :, :].rearrange("(k p) n -> p k n", p=P)) \
                    .then_inc(down_landed, 16)

            sp.wait_ge(y_stored, last_b * 16 + 16)
            sp.wait_ge(y_ready, last_b * 2 + 6)
            y_t = y_rows.rearrange("(t c p) d -> p t c d", p=P, c=TOP)
            for i in range(4):
                sp.dma_start(y_tiles[:, i, :, :], y_t[:, i, :, :]).then_inc(s_y[i], 16)
            for i in range(4):
                sp.wait_ge(s_y[i], 48)
                sp.dma_start(y_tiles[:, 4 + i, :, :], y_t[:, 4 + i, :, :]).then_inc(s_y[i], 16)
            out_t = out[0].rearrange("(t p) d -> t p d", p=P)
            for t in range(T):
                sp.wait_ge(f_out, t + 1)
                sp.dma_start(out_t[t], h2[:, t, :]).then_inc(out_stored, 16)
            sp.wait_ge(out_stored, 16 * T)

        @block.tensor
        def _(pe):
            for a in (SB, DF, CA):
                for g in range(2):
                    pe.sem_inc(a.s[f"pt{g}"], a.group_no(g, 0)[1])
            pe.sem_inc(c_acc, 4)
            pe.sem_inc(u_ready, 1)
            pe.sem_inc(y_ready, 4)
            pe.wait_ge(s_ident, 2)

            def transpose_tile(src, first_bank):
                for k in range(KD):
                    last = pe.transpose(psum[:, first_bank + k // 4, (k % 4) * P:(k % 4 + 1) * P],
                                        src[:, k * P:(k + 1) * P], ident[:, :])
                return last

            with pe.Fori(0, T // 2) as i:
                for j in range(2):
                    pe.wait_ge(n_a, i * 2 + (j + 1))
                    pe.wait_ge(n_aT_act, i * 2 + (j + 1))
                    pe.wait_ge(n_aT_dve, i * 2 + (j + 1))
                    transpose_tile(a_buf[:, j, :], 2 * j).then_inc(n_tp, 1)

            def split_product(out, pairs, start, stop):
                n = 0
                for l_hi, l_lo, r_hi, r_lo in pairs:
                    for lhs, rhs in ((l_hi, r_hi), (l_hi, r_lo), (l_lo, r_hi)):
                        last = pe.matmul(out, lhs, rhs, start=start and n == 0,
                                         stop=stop and n == 3 * len(pairs) - 1)
                        n += 1
                return last

            pe.wait_ge(n_aT_act, 2 + T)
            pe.wait_ge(n_aT_lo, 2 + T)
            with pe.Fori(0, CH) as c:
                for h in range(2):
                    pe.wait_ge(w_lo, c * 2 + (h + 1))
                    for t in range(T):
                        if h == 0:
                            pe.wait_ge(acc_act if t % 2 == 0 else acc_dve, c * (T // 2) + (t // 2 + 1))
                        rows = range(h * KD // 2, (h + 1) * KD // 2)
                        last = split_product(psum[:, t, :],
                                             [(aT_hi[:, k, t * P:(t + 1) * P], aT_lo[:, k, t * P:(t + 1) * P],
                                               w_in_hi[h][:, k % (KD // 2), :], w_in_lo[h][:, k % (KD // 2), :])
                                              for k in rows], start=h == 0, stop=h == 1)
                        if h == 1:
                            last.then_inc(acc_ready, 1)
                    if h == 0:
                        last.then_inc(w_half_used, 1)

            def transpose_qk(a, p):
                pe.wait_ge(a.s["staged"], p * 2 + 2)
                pe.wait_ge(a.s["z_read"], p * a.units + 2)
                for stage, first, done in ((q_stage, 0, "q_tp"), (k_stage, 2, "k_tp")):
                    for t in range(T):
                        last = pe.transpose(psum[:, first + t // 4, (t % 4) * P:(t % 4 + 1) * P], stage[:, t, :],
                                            ident[:, :])
                    last.then_inc(a.s[done], 1)
                pe.wait_ge(a.s["qT_ready"], p * 2 + 2)
                pe.wait_ge(a.s["kT_ready"], p * 2 + 2)

            def logits_of(a, p, u):
                t, m = u // 2, u % 2
                first, n = a.keys(t)
                pe.wait_ge(a.s["z_read"], p * a.units + (u + 1))
                rows = slice(HEAD * m, HEAD * (m + 1))
                for c in range(0, n * P, BANK):
                    w = min(BANK, n * P - c)
                    q, k = slice(t * P, (t + 1) * P), slice(first * P + c, first * P + c + w)
                    last = split_product(psum[:, 2 * m + c // BANK, 0:w],
                                         [(qT_hi[rows, q], qT_lo[rows, q], kT_hi[rows, k], kT_lo[rows, k])],
                                         start=True, stop=True)
                last.then_inc(a.s["z_ready"], 1)

            def transpose_weights(a, p, r, weights):
                pe.wait_ge(a.s["p_ready"], p * a.results + (r + 1))
                groups = a.groups(r)
                for g, tiles in enumerate(groups):
                    before, per = a.group_no(g, r)
                    pe.wait_ge(a.s[f"pt_sb{g}"], p * per + (before + 1))
                    for c in tiles:
                        last = pe.transpose(psum[:, 4 + g, (c % 4) * P:(c % 4 + 1) * P], weights[:, c * P:(c + 1) * P],
                                            ident[:, :])
                    last.then_inc(a.s[f"pt{g}"], 1)

            def result_of(a, p, r):
                first, n = a.keys(a.tile(r))
                width = 2 * HEAD if a.kind == "df" else HEAD
                head = 0 if a.kind == "df" else HEAD * (r % 2)
                groups = a.groups(r)
                pe.wait_ge(a.s["o_read"], p * a.results + (r + 1))
                for g, tiles in enumerate(groups):
                    before, per = a.group_no(g, r)
                    pe.wait_ge(a.s[f"pt_sb{g}"], p * per + (before + 2))
                    for c in tiles:
                        last = pe.matmul(psum[:, 6 + r % 2, 0:width], pt_sb[:, g, (c % 4) * P:(c % 4 + 1) * P],
                                         proj[:, first + c, cols(a.v + head, p, width)], start=(c == 0), stop=(c == n - 1))
                last.then_inc(a.s["o_ready"], 1)

            pe.wait_ge(acc_act, (CH + 1) * T // 2)
            pe.wait_ge(acc_dve, (CH + 1) * T // 2)
            with pe.Fori(0, SB.pairs) as p:
                transpose_qk(SB, p)
                for s in range(SB.units + 2):
                    if s < SB.units:
                        logits_of(SB, p, s)
                    if s >= 2:
                        transpose_weights(SB, p, s - 2, work[:, (s - 2) % 2, :])
                        result_of(SB, p, s - 2)
            pe.wait_ge(SBS["o_read"], 2 + SB.pairs * SB.results)
            with pe.Fori(0, DF.pairs) as p:
                transpose_qk(DF, p)
                for s in range(T + 2):
                    if s >= 2:
                        transpose_weights(DF, p, s - 2, work[:, 2 * ((s - 2) % 3), :])
                    if s < T:
                        logits_of(DF, p, 2 * s)
                        logits_of(DF, p, 2 * s + 1)
                    if s >= 2:
                        result_of(DF, p, s - 2)
            pe.wait_ge(DFS["merged_ready"], DF.pairs * DF.results)
            with pe.Fori(0, CA.pairs) as p:
                transpose_qk(CA, p)
                for s in range(CA.units + 2):
                    if s >= 2:
                        transpose_weights(CA, p, s - 2, work[:, (s - 2) % 4, :])
                    if s < CA.units:
                        logits_of(CA, p, s)
                    if s >= 2:
                        result_of(CA, p, s - 2)
            pe.wait_ge(CAS["o_read"], 2 + CA.pairs * CA.results)

            def merged_tile(i, j):
                pe.wait_ge(c_stage, i * 2 + (j + 1))
                pe.wait_ge(c_mT_act, i * 2 + (j + 1))
                pe.wait_ge(c_mT_dve, i * 2 + (j + 1))
                transpose_tile(m_stage[:, j % 2, :], 0).then_inc(c_tp, 1)

            def out_tile(i, j):
                pe.wait_ge(c_mT_act, i * 2 + (j + 2))
                pe.wait_ge(c_mT_dve, i * 2 + (j + 2))
                for n in range(2):
                    pe.wait_ge(c_h2, i * 4 + (2 * j + n + 1))
                    for k in range(KD):
                        last = pe.matmul(psum[:, 2 + n, :], mT[:, j % 2, k, :], w_out_sb[:, k, n * BANK:(n + 1) * BANK],
                                         start=(k == 0), stop=(k == KD - 1))
                    last.then_inc(c_acc, 1)

            def f_tile(i, j):
                pe.wait_ge(c_f, i * 2 + (j + 1))
                pe.wait_ge(c_logits, i * 2 + (j + 1))
                transpose_tile(f_buf[:, j % 2, :], 4).then_inc(c_ftp, 1)

            def router_tile(i, j):
                pe.wait_ge(c_fT_act, i * 2 + (j + 1))
                pe.wait_ge(c_fT_dve, i * 2 + (j + 1))
                for k in range(KD):
                    last = pe.matmul(psum[:, 6, 0:NR], fT[:, k, :], w_r[:, k, :], start=(k == 0), stop=(k == KD - 1))
                last.then_inc(c_lg, 1)

            pe.wait_ge(s_wout, 16)
            merged_tile(0, 0)
            merged_tile(0, 1)
            out_tile(0, 0)
            with pe.Fori(0, T // 2 - 1) as i:
                for j in (1, 2):
                    merged_tile(i, j + 1)
                    out_tile(i, j)
                    f_tile(i, j - 1)
                    router_tile(i, j - 1)
            out_tile(T // 2 - 1, 1)
            for j in range(2):
                f_tile(T // 2 - 1, j)
                router_tile(T // 2 - 1, j)

            pe.wait_ge(r_hot, 1)
            pe.wait_ge(s_pool_const, 1)
            ranks = psum[:, 0, 0:T * NE].rearrange("p (t e) -> p t e", t=T)
            for t in range(T - 1):
                later = T - 1 - t
                rhs = bass.AP(hot_sum[:, t, :].tensor, t * NE, [[T * NE, P], [0, later], [1, NE]])
                pe.matmul(ranks[:, t + 1:T, :], ones_b[:, :], rhs, start=(t == 0), stop=False, skip_group_check=True)
            pe.matmul(ranks, tri[:, :], hot_sum[:, :, :], start=False, stop=True, skip_group_check=True)
            for t in range(T):
                last = pe.matmul(psum[:, 1, 0:NE], ones_b[:, :], hot_sum[:, t, :], start=(t == 0), stop=(t == T - 1))
            last.then_inc(r_counted, 1)
            pe.wait_ge(r_vals, 1)
            n = 0
            for t in range(T):
                for c in range(TOP):
                    last = pe.matmul(psum[:, 2, 0:3 * NB], pos_hot[:, c, t, :],
                                     blk_vals[:, c, t, :, :].rearrange("p a b -> p (a b)"),
                                     start=(n == 0), stop=(n == TOP * T - 1))
                    n += 1
            last.then_inc(r_rows, 1)

            def gather_tp(b):
                pe.wait_ge(xg_landed, b * 16 + 16)
                for k in range(KD):
                    last = pe.transpose(psum[:, 4 + k // 4, (k % 4) * P:(k % 4 + 1) * P], xg[:, k * P:(k + 1) * P],
                                        ident[:, :])
                last.then_inc(x_tp, 1)

            def gate_up(b, slot):
                pe.wait_ge(xT_act, b + 1)
                pe.wait_ge(xT_dve, b + 1)
                for part_no, landed, ready in ((0, gate_landed, g_ready), (1, up_landed, u_ready)):
                    pe.wait_ge(landed, b * 16 + 16)
                    for k in range(KD):
                        last = pe.matmul(psum[:, part_no, :], xT[:, k, :],
                                         gu_ring[:, slot, k, part_no * DE:(part_no + 1) * DE],
                                         start=(k == 0), stop=(k == KD - 1))
                    last.then_inc(ready, 1)

            def hidden_tp(b):
                pe.wait_ge(h_ready, b + 1)
                for k in range(KE):
                    last = pe.transpose(psum[:, 6, k * P:(k + 1) * P], hid[:, k * P:(k + 1) * P], ident[:, :])
                last.then_inc(h_tp, 1)

            def down(b, slot):
                pe.wait_ge(hT_ready, b + 1)
                pe.wait_ge(down_landed, b * 16 + 16)
                pe.wait_ge(y_act, b + 1)
                pe.wait_ge(y_dve, b + 1)
                for n in range(2):
                    for k in range(KE):
                        last = pe.matmul(psum[:, 2 + n, :], hT[:, k, :], dn_ring[:, slot, k, n * BANK:(n + 1) * BANK],
                                         start=(k == 0), stop=(k == KE - 1))
                    last.then_inc(y_ready, 1)

            pe.wait_ge(r_idx, 1)
            last_b = pe.value_load(last_i[0:1, 0:1], min_val=NE - 1, max_val=NB - 2)
            gather_tp(0)
            gate_up(0, 1)
            gather_tp(1)
            with pe.Fori(1, last_b + 1) as b:
                hidden_tp(b - 1)
                gate_up(b, (b + 1) % 2)
                gather_tp(b + 1)
                down(b - 1, (b + 2) % 3)
            hidden_tp(last_b)
            down(last_b, last_b % 3)

        @block.scalar
        def _(act):
            act.sem_inc(n_aT_act, 2)
            act.sem_inc(n_sq, 1)
            act.sem_inc(c_sq, 1)
            act.sem_inc(acc_act, T // 2)
            for a in (SB, DF, CA):
                act.sem_inc(a.s["pt_sb0"], 1)
            act.sem_inc(SBS["o_read"], 2)
            act.sem_inc(c_mT_act, 1)
            act.sem_inc(y_act, 1)
            act.dma_start(lines_in[:, 0:T5_BUCKETS], t5_bias.rearrange("b h -> h b"), allow_slow_non_contiguous=True) \
                .then_inc(s_lines_in, 16)
            act.dma_start(lines_in[:, T5_BUCKETS:], ca_rel_bias[0].rearrange("b h -> h b"),
                          allow_slow_non_contiguous=True).then_inc(s_lines_in, 16)
            act.dma_start(subln[:, :], diff_subln.to_broadcast([P, 2 * HEAD])).then_inc(s_const, 16)
            act.dma_start(lam_in[:, :], diff_lambda[0].rearrange("(o a) b -> o (a b)", o=1).to_broadcast([P, 4 * HEAD])) \
                .then_inc(s_const, 16)
            for half in range(2):
                for n, gain in enumerate((diff_qk_norm, ca_qk_norm)):
                    act.dma_start(qk_gain[HEAD * half:HEAD * (half + 1), 2 * n:2 * n + 2],
                                  gain[0].rearrange("a b -> b a"), allow_slow_non_contiguous=True).then_inc(s_const, 16)
            act.dma_start(w_r[:, :, 0:NG], group_w[0].rearrange("(k p) n -> p k n", p=P),
                          allow_slow_non_contiguous=True).then_inc(s_const, 16)
            act.dma_start(w_r[:, :, NG:NR], expert_w[0].rearrange("(k p) n -> p k n", p=P)).then_inc(s_const, 16)
            act.dma_start(b_r[:, 0:NG], group_b.to_broadcast([P, NG])).then_inc(s_const, 16)
            act.dma_start(b_r[:, NG:NR], expert_b.to_broadcast([P, NE])).then_inc(s_const, 16)

            def copy_half(dst, src, done):
                act.copy(dst, src).then_inc(done, 1)

            with act.Fori(0, T // 4) as i:
                for j in range(4):
                    act.wait_ge(s_x[j], i * 16 + 16)
                    act.wait_ge(n_sq, i * 4 + (j + 1))
                    act.activation(norm_junk, x_all[:, bass.ds(i * 4 + j, 1), :].rearrange("p a b -> p (a b)"), ACT.Square,
                                   accum_out=ss[:, bass.ds(i * 4 + j, 1)]).then_inc(n_sq, 1)
            with act.Fori(0, T // 2) as i:
                for j in range(2):
                    act.wait_ge(n_tp, i * 2 + (j + 1))
                    act.copy(aT_hi[:, :, bass.ds(i * 2 * P + j * P, P)],
                             banks(2 * j, 2).rearrange("p (a b) -> p a b", a=KD)).then_inc(n_aT_act, 1)

            def high_w_in(c, h):
                act.wait_ge(w_landed[h], c * 16 + 16)
                act.copy(w_in_hi[h][:, :, :], w_in_ring[:, h, :, :]).then_inc(w_hi, 1)

            def copy_proj(c, t):
                act.wait_ge(acc_ready, c * T + (t + 1))
                act.copy(proj[:, t, bass.ds(c * BANK, BANK)], psum[:, t, :]).then_inc(acc_act, 1)

            for h in range(2):
                high_w_in(0, h)
            act.wait_ge(s_lam_sum, 2)
            act.activation(lam_exp[:, :], lam_sum[:, :], ACT.Exp).then_inc(s_lam_exp, 1)
            act.wait_ge(s_lines, 2)
            act.dma_start(t5_line[:, 0:T5_LINE], t5_sb[:, 0:T5_LINE]).then_inc(s_lines_out, 16)
            act.dma_start(ca_line[:, 0:CA_LINE], ca_sb[:, 0:CA_LINE]).then_inc(s_lines_out, 16)
            act.wait_ge(s_lines_out, 32)
            with act.Fori(0, CH - 1) as c:
                copy_proj(c, 0)
                high_w_in(c + 1, 0)
                for t in range(2, T, 2):
                    copy_proj(c, t)
                high_w_in(c + 1, 1)
            for t in range(0, T, 2):
                copy_proj(CH - 1, t)

            def high_qk(a, p, q_gain, k_gain):
                for name, bank, gain, high in (("q", 0, q_gain, qT_hi), ("k", 2, k_gain, kT_hi)):
                    act.wait_ge(a.s[f"{name}_tp"], p + 1)
                    act.activation(high[:, :], banks(bank, 2), ACT.Copy, scale=gain).then_inc(a.s[f"{name}T_ready"], 1)

            def copy_pt0(a, p, r):
                before, per = a.group_no(0, r)
                w = len(a.groups(r)[0]) * P
                act.wait_ge(a.s["pt0"], p * per + (before + 1 + per))
                act.copy(pt_sb[:, 0, 0:w], psum[:, 4, 0:w]).then_inc(a.s["pt_sb0"], 1)

            def squares_of(a, p):
                for n, first in enumerate((a.q, a.k)):
                    act.wait_ge(a.s["qk_ms_ready"], p * 2 + 1)
                    act.activation(squares[:, n, :, :], proj[:, :, cols(first, p)], ACT.Square) \
                        .then_inc(a.s["squared"], 1)

            def exp_rows(a, p, u, slot, stat, m):
                t = u // 2
                w = a.keys(t)[1] * P
                act.wait_ge(a.s["z_read"], p * a.units + (u + 3))
                act.activation(work[:, slot, 0:w], work[:, slot, 0:w], ACT.Exp, bias=low[:, stat, m:m + 1], scale=-1.0,
                               accum_out=total[:, stat, m:m + 1]).then_inc(a.s["summed" if a.kind == "df" else "p_ready"], 1)

            def sb_softplus_tail(p, u):
                w, buf = SB.keys(u // 2)[1] * P, 2 + u % 2
                act.wait_ge(SBS["z_ready"], p * SB.units + (u + 1))
                act.wait_ge(SBS["z_read"], p * SB.units + (u + 1))
                act.activation(work[:, buf, 0:w], banks(2 * (u % 2), 2)[:, 0:w], ACT.Abs).then_inc(SBS["abs_done"], 1)
                act.wait_ge(SBS["abs_done"], p * SB.units + (u + 1))
                act.activation(work[:, buf, 0:w], work[:, buf, 0:w], ACT.Exp, scale=-1.0).then_inc(SBS["exp_done"], 1)
                act.wait_ge(SBS["exp_done"], p * SB.units + (u + 1))
                act.activation(work[:, buf, 0:w], work[:, buf, 0:w], ACT.Ln, bias=1.0).then_inc(SBS["lp_ready"], 1)

            def sb_weights(p, u):
                w, buf = SB.keys(u // 2)[1] * P, u % 2
                act.wait_ge(SBS["z_read"], p * SB.units + (u + 3))
                wait_slot(act, SB, p, u, 2)
                act.activation(work[:, buf, 0:w], work[:, 4 + buf, 0:w], ACT.Exp).then_inc(SBS["w_exp"], 1)

            def sb_merge(p, r):
                act.wait_ge(SBS["o_ready"], p * SB.results + (r + 1))
                act.copy(merged[:, r // 2, cols(SB_O + HEAD * (r % 2), p, HEAD)], psum[:, 6 + r % 2, 0:HEAD]) \
                    .then_inc(SBS["o_read"], 1)

            act.preload_act_table_set("natural_log_exp_and_others")
            def sb_pair(p, after):
                high_qk(SB, p, SCALE, 1.0)
                for s in range(SB.units + 3):
                    if s < SB.units:
                        sb_softplus_tail(p, s)
                    if 2 <= s < SB.units + 2:
                        copy_pt0(SB, p, s - 2)
                    if 1 <= s <= SB.units:
                        sb_weights(p, s - 1)
                    if s >= 3:
                        sb_merge(p, s - 3)
                    if s == 5 and after[0] is DF:
                        squares_of(*after)

            with act.Fori(0, SB.pairs - 1) as p:
                sb_pair(p, (SB, p + 1))
            sb_pair(SB.pairs - 1, (DF, 0))
            act.wait_ge(SBS["o_read"], 2 + SB.pairs * SB.results)
            act.preload_act_table_set("exp_and_others")
            def df_pair(p, after):
                high_qk(DF, p, qk_gain[:, 0:1], qk_gain[:, 1:2])
                for s in range(T + 2):
                    if s >= 2:
                        copy_pt0(DF, p, s - 2)
                    if s < T:
                        for m in range(2):
                            exp_rows(DF, p, 2 * s + m, 2 * (s % 3) + m, s % 4, m)
                    if s == 2:
                        squares_of(*after)

            with act.Fori(0, DF.pairs - 1) as p:
                df_pair(p, (DF, p + 1))
            df_pair(DF.pairs - 1, (CA, 0))
            act.wait_ge(DFS["merged_ready"], DF.pairs * DF.results)
            def ca_pair(p, after):
                high_qk(CA, p, qk_gain[:, 2:3], qk_gain[:, 3:4])
                for s in range(CA.units + 2):
                    if s >= 2:
                        copy_pt0(CA, p, s - 2)
                    if s < CA.units:
                        exp_rows(CA, p, s, s % 4, s % 4, 0)
                    if s == 4 and after:
                        squares_of(*after)

            with act.Fori(0, CA.pairs - 1) as p:
                ca_pair(p, (CA, p + 1))
            ca_pair(CA.pairs - 1, None)
            act.wait_ge(CAS["o_read"], 2 + CA.pairs * CA.results)

            def copy_mT(i, j):
                act.wait_ge(c_tp, i * 2 + (j + 1))
                act.wait_ge(c_acc, i * 4 + (2 * j + 2))
                act.copy(mT[:, j % 2, 0:4, :], psum[:, 0, :].rearrange("p (a b) -> p a b", a=4)).then_inc(c_mT_act, 1)

            def square_sum(i, j):
                act.wait_ge(c_h2, i * 4 + (2 * j + 4))
                act.wait_ge(c_sq, i * 2 + (j + 1))
                act.activation(out_junk, h2[:, bass.ds(i * 2 + j, 1), :].rearrange("p a b -> p (a b)"), ACT.Square,
                               accum_out=ss[:, bass.ds(i * 2 + j, 1)]).then_inc(c_sq, 1)

            def store_f(i, j):
                act.wait_ge(c_f, i * 2 + (j + 1))
                act.wait_ge(c_fsaved, i * 32 + 16 * (j + 2))
                act.dma_start(f_rows[bass.ds(i * 2 * P + j * P, P), :], f_buf[:, j % 2, :]).then_inc(c_fsaved, 16)

            def copy_fT(i, j):
                act.wait_ge(c_ftp, i * 2 + (j + 1))
                act.copy(fT[:, 0:4, :], psum[:, 4, :].rearrange("p (a b) -> p a b", a=4)).then_inc(c_fT_act, 1)

            copy_mT(0, 0)
            copy_mT(0, 1)
            square_sum(0, 0)
            store_f(0, 0)
            with act.Fori(0, T // 2 - 1) as i:
                for j in (1, 2):
                    copy_mT(i, j + 1)
                    square_sum(i, j)
                    copy_fT(i, j - 1)
                    store_f(i, j)
            square_sum(T // 2 - 1, 1)
            copy_fT(T // 2 - 1, 0)
            store_f(T // 2 - 1, 1)
            copy_fT(T // 2 - 1, 1)

            act.wait_ge(r_gexp_in, 1)
            act.activation(g_exp[:, :, :], g_exp[:, :, :], ACT.Exp).then_inc(r_gexp, 1)
            act.wait_ge(r_esec_in, 1)
            act.activation(e_sec[:, :], e_gap[:, :], ACT.Exp).then_inc(r_esec, 1)

            def copy_xT(b):
                act.wait_ge(x_tp, b + 1)
                act.copy(xT[:, 0:4, :], psum[:, 4, :].rearrange("p (a b) -> p a b", a=4)).then_inc(xT_act, 1)

            def silu_of(b):
                act.wait_ge(g_ready, b + 1)
                act.activation(silu, psum[:, 0, :], ACT.Silu).then_inc(silu_ready, 1)

            def copy_hT(b):
                act.wait_ge(h_tp, b + 1)
                act.copy(hT, psum[:, 6, :].rearrange("p (a b) -> p a b", a=KE)).then_inc(hT_ready, 1)

            def copy_y(b, first=False):
                act.wait_ge(y_ready, b * 2 + 5)
                if not first:
                    act.wait_ge(y_stored, b * 16)
                act.copy(y_sb[:, 0:BANK], psum[:, 2, :]).then_inc(y_act, 1)

            act.wait_ge(r_idx, 1)
            last_b = act.value_load(last_i[0:1, 0:1], min_val=NE - 1, max_val=NB - 2)
            copy_xT(0)
            silu_of(0)
            copy_xT(1)

            def block_of(b, first=False):
                copy_hT(b)
                silu_of(b + 1)
                copy_xT(b + 2)
                copy_y(b, first)

            block_of(0, first=True)
            with act.Fori(1, last_b) as b:
                block_of(b)
            copy_hT(last_b)
            copy_y(last_b)

        @block.vector
        def _(dve):
            dve.sem_inc(n_aT_dve, 2)
            dve.sem_inc(acc_dve, T // 2)
            for a in (SB, DF, CA):
                dve.sem_inc(a.s["pt_sb1"], 1)
                dve.sem_inc(a.s["z_read"], 2)
            for a in (DF, CA):
                dve.sem_inc(a.s["o_read"], 2)
                dve.sem_inc(a.s["qk_ms_ready"], 2)
            dve.sem_inc(c_mT_dve, 1)
            dve.sem_inc(c_h2, 2)
            dve.sem_inc(c_logits, 1)
            dve.sem_inc(y_dve, 1)
            dve.memset(ones[:, :], 1.0)
            dve.memset(mhalf[:, :], -0.5).then_inc(s_dve_const, 1)

            def low_aT(t):
                high = aT_hi[:, :, t * P:(t + 1) * P]
                dve.wait_ge(n_aT_act, 2 + t + 1)
                dve.tensor_tensor(aT_lo[:, :, t * P:(t + 1) * P],
                                  banks(2 * (t % 2), 2).rearrange("p (a b) -> p a b", a=KD), high.bitcast(F32), ALU.subtract) \
                    .then_inc(n_aT_lo, 1)

            def low_w_in(c, h):
                dve.wait_ge(w_hi, c * 2 + (h + 1))
                dve.tensor_tensor(w_in_lo[h][:, :, :], w_in_ring[:, h, :, :], w_in_hi[h][:, :, :].bitcast(F32),
                                  ALU.subtract).then_inc(w_lo, 1)

            def copy_proj(c, t):
                dve.wait_ge(acc_ready, c * T + (t + 1))
                dve.tensor_copy(proj[:, t, bass.ds(c * BANK, BANK)], psum[:, t, :]).then_inc(acc_dve, 1)

            dve.wait_ge(s_gain, 16)
            for t in range(T):
                dve.wait_ge(n_sq, t + 2)
                dve.tensor_scalar(ms[:, t:t + 1], ss[:, t:t + 1], 1.0 / D, EPS, ALU.mult, ALU.add).then_inc(n_ms, 1)
                dve.wait_ge(n_rstd, t + 1)
                if t >= 2:
                    dve.wait_ge(n_tp, t - 1)
                dve.scalar_tensor_tensor(a_buf[:, t % 2, :], x_all[:, t, :], rstd[:, t:t + 1], attn_gain[:, :],
                                         ALU.mult, ALU.mult).then_inc(n_a, 1)
                if t >= 1:
                    low_aT(t - 1)
            low_aT(T - 1)
            for h in range(2):
                low_w_in(0, h)
            dve.wait_ge(s_const, 16 * 10)
            for n in range(2):
                if n:
                    dve.wait_ge(s_lam_sum, n)
                dve.tensor_tensor_reduce(out=lam_junk[:, :], in0=lam_in[:, 2 * n * HEAD:(2 * n + 1) * HEAD],
                                         in1=lam_in[:, (2 * n + 1) * HEAD:(2 * n + 2) * HEAD], scale=1.0, scalar=0.0,
                                         op0=ALU.mult, op1=ALU.add, accum_out=lam_sum[:, n:n + 1]).then_inc(s_lam_sum, 1)
            dve.wait_ge(s_lam_exp, 1)
            dve.tensor_tensor(neg_lam[:, :], lam_exp[:, 1:2], lam_exp[:, 0:1], ALU.subtract).then_inc(s_lam, 1)
            dve.wait_ge(s_lam, 1)
            dve.tensor_scalar(neg_lam[:, :], neg_lam[:, :], LAM_INIT, None, ALU.subtract).then_inc(s_lam, 1)
            for c in (0, 2):
                dve.tensor_scalar(qk_gain[:, c:c + 1], qk_gain[:, c:c + 1], SCALE, None, ALU.mult).then_inc(s_lam, 1)
            dve.tensor_scalar(subln[:, :], subln[:, :], 1.0 - LAM_INIT, None, ALU.mult).then_inc(s_lam, 1)
            dve.wait_ge(s_lines_out, 32)
            with dve.Fori(0, CH - 1) as c:
                copy_proj(c, 1)
                low_w_in(c + 1, 0)
                for t in range(3, T, 2):
                    copy_proj(c, t)
                low_w_in(c + 1, 1)
            for t in range(1, T, 2):
                copy_proj(CH - 1, t)
            dve.wait_ge(s_lam, 5)

            def low_qk(a, p, q_gain, k_gain):
                for name, bank, gain, high, low_part in (("q", 0, q_gain, qT_hi, qT_lo), ("k", 2, k_gain, kT_hi, kT_lo)):
                    dve.wait_ge(a.s[f"{name}T_ready"], p * 2 + 1)
                    dve.scalar_tensor_tensor(low_part[:, :], banks(bank, 2), gain, high[:, :].bitcast(F32), ALU.mult,
                                             ALU.subtract).then_inc(a.s[f"{name}T_ready"], 1)

            def copy_pt1(a, p, r):
                if len(a.groups(r)) < 2:
                    return
                before, per = a.group_no(1, r)
                w = len(a.groups(r)[1]) * P
                dve.wait_ge(a.s["pt1"], p * per + (before + 1 + per))
                dve.tensor_copy(pt_sb[:, 1, 0:w], psum[:, 5, 0:w]).then_inc(a.s["pt_sb1"], 1)

            def mean_squares(a, p):
                dve.wait_ge(a.s["squared"], p * 2 + 2)
                dve.tensor_reduce(qk_ss[:, :, :].rearrange("p n g -> p (n g)"),
                                  squares.rearrange("p n t (h d) -> p (n t h) d", h=2), AX.X, ALU.add) \
                    .then_inc(a.s["qk_ms_ready"], 1)
                dve.wait_ge(a.s["qk_ms_ready"], p * 2 + 3)
                dve.tensor_scalar(qk_ms[:, :, :], qk_ss[:, :, :], 1.0 / HEAD, EPS, ALU.mult, ALU.add) \
                    .then_inc(a.s["qk_ms_ready"], 1)

            def biased(a, p, u, slot, stat, m, tile):
                t = u // 2
                first, n = a.keys(t)
                w = n * P
                wait_alone(dve, a.s["z_ready"], p * a.units + (u + 1))
                dve.tensor_tensor_reduce(out=work[:, slot, 0:w], in0=banks(2 * (u % 2), 2)[:, 0:w],
                                         in1=tile[:, 0:w][:, ::-1], scale=-1.0, scalar=-LOWEST,
                                         op0=ALU.add, op1=ALU.min, accum_out=low[:, stat, m:m + 1]) \
                    .then_inc(a.s["z_read"], 1)

            def mask_bias(a, p, tiles):
                dve.wait_ge(a.s["bias_landed"], p * 16 * len(tiles) + 16 * len(tiles))
                for tile in tiles:
                    last = dve.memset(tile[0:HEAD, 0:HEAD], MASKED)
                    if a.kind == "ca":
                        last = dve.memset(tile[HEAD:P, CA_W - HEAD:CA_W], MASKED)
                last.then_inc(a.s["bias_ready"], 1)

            def sb_softplus(p, u):
                w, buf = SB.keys(u // 2)[1] * P, u % 2
                dve.wait_ge(SBS["lp_ready"], p * SB.units + (u + 1))
                dve.scalar_tensor_tensor(work[:, 2 + buf, 0:w], banks(2 * buf, 2)[:, 0:w], 0.0, work[:, 2 + buf, 0:w],
                                         ALU.max, ALU.add).then_inc(SBS["sp_ready"], 1)

            def sb_exponent(p, u):
                w, buf = SB.keys(u // 2)[1] * P, u % 2
                dve.wait_ge(SBS["sp_masked"], p * SB.units + (u + 1))
                dve.tensor_tensor_scan(work[:, 4 + buf, 0:w][:, ::-1], ones[:, 0:1].to_broadcast([P, w]),
                                       work[:, 2 + buf, 0:w][:, ::-1], 0.0, ALU.mult, ALU.add).then_inc(SBS["scanned"], 1)
                dve.wait_ge(SBS["scanned"], p * SB.units + (u + 1))
                dve.tensor_tensor(work[:, 4 + buf, 0:w], banks(2 * buf, 2)[:, 0:w], work[:, 4 + buf, 0:w],
                                  ALU.subtract).then_inc(SBS["z_read"], 1)

            def sb_pair(p, after):
                low_qk(SB, p, SCALE, 1.0)
                for s in range(SB.units + 2):
                    if 1 <= s <= SB.units:
                        sb_exponent(p, s - 1)
                    if s >= 2:
                        copy_pt1(SB, p, s - 2)
                    if s < SB.units:
                        sb_softplus(p, s)
                    if s == 8 and after[0] is DF:
                        mean_squares(*after)

            with dve.Fori(0, SB.pairs - 1) as p:
                sb_pair(p, (SB, p + 1))
            sb_pair(SB.pairs - 1, (DF, 0))

            def df_mix(p, t):
                st = t % 4
                dve.wait_ge(DFS["summed"], p * DF.units + (2 * t + 2))
                dve.reciprocal(inv[:, st, :], total[:, st, :]).then_inc(DFS["inverse"], 1)
                dve.wait_ge(DFS["inverse"], p * 2 * T + (2 * t + 1))
                dve.tensor_scalar(mix[:, st:st + 1], inv[:, st, 1:2], total[:, st, 0:1], neg_lam[:, :], ALU.mult,
                                  ALU.mult).then_inc(DFS["inverse"], 1)
                w, buf = (t + 1) * P, 2 * (t % 3)
                dve.wait_ge(DFS["inverse"], p * 2 * T + (2 * t + 2))
                dve.scalar_tensor_tensor(work[:, buf, 0:w], work[:, buf + 1, 0:w], mix[:, st:st + 1], work[:, buf, 0:w],
                                         ALU.mult, ALU.add).then_inc(DFS["p_ready"], 1)

            def df_result(p, t):
                dve.wait_ge(DFS["o_ready"], p * T + (t + 1))
                dve.tensor_scalar(yd[:, t % 2, :], psum[:, 6 + t % 2, 0:P], inv[:, t % 4, 0:1], None, ALU.mult) \
                    .then_inc(DFS["o_read"], 1)
                dve.wait_ge(DFS["o_read"], p * T + (t + 3))
                dve.tensor_tensor_reduce(out=yd_junk[:, :], in0=yd[:, t % 2, :], in1=yd[:, t % 2, :], scale=1.0,
                                         scalar=0.0, op0=ALU.mult, op1=ALU.add,
                                         accum_out=yd_ss[:, t % 2:t % 2 + 1]).then_inc(DFS["yd_ss_ready"], 1)
                dve.wait_ge(DFS["yd_ss_ready"], p * T + (t + 1))
                dve.tensor_scalar(yd_ms[:, t % 2:t % 2 + 1], yd_ss[:, t % 2:t % 2 + 1], 1.0 / P, EPS, ALU.mult,
                                  ALU.add).then_inc(DFS["yd_ms_ready"], 1)

            def df_merge(p, t):
                dve.wait_ge(DFS["yd_rstd_ready"], p * T + (t + 1))
                dve.scalar_tensor_tensor(merged[:, t, cols(DF_O, p)], yd[:, t % 2, :], yd_rstd[:, t % 2:t % 2 + 1],
                                         subln[:, :], ALU.mult, ALU.mult).then_inc(DFS["merged_ready"], 1)

            dve.wait_ge(SBS["o_read"], 2 + SB.pairs * SB.results)
            def df_pair(p, after):
                low_qk(DF, p, qk_gain[:, 0:1], qk_gain[:, 1:2])
                mask_bias(DF, p, [df_bias])
                dve.wait_ge(DFS["bias_ready"], p + 1)
                for s in range(T + 4):
                    if 2 <= s < T + 2:
                        copy_pt1(DF, p, s - 2)
                    if 1 <= s <= T:
                        df_mix(p, s - 1)
                    if s < T:
                        wait_slot(dve, DF, p, s, 3)
                        for m in range(2):
                            biased(DF, p, 2 * s + m, 2 * (s % 3) + m, s % 4, m, df_bias)
                    if s == 3:
                        mean_squares(*after)
                    if s >= 4:
                        df_merge(p, s - 4)
                    if 3 <= s < T + 3:
                        df_result(p, s - 3)

            with dve.Fori(0, DF.pairs - 1) as p:
                df_pair(p, (DF, p + 1))
            df_pair(DF.pairs - 1, (CA, 0))

            dve.wait_ge(DFS["merged_ready"], DF.pairs * DF.results)
            def ca_pair(p, after):
                low_qk(CA, p, qk_gain[:, 2:3], qk_gain[:, 3:4])
                mask_bias(CA, p, ca_bias)
                dve.wait_ge(CAS["bias_ready"], p + 1)
                for s in range(CA.units + 3):
                    if 2 <= s < CA.units + 2:
                        copy_pt1(CA, p, s - 2)
                    if s < CA.units:
                        wait_slot(dve, CA, p, s, 4)
                        biased(CA, p, s, s % 4, s % 4, 0, ca_bias[s % 2])
                    if 1 <= s <= CA.units:
                        dve.wait_ge(CAS["p_ready"], p * CA.units + s)
                        dve.reciprocal(inv[:, (s - 1) % 4, 0:1], total[:, (s - 1) % 4, 0:1]).then_inc(CAS["inverse"], 1)
                    if s == 5 and after:
                        mean_squares(*after)
                    if s >= 3:
                        r = s - 3
                        dve.wait_ge(CAS["o_ready"], p * CA.results + (r + 1))
                        dve.wait_ge(CAS["inverse"], p * CA.results + (r + 1))
                        dve.tensor_scalar(merged[:, r // 2, cols(CA_O + HEAD * (r % 2), p, HEAD)],
                                          psum[:, 6 + r % 2, 0:HEAD], inv[:, r % 4, 0:1], None, ALU.mult) \
                            .then_inc(CAS["o_read"], 1)

            with dve.Fori(0, CA.pairs - 1) as p:
                ca_pair(p, (CA, p + 1))
            ca_pair(CA.pairs - 1, None)

            def row(tensor, i, j):
                return tensor[:, bass.ds(i * 2 + j, 1), :].rearrange("p a b -> p (a b)")

            dve.wait_ge(CAS["o_read"], 2 + CA.pairs * CA.results)
            dve.wait_ge(s_pool_const, 1)
            dve.wait_ge(s_gain, 32)
            dve.wait_ge(s_x_again, 32)
            def copy_mT(i, j):
                dve.wait_ge(c_tp, i * 2 + (j + 1))
                dve.wait_ge(c_acc, i * 4 + (2 * j + 2))
                dve.tensor_copy(mT[:, j % 2, 4:8, :], psum[:, 1, :].rearrange("p (a b) -> p a b", a=4)) \
                    .then_inc(c_mT_dve, 1)

            def residual(i, j):
                for n in range(2):
                    half = h2[:, bass.ds(i * 2 + j, 1), n * BANK:(n + 1) * BANK].rearrange("p a b -> p (a b)")
                    dve.wait_ge(c_acc, i * 4 + (2 * j + n + 5))
                    dve.tensor_tensor(half, psum[:, 2 + n, :], half, ALU.add).then_inc(c_h2, 1)

            def copy_fT(i, j):
                dve.wait_ge(c_ftp, i * 2 + (j + 1))
                dve.tensor_copy(fT[:, 4:8, :], psum[:, 5, :].rearrange("p (a b) -> p a b", a=4)).then_inc(c_fT_dve, 1)

            def second_norm(i, j):
                dve.wait_ge(c_sq, i * 2 + (j + 2))
                dve.tensor_scalar(ms[:, bass.ds(i * 2 + j, 1)], ss[:, bass.ds(i * 2 + j, 1)], 1.0 / D, EPS, ALU.mult,
                                  ALU.add).then_inc(c_ms, 1)
                dve.wait_ge(c_rstd, i * 2 + (j + 1))
                dve.wait_ge(c_fsaved, i * 32 + 16 * (j + 1))
                dve.scalar_tensor_tensor(f_buf[:, j % 2, :], row(h2, i, j), rstd[:, bass.ds(i * 2 + j, 1)],
                                         attn_gain[:, :], ALU.mult, ALU.mult).then_inc(c_f, 1)

            def router_logits(i, j):
                dve.wait_ge(c_lg, i * 2 + (j + 1))
                dve.tensor_tensor(row(logits, i, j), psum[:, 6, 0:NR], b_r[:, :], ALU.add).then_inc(c_logits, 1)

            copy_mT(0, 0)
            copy_mT(0, 1)
            residual(0, 0)
            second_norm(0, 0)
            with dve.Fori(0, T // 2 - 1) as i:
                for j in (1, 2):
                    copy_mT(i, j + 1)
                    residual(i, j)
                    copy_fT(i, j - 1)
                    second_norm(i, j)
                    router_logits(i, j - 1)
            residual(T // 2 - 1, 1)
            copy_fT(T // 2 - 1, 0)
            second_norm(T // 2 - 1, 1)
            router_logits(T // 2 - 1, 0)
            copy_fT(T // 2 - 1, 1)
            router_logits(T // 2 - 1, 1)

            steps = [0]

            def step(ins, told=None):
                if told is not None:
                    ins.then_inc(told, 1)
                    dve.wait_ge(told, 1)
                else:
                    steps[0] += 1
                    ins.then_inc(r_dve, 1)
                    dve.wait_ge(r_dve, steps[0])

            def over(ap, axis, n):
                dims = [list(d) for d in ap.ap]
                return bass.AP(ap.tensor, ap.offset, dims[:1 + axis] + [[0, n]] + dims[1 + axis:])

            dve.wait_ge(c_logits, T + 1)
            step(dve.memset(g8[:, :, :], LOWEST))
            step(dve.tensor_copy(g8[:, :, 0:NG], logits[:, :, 0:NG]))
            for t in range(T):
                last = dve.max(g_top[:, t, :], g8[:, t, :])
            step(last)
            for t in range(T):
                last = dve.max_index(g_idx[:, t, :], g_top[:, t, :], g8[:, t, :])
            step(last)
            step(dve.tensor_tensor(g_exp[:, :, :], logits[:, :, 0:NG], over(g_top[:, :, 0], 1, NG), ALU.subtract), r_gexp_in)
            step(dve.tensor_copy(g_sel[:, :], g_idx[:, :, 0]))
            step(dve.tensor_tensor(g_hot[:, :, :], over(iota_f[:, 0:NG], 0, T), over(g_sel[:, :], 1, NG), ALU.is_equal))
            step(dve.tensor_tensor(e_all[:, :, :, :], logits[:, :, NG:NR].rearrange("p t (g e) -> p t g e", g=NG),
                                   over(g_hot[:, :, :], 2, EG), ALU.mult))
            step(dve.tensor_reduce(e8[:, :, :], e_all[:, :, :, :].rearrange("p t g e -> p t e g"), AX.X, ALU.add))
            for t in range(T):
                last = dve.max(e_top[:, t, :], e8[:, t, :])
            step(last)
            for t in range(T):
                last = dve.max_index(e_idx[:, t, :], e_top[:, t, :], e8[:, t, :])
            step(last)
            step(dve.tensor_tensor(e_gap[:, :], e_top[:, :, 1], e_top[:, :, 0], ALU.subtract), r_esec_in)
            step(dve.tensor_copy(e_idf[:, :, :], e_idx[:, :, 0:TOP]))
            step(dve.scalar_tensor_tensor(eid[:, :, :], over(g_sel[:, :], 1, TOP), float(EG), e_idf[:, :, :], ALU.mult,
                                          ALU.add))
            for c in range(TOP):
                step(dve.tensor_tensor(hot[:, c, :, :], over(iota_f[:, 0:NE], 0, T), over(eid[:, :, c], 1, NE),
                                       ALU.is_equal))
            step(dve.tensor_tensor(hot_sum[:, :, :], hot[:, 0, :, :], hot[:, 1, :, :], ALU.add), r_hot)
            dve.wait_ge(r_gexp, 1)
            step(dve.tensor_reduce(g_sum[:, :], g_exp[:, :, :], AX.X, ALU.add))
            step(dve.reciprocal(g_w[:, :], g_sum[:, :]))
            dve.wait_ge(r_esec, 1)
            step(dve.tensor_scalar(e_den[:, :], e_sec[:, :], 1.0, None, ALU.add))
            step(dve.reciprocal(e_inv[:, :], e_den[:, :]))
            step(dve.tensor_tensor(gates[:, :, 0], g_w[:, :], e_inv[:, :], ALU.mult))
            step(dve.tensor_tensor(gates[:, :, 1], gates[:, :, 0], e_sec[:, :], ALU.mult))
            dve.wait_ge(r_counted, 1)
            step(dve.tensor_scalar(cnt_i[:, :], psum[:, 1, 0:NE], float(P - 1), None, ALU.add))
            step(dve.tensor_scalar(cnt_i[:, :], cnt_i[:, :], 7, None, ALU.arith_shift_right))
            step(dve.tensor_scalar(nblk[:, :], cnt_i[:, :], 1.0, None, ALU.max))
            step(dve.tensor_tensor_scan(blk_end[:, :], ones[:, 0:1].to_broadcast([P, NE]), nblk[:, :], 0.0, ALU.mult,
                                        ALU.add))
            step(dve.tensor_tensor(blk_start[:, :], blk_end[:, :], nblk[:, :], ALU.subtract))
            ranks = psum[:, 0, 0:T * NE].rearrange("p (t e) -> p t e", t=T)
            for c in range(TOP):
                step(dve.tensor_tensor(picked[:, c, :, :], ranks, hot[:, c, :, :], ALU.mult))
            step(dve.tensor_reduce(rank[:, :, :], picked[:, :, :, :], AX.X, ALU.add))
            for c in range(TOP):
                step(dve.tensor_tensor(picked[:, c, :, :], over(blk_start[:, :], 0, T), hot[:, c, :, :], ALU.mult))
            step(dve.tensor_reduce(first_blk[:, :, :], picked[:, :, :, :], AX.X, ALU.add))
            step(dve.tensor_copy(rank_i[:, :, :], rank[:, :, :]))
            step(dve.tensor_scalar(hi_i[:, :, :], rank_i[:, :, :], 7, None, ALU.arith_shift_right))
            step(dve.tensor_scalar(lo_i[:, :, :], rank_i[:, :, :], P - 1, None, ALU.bitwise_and))
            step(dve.tensor_copy(hi_f[:, :, :], hi_i[:, :, :]))
            step(dve.tensor_copy(lo_f[:, :, :], lo_i[:, :, :]))
            step(dve.tensor_tensor(blk[:, :, :], first_blk[:, :, :], hi_f[:, :, :], ALU.add))
            for c in range(TOP):
                step(dve.tensor_tensor(pos_hot[:, c, :, :], over(iota_f[:, :], 0, T), over(lo_f[:, c, :], 1, P),
                                       ALU.is_equal))
                step(dve.tensor_tensor(blk_hot[:, c, :, :], over(iota_f[:, 0:NB], 0, T), over(blk[:, c, :], 1, NB),
                                       ALU.is_equal))
                step(dve.tensor_scalar(blk_vals[:, c, :, 0, :], blk_hot[:, c, :, :], part_id[:, 0:1], None, ALU.mult))
                step(dve.tensor_tensor(blk_vals[:, c, :, 1, :], blk_hot[:, c, :, :], over(tile_id[:, :], 1, NB), ALU.mult))
                step(dve.tensor_scalar(blk_vals[:, c, :, 2, :], blk_hot[:, c, :, :], float(c), None, ALU.mult))
            step(dve.tensor_scalar(last_i[0:1, 0:1], blk_end[0:1, NE - 1:NE], 1.0, None, ALU.subtract), r_vals)
            step(dve.tensor_tensor(be_cmp[:, :, :], over(blk_end[0:1, :], 0, NB), over(iota_f[0:1, 0:NB], 1, NE), ALU.is_le))
            step(dve.tensor_reduce(be_f[:, :], be_cmp[:, :, :], AX.X, ALU.add))
            step(dve.tensor_scalar(be_i[:, :], be_f[:, :], float(NE - 1), None, ALU.min), r_idx)
            dve.wait_ge(r_rows, 1)
            told = psum[:, 2, 0:3 * NB].rearrange("p (a b) -> p a b", a=3)
            step(dve.tensor_scalar(empty[:, :], told[:, 0, :], 0.0, 65536.0, ALU.is_equal, ALU.mult))
            step(dve.scalar_tensor_tensor(empty[:, :], told[:, 0, :], 1.0, empty[:, :], ALU.subtract, ALU.add))
            step(dve.scalar_tensor_tensor(row_f[:, 0, :], told[:, 1, :], float(P), empty[:, :], ALU.mult, ALU.add))
            step(dve.scalar_tensor_tensor(row_f[:, 1, :], told[:, 1, :], float(P), row_f[:, 0, :], ALU.mult, ALU.add))
            step(dve.scalar_tensor_tensor(row_f[:, 1, :], told[:, 2, :], float(P), row_f[:, 1, :], ALU.mult, ALU.add))
            step(dve.tensor_copy(row_i[:, :, :], row_f[:, :, :]), r_table)

            def copy_xT(b):
                dve.wait_ge(x_tp, b + 1)
                dve.tensor_copy(xT[:, 4:8, :], psum[:, 5, :].rearrange("p (a b) -> p a b", a=4)).then_inc(xT_dve, 1)

            def hidden(b):
                dve.wait_ge(u_ready, b + 2)
                dve.wait_ge(silu_ready, b + 1)
                dve.tensor_tensor(hid, silu, psum[:, 1, :], ALU.mult).then_inc(h_ready, 1)

            def copy_y(b, first=False):
                dve.wait_ge(y_ready, b * 2 + 6)
                if not first:
                    dve.wait_ge(y_stored, b * 16)
                dve.tensor_copy(y_sb[:, BANK:2 * BANK], psum[:, 3, :]).then_inc(y_dve, 1)

            dve.wait_ge(r_idx, 1)
            last_b = dve.value_load(last_i[0:1, 0:1], min_val=NE - 1, max_val=NB - 2)
            copy_xT(0)
            hidden(0)
            copy_xT(1)

            def block_of(b, first=False):
                hidden(b + 1)
                copy_xT(b + 2)
                copy_y(b, first)

            block_of(0, first=True)
            with dve.Fori(1, last_b) as b:
                block_of(b)
            copy_y(last_b)

            for t in range(T):
                dve.wait_ge(s_y[t % 4], 16 * (t // 4 + 3))
                dve.scalar_tensor_tensor(h2[:, t, :], y_tiles[:, t, 0, :], gates[:, t, 0:1], h2[:, t, :], ALU.mult,
                                         ALU.add).then_inc(f_part, 1)
                dve.wait_ge(f_part, t + 1)
                dve.scalar_tensor_tensor(h2[:, t, :], y_tiles[:, t, 1, :], gates[:, t, 1:2], h2[:, t, :], ALU.mult,
                                         ALU.add).then_inc(f_out, 1)

        @block.gpsimd
        def _(pool):
            pool.sem_inc(c_fsaved, 32)
            pool.memset(ident[:, :], 0.0).then_inc(s_ident, 1)
            pool.wait_ge(s_ident, 1)
            pool.affine_select(out=ident[:, :], in_=ident[:, :], compare_op=ALU.not_equal, fill=1.0, base=0,
                               pattern=[[-1, P]], channel_multiplier=1).then_inc(s_ident, 1)
            pool.wait_ge(s_dve_const, 1)
            for t in range(T):
                pool.wait_ge(n_ms, t + 1)
                pool.tensor_tensor(rstd[:, t:t + 1], ms[:, t:t + 1], mhalf[:, 0:1], ALU.pow).then_inc(n_rstd, 1)
            pool.wait_ge(s_lines_in, 32)
            pool.memset(t5_sb[:, :], 0.0)
            pool.memset(ca_sb[:, :], 0.0).then_inc(s_ident, 1)
            pool.wait_ge(s_ident, 3)
            for lo, hi, bucket in t5_runs(-(S - 1), P):
                run = t5_sb[:, P - hi:P - lo]
                last = pool.tensor_scalar(run, run, lines_in[:, bucket:bucket + 1], None, ALU.add)
            last.then_inc(s_lines, 1)
            near = P + CLIP
            pool.tensor_scalar(ca_sb[:, near:CA_LINE], ca_sb[:, near:CA_LINE], lines_in[:, T5_BUCKETS:T5_BUCKETS + 1],
                               None, ALU.add)
            pool.tensor_copy(ca_sb[:, 0:near], lines_in[:, T5_BUCKETS:T5_BUCKETS + near][:, ::-1]) \
                .then_inc(s_lines, 1)
            pool.iota(iota_f[:, :], [[1, P]], base=0, channel_multiplier=0, allow_small_or_imprecise_dtypes=True)
            pool.iota(part_id[:, :], [[1, 1]], base=1, channel_multiplier=1, allow_small_or_imprecise_dtypes=True)
            pool.iota(tile_id[:, :], [[1, T]], base=0, channel_multiplier=0, allow_small_or_imprecise_dtypes=True)
            pool.memset(ones_b[:, :], 1.0).then_inc(s_ident, 1)
            pool.wait_ge(s_ident, 4)
            pool.affine_select(out=tri[:, :], in_=ones_b[:, :], compare_op=ALU.is_gt, fill=0.0, base=0,
                               pattern=[[1, P]], channel_multiplier=-1).then_inc(s_pool_const, 1)

            def stage_plain(a, p, n):
                first, stage = ((a.q, q_stage), (a.k, k_stage))[n]
                pool.tensor_copy(stage, proj[:, :, cols(first, p)]).then_inc(a.s["staged"], 1)

            def root_mean_squares(a, p):
                pool.wait_ge(a.s["qk_ms_ready"], p * 2 + 4)
                pool.tensor_tensor(qk_rstd[:, :, :], qk_ms[:, :, :], mhalf[:, :].rearrange("p (a b) -> p a b", a=2),
                                   ALU.pow).then_inc(a.s["qk_rstd_ready"], 1)

            def stage_normed(a, p, part_no):
                n, h = part_no // 2, part_no % 2
                first, stage = ((a.q, q_stage), (a.k, k_stage))[n]
                if part_no == 0:
                    pool.wait_ge(a.s["qk_rstd_ready"], p + 1)
                r = qk_rstd[:, n, h:2 * T:2]
                last = pool.tensor_tensor(stage[:, :, h * HEAD:(h + 1) * HEAD], proj[:, :, cols(first + h * HEAD, p, HEAD)],
                                          bass.AP(r.tensor, r.offset, [*[list(d) for d in r.ap], [0, HEAD]]), ALU.mult)
                if h == 1:
                    last.then_inc(a.s["staged"], 1)

            def keep_earlier(buf, t, wait, done, value):
                diag = work[:, buf, t * P:(t + 1) * P]
                wait_alone(pool, wait, value)
                pool.affine_select(out=diag, in_=diag, compare_op=ALU.is_gt, fill=0.0, base=0, pattern=[[-1, P]],
                                   channel_multiplier=1).then_inc(done, 1)

            pool.wait_ge(acc_act, (CH + 1) * T // 2)
            pool.wait_ge(acc_dve, (CH + 1) * T // 2)
            for n in range(2):
                stage_plain(SB, 0, n)

            def sb_pair(p, after):
                for s in range(SB.units + 1):
                    if s < SB.units:
                        keep_earlier(2 + s % 2, s // 2, SBS["sp_ready"], SBS["sp_masked"], p * SB.units + (s + 1))
                    if s >= 1:
                        keep_earlier((s - 1) % 2, (s - 1) // 2, SBS["w_exp"], SBS["p_ready"], p * SB.units + s)
                    if s == 4:
                        pool.wait_ge(SBS["k_tp"], p + 1)
                    if after[0] is SB and s in (4, 6):
                        stage_plain(*after, s // 2 - 2)
                    if after[0] is DF and s == 9:
                        root_mean_squares(*after)
                    if after[0] is DF and 10 <= s < 14:
                        stage_normed(*after, s - 10)

            with pool.Fori(0, SB.pairs - 1) as p:
                sb_pair(p, (SB, p + 1))
            sb_pair(SB.pairs - 1, (DF, 0))

            pool.wait_ge(SBS["o_read"], 2 + SB.pairs * SB.results)
            def df_pair(p, after):
                for s in range(T + 4):
                    if 3 <= s < T + 3:
                        t = s - 3
                        pool.wait_ge(DFS["yd_ms_ready"], p * T + (t + 1))
                        pool.tensor_tensor(yd_rstd[:, t % 2:t % 2 + 1], yd_ms[:, t % 2:t % 2 + 1], mhalf[:, 0:1],
                                           ALU.pow).then_inc(DFS["yd_rstd_ready"], 1)
                    if s == 3:
                        pool.wait_ge(DFS["k_tp"], p + 1)
                        root_mean_squares(*after)
                    if 4 <= s < 8:
                        stage_normed(*after, s - 4)

            with pool.Fori(0, DF.pairs - 1) as p:
                df_pair(p, (DF, p + 1))
            df_pair(DF.pairs - 1, (CA, 0))
            pool.wait_ge(DFS["merged_ready"], DF.pairs * DF.results)
            with pool.Fori(0, CA.pairs - 1) as p:
                pool.wait_ge(CAS["k_tp"], p + 1)
                root_mean_squares(CA, p + 1)
                for n in range(4):
                    stage_normed(CA, p + 1, n)

            pool.wait_ge(CAS["o_read"], 2 + CA.pairs * CA.results)

            def stage_merged(i, j):
                pool.wait_ge(c_tp, i * 2 + (j - 1))
                pool.tensor_copy(m_stage[:, j % 2, :], merged[:, bass.ds(i * 2 + j, 1), :].rearrange("p a b -> p (a b)")) \
                    .then_inc(c_stage, 1)

            def inverse_root(i, j):
                pool.wait_ge(c_ms, i * 2 + (j + 1))
                pool.tensor_tensor(rstd[:, bass.ds(i * 2 + j, 1)], ms[:, bass.ds(i * 2 + j, 1)], mhalf[:, 0:1],
                                   ALU.pow).then_inc(c_rstd, 1)

            for j in range(2):
                pool.tensor_copy(m_stage[:, j, :], merged[:, j, :]).then_inc(c_stage, 1)
            with pool.Fori(0, T // 2 - 1) as i:
                for j in range(2):
                    stage_merged(i, j + 2)
                    inverse_root(i, j)
            for j in range(2):
                inverse_root(T // 2 - 1, j)

            pool.wait_ge(c_h2, 2 * T + 2)
            pool.memset(xg, 0.0).then_inc(xg_zero, 1)
            pool.wait_ge(r_table, 1)
            pool.wait_ge(xg_zero, 1)
            pool.wait_ge(c_fsaved, 16 * T + 32)

            def gather(b):
                pool.tensor_copy(tok_col[:, :], row_i[:, 0, bass.ds(b, 1)]).then_inc(tok_ready, 1)
                wait_alone(pool, tok_ready, b + 1)
                pool.indirect_dma_start(out=xg, out_offset=None, in_=f_rows,
                                        in_offset=bass.IndirectOffsetOnAxis(ap=tok_col[:, 0:1], axis=0),
                                        bounds_check=S - 1, oob_is_err=False).then_inc(xg_landed, 16)

            def scatter(b):
                pool.wait_ge(y_act, b + 2)
                pool.wait_ge(y_dve, b + 2)
                pool.tensor_copy(row_col[:, :], row_i[:, 1, bass.ds(b, 1)]).then_inc(row_ready, 1)
                wait_alone(pool, row_ready, b + 1)
                pool.indirect_dma_start(out=y_rows, out_offset=bass.IndirectOffsetOnAxis(ap=row_col[:, 0:1], axis=0),
                                        in_=y_sb, in_offset=None, bounds_check=TOP * S - 1,
                                        oob_is_err=False).then_inc(y_stored, 16)

            last_b = pool.value_load(last_i[0:1, 0:1], min_val=NE - 1, max_val=NB - 2)
            gather(0)
            pool.wait_ge(x_tp, 1)
            gather(1)
            with pool.Fori(1, last_b + 1) as b:
                pool.wait_ge(x_tp, b + 1)
                gather(b + 1)
                scatter(b - 1)
            scatter(last_b)


_INS = ['x', 't5_bias', 'attn_norm', 'w_in', 'diff_qk_norm', 'diff_lambda', 'diff_subln', 'ca_qk_norm',
        'ca_rel_bias', 'w_out', 'ffn_norm', 'router_group_w', 'router_group_b', 'router_expert_w',
        'router_expert_b', 'expert_w_gate', 'expert_w_up', 'expert_w_down']
_OUTS = [((1, 1024, 1024), 'float32')]


def kernel(**inputs):
    import numpy as _np
    import concourse.bacc as _bacc
    from concourse import mybir as _mybir
    from concourse.bass_utils import run_bass_kernel_spmd as _run

    nc = _bacc.Bacc("TRN2", target_bir_lowering=False, num_devices=1)
    arrays, args = {}, []
    for name in _INS:
        a = _np.ascontiguousarray(inputs[name])
        arrays[f"in_{name}_dram"] = a
        args.append(nc.dram_tensor(f"in_{name}_dram", a.shape, _mybir.dt.from_np(a.dtype), kind="ExternalInput").ap())
    for i, (shape, dtype) in enumerate(_OUTS):
        dt = _mybir.dt.from_np(_np.dtype(dtype))
        args.append(nc.dram_tensor(f"out_{i}_dram", shape, dt, kind="ExternalOutput").ap())
    hybrid_block(nc, *args)
    r = _run(nc, [arrays], core_ids=[0])
    got = tuple(r.results[0][f"out_{i}_dram"] for i in range(len(_OUTS)))
    return got[0]
```

```python
import math
from contextlib import ExitStack

import numpy as np

import concourse.bass as bass
from concourse import mybir

ALU = mybir.AluOpType
ACT = mybir.ActivationFunctionType
AX = mybir.AxisListType
F32 = mybir.dt.float32
F32R = mybir.dt.float32r
BF16 = mybir.dt.bfloat16
I32 = mybir.dt.int32
U32 = mybir.dt.uint32

P = 128
BANK = 512
EPS = 1e-6
MASKED = -1e30
LOWEST = -3e38
LAM_INIT = 0.8 - 0.6 * math.exp(-0.3 * 0)
HEAD = 64
SCALE = HEAD ** -0.5
T5_BUCKETS, T5_MAX_DIST = 32, 256
CLIP = 128
BAND = 4
TOP = 2


def t5_runs(lo, hi):
    half = T5_BUCKETS // 2
    exact = half // 2
    runs = []
    for rel in range(lo, hi):
        n = abs(rel)
        if n < exact:
            b = n
        else:
            b = exact + int(np.float32(np.log(np.float32(n / exact))) / np.float32(math.log(T5_MAX_DIST / exact))
                            * np.float32(half - exact))
            b = min(b, half - 1)
        b += half if rel > 0 else 0
        if runs and runs[-1][2] == b:
            runs[-1][1] = rel + 1
        else:
            runs.append([rel, rel + 1, b])
    return runs


def hybrid_block(nc, x, t5_bias, attn_norm, w_in, diff_qk_norm, diff_lambda, diff_subln, ca_qk_norm,
                 ca_rel_bias, w_out, ffn_norm, group_w, group_b, expert_w, expert_b, w_gate, w_up, w_down, out):
    _, S, D = x.shape
    QKV = w_in.shape[2]
    NE, _, DE = w_gate.shape[1:]
    NG = group_w.shape[2]
    EG = NE // NG
    T = S // P
    KD = D // P
    KE = DE // P
    CH = QKV // BANK
    NR = NG + NE
    NB = NE + TOP * S // P
    SBW = D // 4
    SB_Q, SB_K, SB_V = 0, SBW, 2 * SBW
    DF_Q, DF_K, DF_V = 3 * SBW, 5 * SBW, 7 * SBW
    CA_Q, CA_K, CA_V = 9 * SBW, 10 * SBW, 11 * SBW
    SB_O, DF_O, CA_O = 0, SBW, 3 * SBW
    SB_PAIRS, DF_PAIRS, CA_PAIRS = SBW // P, 2 * SBW // P, SBW // P
    NH = ca_rel_bias.shape[2]

    T5_LINE = S + P - 1
    CA_W = (BAND + 1) * P
    CA_LINE = CA_W + P - 1

    x_rows = x[0]
    t5_line = nc.dram_tensor("t5_line", [NH, T5_LINE + 1], F32).ap()
    ca_line = nc.dram_tensor("ca_line", [NH, CA_LINE + 1], F32).ap()
    f_rows = nc.dram_tensor("f_rows", [S, D], F32).ap()
    y_rows = nc.dram_tensor("y_rows", [TOP * S, D], F32).ap()

    with ExitStack() as ctx:
        def sb(name, shape, dt=F32):
            return ctx.enter_context(nc.sbuf_tensor(name, shape, dt))

        def sem(name):
            return ctx.enter_context(nc.semaphore(name))

        ARENA = 49152
        arena = sb("arena", [P, ARENA])
        arena_at = nc.sbuf_base - 4 * ARENA

        def rounded(name, first, *dims):
            return nc.alloc_sbuf_tensor_at(name, [P, *dims], F32R, offset=arena_at + 4 * first)

        def whole(name, first, *dims):
            return nc.alloc_sbuf_tensor_at(name, [P, *dims], F32, offset=arena_at + 4 * first)

        def part(first, *dims, dt=F32):
            n = int(np.prod(dims)) * (2 if dt == BF16 else 4) // 4
            v = arena[:, first:first + n]
            if dt != F32:
                v = v.bitcast(dt)
            if len(dims) == 1:
                return v
            names = "abcd"[:len(dims)]
            sizes = {c: d for c, d in zip(names[1:], dims[1:])}
            return v.rearrange(f"p ({' '.join(names)}) -> p {' '.join(names)}", **sizes)

        proj = part(0, T, QKV)
        x_all = part(16384, T, D)
        aT_hi = rounded("aT_hi", 24576, KD, S)
        merged = part(24576, T, D)
        aT_lo = rounded("aT_lo", 32768, KD, S)
        w_in_ring = part(40960, 2, KD // 2, BANK)
        w_in_lo = [rounded(f"w_in_lo{h}", 40960 + h * 2048, KD // 2, BANK) for h in range(2)]
        w_in_hi = [rounded(f"w_in_hi{h}", 45056 + h * 2048, KD // 2, BANK) for h in range(2)]
        a_buf = part(0, 2, D)
        norm_junk = part(2 * D, D)
        t5_sb = part(3 * QKV + 3 * BANK, T5_LINE + 1)[0:NH]
        ca_sb = part(4 * QKV + 3 * BANK, CA_LINE + 1)[0:NH]
        lam_in = part(4 * QKV + 3 * BANK + CA_LINE + 1, 4 * HEAD)
        lam_junk = part(4 * QKV + 3 * BANK + CA_LINE + 1 + 4 * HEAD, HEAD)
        lines_in = part(5 * QKV - 304, T5_BUCKETS + 2 * CLIP + 1)[0:NH]
        q_stage, k_stage = part(32768, T, P), part(33792, T, P)
        squares = part(32768, 2, T, P)
        qT_hi, qT_lo = rounded("qT_hi", 34816, S), rounded("qT_lo", 35840, S)
        kT_hi, kT_lo = rounded("kT_hi", 36864, S), rounded("kT_lo", 37888, S)
        df_bias = part(38912, S)
        ca_bias = [part(39936, CA_W), part(48128, CA_W)]
        work = part(40960, 6, S)
        pt_sb = part(47104, 2, BANK)
        w_out_in = whole("w_out_in", 0, T, QKV)[:, :, 0:D]
        w_out_r = rounded("w_out_r", 0, T, QKV)
        w_out_lo, w_out_hi = w_out_r[:, :, 0:D], w_out_r[:, :, D:2 * D]
        m_stage = [part((6 + i) * QKV + 2 * D, D) for i in range(2)]
        out_junk = part(5 * QKV + 2 * D, D)
        h2 = part(32768, T, D)
        mT_hi = [rounded(f"mT_hi{i}", 40960 + i * D, KD, P) for i in range(2)]
        mT_lo = [rounded(f"mT_lo{i}", 43008 + i * D, KD, P) for i in range(2)]
        f_buf = part(45056, 2, D)
        fT = part(47104, KD, P)
        UNITS = 6
        unit_in = [part(u * 4096, KE, BANK) for u in range(UNITS)]
        unit_lo_w = [rounded(f"unit_lo_w{u}", u * 4096, KE, BANK) for u in range(UNITS)]
        unit_hi_w = [rounded(f"unit_hi_w{u}", u * 4096 + 2048, KE, BANK) for u in range(UNITS)]
        xg = part(40960, D)
        xT_hi, xT_lo = rounded("xT_hi", 41984, KD, P), rounded("xT_lo", 43008, KD, P)
        hT_hi, hT_lo = rounded("hT_hi", 44032, KE, P), rounded("hT_lo", 44544, KE, P)
        y_sb = part(45056, D)
        silu = part(46080, DE)
        hid = part(46592, DE)
        pos_hot = part(28672, TOP, T, P, dt=BF16)
        blk_hot = part(29696, TOP, T, NB)
        blk_vals = part(30464, TOP, T, 3 * NB, dt=BF16).rearrange("p c t (a b) -> p c t a b", a=3)
        hot = part(31616, TOP, T, NE)
        picked = part(32128, TOP, T, NE)
        be_cmp = part(24576, NB, NE)[0:1]
        e_all = part(48128, T, NG, EG)
        row_f = part(48384, 2, NB)
        logits = part(48480, T, NR)
        y_tiles = part(0, T, TOP, D)

        ident = sb("ident", [P, P])
        attn_gain = sb("attn_gain", [P, D])
        subln = sb("subln", [P, 2 * HEAD])
        qk_gain = sb("qk_gain", [P, 4])
        lam_sum = sb("lam_sum", [P, 2])
        lam_exp = sb("lam_exp", [P, 2])
        neg_lam = sb("neg_lam", [P, 1])
        ones = sb("ones", [P, 1])
        mhalf = sb("mhalf", [P, 2 * T * 2])
        ss = sb("ss", [P, T])
        ms = sb("ms", [P, T])
        rstd = sb("rstd", [P, T])
        qk_ss = sb("qk_ss", [P, 2, 2 * T])
        qk_ms = sb("qk_ms", [P, 2, 2 * T])
        qk_rstd = sb("qk_rstd", [P, 2, 2 * T])
        low = sb("low", [P, 4, 2])
        total = sb("total", [P, 4, 2])
        inv = sb("inv", [P, 4, 2])
        mix = sb("mix", [P, 4])
        yd = sb("yd", [P, 2, 2 * HEAD])
        yd_junk = sb("yd_junk", [P, 2 * HEAD])
        yd_ss = sb("yd_ss", [P, 2])
        yd_ms = sb("yd_ms", [P, 2])
        yd_rstd = sb("yd_rstd", [P, 2])
        w_r = sb("w_r", [P, KD, NR])
        b_r = sb("b_r", [P, NR])
        g8 = sb("g8", [P, T, 8])
        g_top = sb("g_top", [P, T, 8])
        g_idx = sb("g_idx", [P, T, 8], U32)
        e_top = sb("e_top", [P, T, 8])
        e_idx = sb("e_idx", [P, T, 8], U32)
        g_sel = sb("g_sel", [P, T])
        g_exp = sb("g_exp", [P, T, NG])
        g_sum = sb("g_sum", [P, T])
        g_w = sb("g_w", [P, T])
        g_hot = sb("g_hot", [P, T, NG])
        e8 = sb("e8", [P, T, EG])
        e_gap = sb("e_gap", [P, T])
        e_sec = sb("e_sec", [P, T])
        e_den = sb("e_den", [P, T])
        e_inv = sb("e_inv", [P, T])
        gates = sb("gates", [P, T, TOP])
        e_idf = sb("e_idf", [P, T, TOP])
        eid = sb("eid", [P, T, TOP])
        hot_sum = sb("hot_sum", [P, T, NE], BF16)
        iota_f = sb("iota_f", [P, P])
        part_id = sb("part_id", [P, 1])
        tri = sb("tri", [P, P], BF16)
        ones_b = sb("ones_b", [P, P], BF16)
        tile_id = sb("tile_id", [P, T])
        cnt_i = sb("cnt_i", [P, NE], I32)
        nblk = sb("nblk", [P, NE])
        blk_end = sb("blk_end", [P, NE])
        blk_start = sb("blk_start", [P, NE])
        rank = sb("rank", [P, TOP, T])
        rank_i = sb("rank_i", [P, TOP, T], I32)
        hi_i = sb("hi_i", [P, TOP, T], I32)
        lo_i = sb("lo_i", [P, TOP, T], I32)
        hi_f = sb("hi_f", [P, TOP, T])
        lo_f = sb("lo_f", [P, TOP, T])
        first_blk = sb("first_blk", [P, TOP, T])
        blk = sb("blk", [P, TOP, T])
        empty = sb("empty", [P, NB])
        row_i = sb("row_i", [P, 2, NB], I32)
        be_f = sb("be_f", [1, NB])
        be_i = sb("be_i", [1, NB], I32)
        last_i = sb("last_i", [1, 2], I32)
        tok_col = sb("tok_col", [P, 1], I32)
        row_col = sb("row_col", [P, 1], I32)

        psum = ctx.enter_context(nc.psum_tensor("psum", [P, 8, BANK], F32))

        def banks(first, n):
            return psum[:, first:first + n, :].rearrange("p a b -> p (a b)")

        s_const = sem("s_const")
        s_ident = sem("s_ident")
        s_waits_met = sem("s_waits_met")
        s_pool_const = sem("s_pool_const")
        s_lines_in = sem("s_lines_in")
        s_lines = sem("s_lines")
        s_lines_out = sem("s_lines_out")
        s_dve_const = sem("s_dve_const")
        s_lam_sum = sem("s_lam_sum")
        s_lam_exp = sem("s_lam_exp")
        s_lam = sem("s_lam")
        s_x = [sem(f"s_x{i}") for i in range(4)]
        n_sq = sem("n_sq"); n_ms = sem("n_ms"); n_rstd = sem("n_rstd"); n_a = sem("n_a")
        n_tp = sem("n_tp"); n_aT_hi = sem("n_aT_hi"); n_aT_lo = sem("n_aT_lo")
        w_landed = [sem(f"w_landed{i}") for i in range(2)]
        w_hi = sem("w_hi"); w_lo = sem("w_lo"); w_half_used = sem("w_half_used")
        acc_ready = sem("acc_ready"); acc_act = sem("acc_act"); acc_dve = sem("acc_dve")

        def attention_sems(kind):
            names = ["squared", "qk_ms_ready", "qk_rstd_ready", "staged", "q_tp", "k_tp", "qT_ready",
                     "kT_ready", "z_ready", "z_read", "p_ready", "pt0", "pt1", "pt_sb0", "pt_sb1",
                     "o_ready", "o_read", "bias_landed", "bias_ready", "abs_done", "exp_done", "lp_ready",
                     "sp_ready", "sp_masked", "scanned", "w_exp", "summed", "inverse", "mixed", "yd_ready",
                     "yd_ss_ready", "yd_ms_ready", "yd_rstd_ready", "merged_ready"]
            used = {"sb": set(names) - {"squared", "qk_ms_ready", "qk_rstd_ready", "bias_landed", "bias_ready",
                                        "summed", "inverse", "mixed", "yd_ready", "yd_ss_ready", "yd_ms_ready",
                                        "yd_rstd_ready", "merged_ready"},
                    "df": set(names) - {"abs_done", "exp_done", "lp_ready", "sp_ready", "sp_masked", "scanned",
                                        "w_exp"},
                    "ca": set(names) - {"abs_done", "exp_done", "lp_ready", "sp_ready", "sp_masked", "scanned",
                                        "w_exp", "mixed", "yd_ready", "yd_ss_ready", "yd_ms_ready",
                                        "yd_rstd_ready", "merged_ready"}}[kind]
            return {n: sem(f"{kind}_{n}") for n in names if n in used}

        SBS, DFS, CAS = attention_sems("sb"), attention_sems("df"), attention_sems("ca")

        s_wout = sem("s_wout"); c_w_hi = sem("c_w_hi"); c_w_lo = sem("c_w_lo"); s_x_again = [sem("s_x_again0"), sem("s_x_again1")]
        c_stage = sem("c_stage"); c_tp = sem("c_tp"); c_mT_act = sem("c_mT_act"); c_mT_dve = sem("c_mT_dve")
        c_acc = sem("c_acc"); c_h2 = sem("c_h2"); c_sq = sem("c_sq"); c_ms = sem("c_ms"); c_rstd = sem("c_rstd")
        c_f = sem("c_f"); c_fsaved = sem("c_fsaved"); c_ftp = sem("c_ftp")
        c_fT_act = sem("c_fT_act"); c_fT_dve = sem("c_fT_dve"); c_lg = sem("c_lg"); c_logits = sem("c_logits")
        r_dve = sem("r_dve"); r_gexp_in = sem("r_gexp_in"); r_gexp = sem("r_gexp"); r_esec_in = sem("r_esec_in")
        r_esec = sem("r_esec"); r_hot = sem("r_hot"); r_counted = sem("r_counted"); r_vals = sem("r_vals")
        r_rows = sem("r_rows"); r_table = sem("r_table"); r_idx = sem("r_idx"); s_gain = sem("s_gain")
        unit_landed = [(w_landed[0], CH), (w_landed[1], CH), (DFS["bias_landed"], DF_PAIRS),
                       (CAS["bias_landed"], 2 * CA_PAIRS), (s_wout, 1), (sem("unit_landed5"), 0)]
        unit_hi = sem("unit_hi"); unit_lo = sem("unit_lo"); unit_used = sem("unit_used")
        tok_ready = sem("tok_ready"); row_ready = sem("row_ready"); xg_zero = sem("xg_zero"); xg_landed = sem("xg_landed")
        x_tp = sem("x_tp"); xT_act = sem("xT_act"); xT_dve = sem("xT_dve")
        silu_ready = sem("silu_ready"); hT_high = sem("hT_high")
        h_ready = sem("h_ready"); h_tp = sem("h_tp"); hT_ready = sem("hT_ready")
        y_act = sem("y_act"); y_dve = sem("y_dve"); y_stored = sem("y_stored")
        s_y = s_x
        f_part = sem("f_part"); f_out = sem("f_out"); out_stored = sem("out_stored")

        class Plan:

            def __init__(self, kind, s, q, k, v, o, pairs):
                self.kind, self.s, self.q, self.k, self.v, self.o, self.pairs = kind, s, q, k, v, o, pairs
                self.units = 2 * T
                self.results = T if kind == "df" else 2 * T

            def tile(self, r):
                return r if self.kind == "df" else r // 2

            def keys(self, t):
                first = max(0, t - BAND) if self.kind == "ca" else 0
                return first, t + 1 - first

            def groups(self, r):
                n = self.keys(self.tile(r))[1]
                return [list(range(g, min(g + 4, n))) for g in range(0, n, 4)]

            def group_no(self, g, r):
                has = [len(self.groups(i)) > g for i in range(self.results)]
                return sum(has[:r]), sum(has)

        SB = Plan("sb", SBS, SB_Q, SB_K, SB_V, SB_O, SB_PAIRS)
        DF = Plan("df", DFS, DF_Q, DF_K, DF_V, DF_O, DF_PAIRS)
        CA = Plan("ca", CAS, CA_Q, CA_K, CA_V, CA_O, CA_PAIRS)

        def qk_gains(a):
            if a.kind == "sb":
                return SCALE, 1.0
            c = 0 if a.kind == "df" else 2
            return qk_gain[:, c:c + 1], qk_gain[:, c + 1:c + 2]

        def cols(first, p, width=P, step=P):
            return bass.ds(p * step + first, width)

        def wait_alone(eng, semaphore, value):
            eng.wait_ge(semaphore, value)
            eng.sem_inc(s_waits_met, 1)

        def wait_slot(eng, a, p, r, slots):
            back = r - slots if r >= slots else max(i for i in range(a.results) if i % slots == r % slots)
            g = len(a.groups(back)) - 1
            before, per = a.group_no(g, back)
            eng.wait_ge(a.s[f"pt{g}"], p * per + (before + 1 + (per if r >= slots else 0)))

        block = ctx.enter_context(nc.Block())

        @block.sync
        def _(sp):
            for i in range(4):
                sp.dma_start(x_all[:, i, :], x_rows[i * P:(i + 1) * P, :]).then_inc(s_x[i], 16)
                if i == 0:
                    sp.dma_start(attn_gain[:, :], attn_norm.to_broadcast([P, D])).then_inc(s_gain, 16)
            for i in range(4):
                sp.wait_ge(s_x[i], 16)
                sp.dma_start(x_all[:, 4 + i, :], x_rows[(4 + i) * P:(5 + i) * P, :]).then_inc(s_x[i], 16)
            w_in_tiles = w_in[0].rearrange("(h k p) n -> h p k n", p=P, h=2)
            for h in range(2):
                sp.dma_start(w_in_ring[:, h, :, :], w_in_tiles[h, :, :, 0:BANK]).then_inc(w_landed[h], 16)
            sp.dma_start(lines_in[:, 0:T5_BUCKETS], t5_bias.rearrange("b h -> h b"), allow_slow_non_contiguous=True) \
                .then_inc(s_lines_in, 16)
            sp.dma_start(lines_in[:, T5_BUCKETS:], ca_rel_bias[0].rearrange("b h -> h b"),
                         allow_slow_non_contiguous=True).then_inc(s_lines_in, 16)
            sp.dma_start(subln[:, :], diff_subln.to_broadcast([P, 2 * HEAD])).then_inc(s_const, 16)
            sp.dma_start(lam_in[:, :], diff_lambda[0].rearrange("(o a) b -> o (a b)", o=1).to_broadcast([P, 4 * HEAD])) \
                .then_inc(s_const, 16)
            for half in range(2):
                for n, gain in enumerate((diff_qk_norm, ca_qk_norm)):
                    sp.dma_start(qk_gain[HEAD * half:HEAD * (half + 1), 2 * n:2 * n + 2],
                                 gain[0].rearrange("a b -> b a"), allow_slow_non_contiguous=True).then_inc(s_const, 16)
            sp.dma_start(w_r[:, :, 0:NG], group_w[0].rearrange("(k p) n -> p k n", p=P),
                         allow_slow_non_contiguous=True).then_inc(s_const, 16)
            sp.dma_start(w_r[:, :, NG:NR], expert_w[0].rearrange("(k p) n -> p k n", p=P)).then_inc(s_const, 16)
            sp.dma_start(b_r[:, 0:NG], group_b.to_broadcast([P, NG])).then_inc(s_const, 16)
            sp.dma_start(b_r[:, NG:NR], expert_b.to_broadcast([P, NE])).then_inc(s_const, 16)
            with sp.Fori(1, CH) as c:
                for h in range(2):
                    if h == 0:
                        sp.wait_ge(w_half_used, c)
                    else:
                        sp.wait_ge(acc_ready, c * T)
                    sp.dma_start(w_in_ring[:, h, :, :], w_in_tiles[h, :, :, bass.ds(c * BANK, BANK)]).then_inc(w_landed[h], 16)

            def bias_loads(a, line, tiles):
                with sp.Fori(0, a.pairs) as p:
                    sp.wait_ge(a.s["z_read"], p * a.units + 2)
                    for m, tile in enumerate(tiles):
                        src = bass.AP(line.tensor, (p * len(tiles) + m) * line.shape[1], [[1, P], [1, tile.shape[1]]])
                        sp.dma_start(tile, src).then_inc(a.s["bias_landed"], 16)

            sp.wait_ge(n_a, T)
            sp.dma_start(attn_gain[:, :], ffn_norm.to_broadcast([P, D])).then_inc(s_gain, 16)
            sp.wait_ge(s_lines_out, 32)
            sp.wait_ge(acc_act, (CH + 1) * T // 2)
            sp.wait_ge(acc_dve, (CH + 1) * T // 2)
            bias_loads(DF, t5_line, [df_bias])
            bias_loads(CA, ca_line, ca_bias)

            sp.wait_ge(DFS["merged_ready"], DF.pairs * DF.results)
            sp.dma_start(w_out_in, w_out[0].rearrange("(k p) n -> p k n", p=P)).then_inc(s_wout, 16)
            sp.wait_ge(CAS["o_read"], 2 + CA.pairs * CA.results)
            for j in range(2):
                half = T // 2 * P
                sp.dma_start(h2[:, j * (T // 2):(j + 1) * (T // 2), :],
                             x_rows[j * half:(j + 1) * half, :].rearrange("(t p) d -> p t d", p=P)).then_inc(s_x_again[j], 16)

            def load_unit(u, e):
                if u < 4:
                    src = (w_gate, w_up)[u // 2][0, e, :, :].rearrange("(h k p) n -> h p k n", p=P, h=2)[u % 2]
                else:
                    src = w_down[0, e, :, :].rearrange("(k p) n -> p k n", p=P)[:, :, (u - 4) * BANK:(u - 3) * BANK]
                sp.dma_start(unit_in[u], src).then_inc(unit_landed[u][0], 16)

            sp.wait_ge(c_acc, 4 + 2 * T)
            for u in range(4):
                load_unit(u, 0)
            sp.wait_ge(c_sq, T + 1)
            for u in (4, 5):
                load_unit(u, 0)
            sp.wait_ge(r_idx, 1)
            last_b = sp.value_load(last_i[0:1, 0:1], min_val=NE - 1, max_val=NB - 2)
            e = sp.value_load(be_i[0:1, 1:2], min_val=0, max_val=NE - 1)
            for u in range(4):
                sp.wait_ge(unit_used, u + 1)
                load_unit(u, e)
            with sp.Fori(2, last_b + 1) as b:
                for u in range(UNITS):
                    if u in (0, 4):
                        e = sp.value_load(be_i[0:1, bass.ds(b if u == 0 else b - 1, 1)], min_val=0, max_val=NE - 1)
                    wait_alone(sp, unit_used, b * UNITS + (u + 1 - UNITS))
                    load_unit(u, e)
            e = sp.value_load(be_i[0:1, bass.ds(last_b, 1)], min_val=0, max_val=NE - 1)
            for u in (4, 5):
                wait_alone(sp, unit_used, last_b * UNITS + (u + 1))
                load_unit(u, e)

            wait_alone(sp, y_stored, last_b * 16 + 16)
            sp.wait_ge(unit_used, last_b * UNITS + (UNITS + 2))
            y_t = y_rows.rearrange("(t c p) d -> p t c d", p=P, c=TOP)
            for i in range(4):
                sp.dma_start(y_tiles[:, i, :, :], y_t[:, i, :, :]).then_inc(s_y[i], 16)
            for i in range(4):
                sp.wait_ge(s_y[i], 48)
                sp.dma_start(y_tiles[:, 4 + i, :, :], y_t[:, 4 + i, :, :]).then_inc(s_y[i], 16)
            out_t = out[0].rearrange("(t p) d -> t p d", p=P)
            for t in range(T):
                sp.wait_ge(f_out, t + 1)
                sp.dma_start(out_t[t], h2[:, t, :]).then_inc(out_stored, 16)
            sp.wait_ge(out_stored, 16 * T)

        @block.tensor
        def _(pe):
            for a in (SB, DF, CA):
                for g in range(2):
                    pe.sem_inc(a.s[f"pt{g}"], a.group_no(g, 0)[1])
            pe.sem_inc(c_acc, 4)
            pe.wait_ge(s_ident, 2)

            def transpose_tile(src, first_bank):
                for k in range(KD):
                    last = pe.transpose(psum[:, first_bank + k // 4, (k % 4) * P:(k % 4 + 1) * P],
                                        src[:, k * P:(k + 1) * P], ident[:, :])
                return last

            with pe.Fori(0, T // 2) as i:
                for j in range(2):
                    pe.wait_ge(n_a, i * 2 + (j + 1))
                    pe.wait_ge(n_aT_hi, i * 2 + (j + 1))
                    pe.wait_ge(n_aT_lo, i * 2 + (j + 1))
                    transpose_tile(a_buf[:, j, :], 2 * j).then_inc(n_tp, 1)

            def split_product(out, pairs, start, stop):
                n = 0
                for l_hi, l_lo, r_hi, r_lo in pairs:
                    for lhs, rhs in ((l_hi, r_hi), (l_hi, r_lo), (l_lo, r_hi)):
                        last = pe.matmul(out, lhs, rhs, start=start and n == 0,
                                         stop=stop and n == 3 * len(pairs) - 1)
                        n += 1
                return last

            pe.wait_ge(n_aT_hi, 2 + T)
            pe.wait_ge(n_aT_lo, 2 + T)
            with pe.Fori(0, CH) as c:
                for h in range(2):
                    pe.wait_ge(w_lo, c * 2 + (h + 1))
                    for t in range(T):
                        if h == 0:
                            pe.wait_ge(acc_act if t % 2 == 0 else acc_dve, c * (T // 2) + (t // 2 + 1))
                        rows = range(h * KD // 2, (h + 1) * KD // 2)
                        last = split_product(psum[:, t, :],
                                             [(aT_hi[:, k, t * P:(t + 1) * P], aT_lo[:, k, t * P:(t + 1) * P],
                                               w_in_hi[h][:, k % (KD // 2), :], w_in_lo[h][:, k % (KD // 2), :])
                                              for k in rows], start=h == 0, stop=h == 1)
                        if h == 1:
                            last.then_inc(acc_ready, 1)
                    if h == 0:
                        last.then_inc(w_half_used, 1)

            def transpose_qk(a, p):
                pe.wait_ge(a.s["staged"], p * 2 + 2)
                for stage, first, done in ((q_stage, 0, "q_tp"), (k_stage, 2, "k_tp")):
                    for t in range(T):
                        last = pe.transpose(psum[:, first + t // 4, (t % 4) * P:(t % 4 + 1) * P], stage[:, t, :],
                                            ident[:, :])
                    last.then_inc(a.s[done], 1)

            def transpose_next(a, p, after):
                pe.wait_ge(a.s["z_read"], (p + 1) * a.units + 2)
                transpose_qk(*after)

            def wait_qk(a, p):
                pe.wait_ge(a.s["qT_ready"], p * 2 + 2)
                pe.wait_ge(a.s["kT_ready"], p * 2 + 2)

            def logits_of(a, p, u):
                t, m = u // 2, u % 2
                first, n = a.keys(t)
                pe.wait_ge(a.s["z_read"], p * a.units + (u + 1))
                rows = slice(HEAD * m, HEAD * (m + 1))
                for c in range(0, n * P, BANK):
                    w = min(BANK, n * P - c)
                    q, k = slice(t * P, (t + 1) * P), slice(first * P + c, first * P + c + w)
                    last = split_product(psum[:, 2 * m + c // BANK, 0:w],
                                         [(qT_hi[rows, q], qT_lo[rows, q], kT_hi[rows, k], kT_lo[rows, k])],
                                         start=True, stop=True)
                last.then_inc(a.s["z_ready"], 1)

            def transpose_weights(a, p, r, weights):
                pe.wait_ge(a.s["p_ready"], p * a.results + (r + 1))
                groups = a.groups(r)
                for g, tiles in enumerate(groups):
                    before, per = a.group_no(g, r)
                    pe.wait_ge(a.s[f"pt_sb{g}"], p * per + (before + 1))
                    for c in tiles:
                        last = pe.transpose(psum[:, 4 + g, (c % 4) * P:(c % 4 + 1) * P], weights[:, c * P:(c + 1) * P],
                                            ident[:, :])
                    last.then_inc(a.s[f"pt{g}"], 1)

            def result_of(a, p, r):
                first, n = a.keys(a.tile(r))
                width = 2 * HEAD if a.kind == "df" else HEAD
                head = 0 if a.kind == "df" else HEAD * (r % 2)
                groups = a.groups(r)
                pe.wait_ge(a.s["o_read"], p * a.results + (r + 1))
                for g, tiles in enumerate(groups):
                    before, per = a.group_no(g, r)
                    pe.wait_ge(a.s[f"pt_sb{g}"], p * per + (before + 2))
                    for c in tiles:
                        last = pe.matmul(psum[:, 6 + r % 2, 0:width], pt_sb[:, g, (c % 4) * P:(c % 4 + 1) * P],
                                         proj[:, first + c, cols(a.v + head, p, width)], start=(c == 0), stop=(c == n - 1))
                last.then_inc(a.s["o_ready"], 1)

            pe.wait_ge(acc_act, (CH + 1) * T // 2)
            pe.wait_ge(acc_dve, (CH + 1) * T // 2)
            transpose_qk(SB, 0)

            def sb_pair(p, after):
                wait_qk(SB, p)
                for s in range(SB.units + 3):
                    if s < SB.units:
                        logits_of(SB, p, s)
                    if s == SB.units + 1:
                        transpose_next(SB, p, after)
                    if s >= 3:
                        result_of(SB, p, s - 3)
                    if 2 <= s < SB.units + 2:
                        transpose_weights(SB, p, s - 2, work[:, (s - 2) % 2, :])

            with pe.Fori(0, SB.pairs - 1) as p:
                sb_pair(p, (SB, p + 1))
            sb_pair(SB.pairs - 1, (DF, 0))
            pe.wait_ge(SBS["o_read"], 2 + SB.pairs * SB.results)

            def df_pair(p, after):
                wait_qk(DF, p)
                for s in range(T + 2):
                    if s >= 2:
                        transpose_weights(DF, p, s - 2, work[:, 2 * ((s - 2) % 3), :])
                    if s < T:
                        logits_of(DF, p, 2 * s)
                        logits_of(DF, p, 2 * s + 1)
                    if s == T:
                        transpose_next(DF, p, after)
                    if s >= 2:
                        result_of(DF, p, s - 2)

            with pe.Fori(0, DF.pairs - 1) as p:
                df_pair(p, (DF, p + 1))
            df_pair(DF.pairs - 1, (CA, 0))
            pe.wait_ge(DFS["merged_ready"], DF.pairs * DF.results)

            def ca_pair(p, after):
                wait_qk(CA, p)
                for s in range(CA.units + 2):
                    if s >= 2:
                        transpose_weights(CA, p, s - 2, work[:, (s - 2) % 4, :])
                    if s < CA.units:
                        logits_of(CA, p, s)
                    if s == CA.units and after:
                        transpose_next(CA, p, after)
                    if s >= 2:
                        result_of(CA, p, s - 2)

            with pe.Fori(0, CA.pairs - 1) as p:
                ca_pair(p, (CA, p + 1))
            ca_pair(CA.pairs - 1, None)
            pe.wait_ge(CAS["o_read"], 2 + CA.pairs * CA.results)

            def merged_tile(i, j, first=False):
                if not first:
                    pe.wait_ge(c_stage, i * 2 + (j - 1))
                pe.wait_ge(c_mT_act, i * 2 + (j + 1))
                pe.wait_ge(c_mT_dve, i * 2 + (j + 1))
                transpose_tile(merged[:, j, :] if first else m_stage[j % 2], 0).then_inc(c_tp, 1)

            def out_half(i, j, n):
                if n == 0:
                    pe.wait_ge(c_mT_act, i * 2 + (j + 2))
                    pe.wait_ge(c_mT_dve, i * 2 + (j + 2))
                pe.wait_ge(c_h2, i * 4 + (2 * j + n + 1))
                cs = slice(n * BANK, (n + 1) * BANK)
                split_product(psum[:, 2 + n, :], [(mT_hi[j % 2][:, k, :], mT_lo[j % 2][:, k, :], w_out_hi[:, k, cs],
                                                   w_out_lo[:, k, cs]) for k in range(KD)],
                              start=True, stop=True).then_inc(c_acc, 1)

            def f_tile(i, j):
                pe.wait_ge(c_f, i * 2 + (j + 1))
                pe.wait_ge(c_logits, i * 2 + (j + 1))
                transpose_tile(f_buf[:, j % 2, :], 4).then_inc(c_ftp, 1)

            def router_tile(i, j):
                pe.wait_ge(c_fT_act, i * 2 + (j + 1))
                pe.wait_ge(c_fT_dve, i * 2 + (j + 1))
                for k in range(KD):
                    last = pe.matmul(psum[:, 6, 0:NR], fT[:, k, :], w_r[:, k, :], start=(k == 0), stop=(k == KD - 1))
                last.then_inc(c_lg, 1)

            merged_tile(0, 0, first=True)
            merged_tile(0, 1, first=True)
            pe.wait_ge(c_w_lo, KD)
            out_half(0, 0, 0)
            out_half(0, 0, 1)
            with pe.Fori(0, T // 2 - 1) as i:
                for j in (1, 2):
                    merged_tile(i, j + 1)
                    out_half(i, j, 0)
                    f_tile(i, j - 1)
                    out_half(i, j, 1)
                    router_tile(i, j - 1)
            out_half(T // 2 - 1, 1, 0)
            f_tile(T // 2 - 1, 0)
            out_half(T // 2 - 1, 1, 1)
            router_tile(T // 2 - 1, 0)
            f_tile(T // 2 - 1, 1)
            router_tile(T // 2 - 1, 1)

            pe.wait_ge(r_hot, 1)
            pe.wait_ge(s_pool_const, 1)
            ranks = psum[:, 0, 0:T * NE].rearrange("p (t e) -> p t e", t=T)
            for t in range(T - 1):
                later = T - 1 - t
                rhs = bass.AP(hot_sum[:, t, :].tensor, t * NE, [[T * NE, P], [0, later], [1, NE]])
                pe.matmul(ranks[:, t + 1:T, :], ones_b[:, :], rhs, start=(t == 0), stop=False, skip_group_check=True)
            pe.matmul(ranks, tri[:, :], hot_sum[:, :, :], start=False, stop=True, skip_group_check=True)
            for t in range(T):
                last = pe.matmul(psum[:, 1, 0:NE], ones_b[:, :], hot_sum[:, t, :], start=(t == 0), stop=(t == T - 1))
            last.then_inc(r_counted, 1)
            pe.wait_ge(r_vals, 1)
            n = 0
            for t in range(T):
                for c in range(TOP):
                    last = pe.matmul(psum[:, 2, 0:3 * NB], pos_hot[:, c, t, :],
                                     blk_vals[:, c, t, :, :].rearrange("p a b -> p (a b)"),
                                     start=(n == 0), stop=(n == TOP * T - 1))
                    n += 1
            last.then_inc(r_rows, 1)

            def gather_tp(b):
                pe.wait_ge(xg_landed, b * 16 + 16)
                for k in range(KD):
                    last = pe.transpose(psum[:, 4 + k // 4, (k % 4) * P:(k % 4 + 1) * P], xg[:, k * P:(k + 1) * P],
                                        ident[:, :])
                last.then_inc(x_tp, 1)

            def unit_product(u, i, bank, high, low_part, start, stop):
                pe.wait_ge(unit_lo, i + 1)
                split_product(psum[:, bank, :], [(high[:, k, :], low_part[:, k, :], unit_hi_w[u][:, k, :], unit_lo_w[u][:, k, :])
                                                 for k in range(KE)], start=start, stop=stop).then_inc(unit_used, 1)

            def gate_up(b):
                pe.wait_ge(xT_act, b + 1)
                pe.wait_ge(xT_dve, b + 1)
                for u in range(4):
                    rows = slice(u % 2 * KE, (u % 2 + 1) * KE)
                    unit_product(u, b * UNITS + u, u // 2, xT_hi[:, rows, :], xT_lo[:, rows, :], u % 2 == 0, u % 2 == 1)

            def hidden_tp(b):
                pe.wait_ge(h_ready, b + 1)
                for k in range(KE):
                    last = pe.transpose(psum[:, 6, k * P:(k + 1) * P], hid[:, k * P:(k + 1) * P], ident[:, :])
                last.then_inc(h_tp, 1)

            def down(b, i):
                pe.wait_ge(hT_ready, b + 1)
                pe.wait_ge(y_act, b + 1)
                pe.wait_ge(y_dve, b + 1)
                for n in range(2):
                    unit_product(4 + n, i + n, 2 + n, hT_hi[:, :, :], hT_lo[:, :, :], True, True)

            pe.wait_ge(r_vals, 1)
            last_b = pe.value_load(last_i[0:1, 0:1], min_val=NE - 1, max_val=NB - 2)
            gather_tp(0)
            gate_up(0)
            pe.wait_ge(unit_used, 4)
            pe.sem_inc(unit_used, 2)
            gather_tp(1)
            with pe.Fori(1, last_b + 1) as b:
                hidden_tp(b - 1)
                gate_up(b)
                gather_tp(b + 1)
                down(b - 1, b * UNITS + 4)
            hidden_tp(last_b)
            down(last_b, last_b * UNITS + UNITS)

        @block.scalar
        def _(act):
            act.sem_inc(n_aT_hi, 2)
            act.sem_inc(n_sq, 1)
            act.sem_inc(c_sq, 1)
            act.sem_inc(acc_act, T // 2)
            for a in (SB, DF, CA):
                act.sem_inc(a.s["pt_sb0"], 1)
            act.sem_inc(SBS["o_read"], 2)
            act.sem_inc(c_mT_act, 1)
            act.sem_inc(y_act, 1)
            def high_w_in(c, h):
                act.wait_ge(w_landed[h], c * 16 + 16)
                act.copy(w_in_hi[h][:, :, :], w_in_ring[:, h, :, :]).then_inc(w_hi, 1)

            def copy_proj(c, t):
                act.wait_ge(acc_ready, c * T + (t + 1))
                act.copy(proj[:, t, bass.ds(c * BANK, BANK)], psum[:, t, :]).then_inc(acc_act, 1)

            for t in range(T + 2):
                if t < T:
                    act.wait_ge(s_x[t % 4], 16 * (t // 4 + 1))
                    act.wait_ge(n_sq, t + 1)
                    act.activation(norm_junk, x_all[:, t, :], ACT.Square, accum_out=ss[:, t:t + 1]).then_inc(n_sq, 1)
                if t >= 2:
                    act.wait_ge(n_tp, t - 1)
                    act.copy(aT_hi[:, :, (t - 2) * P:(t - 1) * P],
                             banks(2 * (t % 2), 2).rearrange("p (a b) -> p a b", a=KD)).then_inc(n_aT_hi, 1)
                if t == T - 1:
                    high_w_in(0, 0)
            high_w_in(0, 1)
            act.wait_ge(s_lam_sum, 2)
            act.activation(lam_exp[:, :], lam_sum[:, :], ACT.Exp).then_inc(s_lam_exp, 1)
            act.wait_ge(s_lines, 2)
            act.dma_start(t5_line[:, 0:T5_LINE], t5_sb[:, 0:T5_LINE]).then_inc(s_lines_out, 16)
            act.dma_start(ca_line[:, 0:CA_LINE], ca_sb[:, 0:CA_LINE]).then_inc(s_lines_out, 16)
            act.wait_ge(s_lines_out, 32)
            with act.Fori(0, CH - 1) as c:
                copy_proj(c, 0)
                high_w_in(c + 1, 0)
                for t in range(2, T, 2):
                    copy_proj(c, t)
                high_w_in(c + 1, 1)
            for t in range(0, T, 2):
                copy_proj(CH - 1, t)

            def high_qk(a, p):
                q_gain, k_gain = qk_gains(a)
                for name, bank, gain, high in (("q", 0, q_gain, qT_hi), ("k", 2, k_gain, kT_hi)):
                    act.wait_ge(a.s[f"{name}_tp"], p + 1)
                    act.activation(high[:, :], banks(bank, 2), ACT.Copy, scale=gain).then_inc(a.s[f"{name}T_ready"], 1)

            def copy_pt0(a, p, r):
                before, per = a.group_no(0, r)
                w = len(a.groups(r)[0]) * P
                act.wait_ge(a.s["pt0"], p * per + (before + 1 + per))
                act.copy(pt_sb[:, 0, 0:w], psum[:, 4, 0:w]).then_inc(a.s["pt_sb0"], 1)

            def squares_of(a, p):
                for n, first in enumerate((a.q, a.k)):
                    act.wait_ge(a.s["qk_ms_ready"], p * 2 + 1)
                    act.activation(squares[:, n, :, :], proj[:, :, cols(first, p)], ACT.Square) \
                        .then_inc(a.s["squared"], 1)

            def exp_rows(a, p, u, slot, stat, m):
                t = u // 2
                w = a.keys(t)[1] * P
                act.wait_ge(a.s["z_read"], p * a.units + (u + 3))
                act.activation(work[:, slot, 0:w], work[:, slot, 0:w], ACT.Exp, bias=low[:, stat, m:m + 1], scale=-1.0,
                               accum_out=total[:, stat, m:m + 1]).then_inc(a.s["summed" if a.kind == "df" else "p_ready"], 1)

            def sb_softplus_tail(p, u):
                w, buf = SB.keys(u // 2)[1] * P, 2 + u % 2
                act.wait_ge(SBS["z_ready"], p * SB.units + (u + 1))
                act.wait_ge(SBS["z_read"], p * SB.units + (u + 1))
                act.activation(work[:, buf, 0:w], banks(2 * (u % 2), 2)[:, 0:w], ACT.Abs).then_inc(SBS["abs_done"], 1)
                act.wait_ge(SBS["abs_done"], p * SB.units + (u + 1))
                act.activation(work[:, buf, 0:w], work[:, buf, 0:w], ACT.Exp, scale=-1.0).then_inc(SBS["exp_done"], 1)
                act.wait_ge(SBS["exp_done"], p * SB.units + (u + 1))
                act.activation(work[:, buf, 0:w], work[:, buf, 0:w], ACT.Ln, bias=1.0).then_inc(SBS["lp_ready"], 1)

            def sb_weights(p, u):
                w, buf = SB.keys(u // 2)[1] * P, u % 2
                act.wait_ge(SBS["z_read"], p * SB.units + (u + 3))
                wait_slot(act, SB, p, u, 2)
                act.activation(work[:, buf, 0:w], work[:, 4 + buf, 0:w], ACT.Exp).then_inc(SBS["w_exp"], 1)

            def sb_merge(p, r):
                act.wait_ge(SBS["o_ready"], p * SB.results + (r + 1))
                act.copy(merged[:, r // 2, cols(SB_O + HEAD * (r % 2), p, HEAD)], psum[:, 6 + r % 2, 0:HEAD]) \
                    .then_inc(SBS["o_read"], 1)

            act.preload_act_table_set("natural_log_exp_and_others")
            high_qk(SB, 0)

            def sb_pair(p, after):
                for s in range(SB.units + 4):
                    if 3 <= s < SB.units + 3:
                        copy_pt0(SB, p, s - 3)
                    if s < SB.units:
                        sb_softplus_tail(p, s)
                    if 1 <= s <= SB.units:
                        sb_weights(p, s - 1)
                    if s == SB.units + 1:
                        high_qk(*after)
                    if s >= 4:
                        sb_merge(p, s - 4)
                    if s == 5 and after[0] is DF:
                        squares_of(*after)

            with act.Fori(0, SB.pairs - 1) as p:
                sb_pair(p, (SB, p + 1))
            sb_pair(SB.pairs - 1, (DF, 0))
            act.wait_ge(SBS["o_read"], 2 + SB.pairs * SB.results)
            act.preload_act_table_set("exp_and_others")

            def df_pair(p, after):
                for s in range(T + 2):
                    if s >= 2:
                        copy_pt0(DF, p, s - 2)
                    if s == T:
                        high_qk(*after)
                    if s < T:
                        for m in range(2):
                            exp_rows(DF, p, 2 * s + m, 2 * (s % 3) + m, s % 4, m)
                    if s == 2:
                        squares_of(*after)

            with act.Fori(0, DF.pairs - 1) as p:
                df_pair(p, (DF, p + 1))
            df_pair(DF.pairs - 1, (CA, 0))
            act.wait_ge(DFS["merged_ready"], DF.pairs * DF.results)

            def ca_pair(p, after):
                for s in range(CA.units + 2):
                    if s >= 2:
                        copy_pt0(CA, p, s - 2)
                    if s == CA.units and after:
                        high_qk(*after)
                    if s < CA.units:
                        exp_rows(CA, p, s, s % 4, s % 8 // 2, s % 2)
                    if s == 4 and after:
                        squares_of(*after)
                    if 4 <= s < 4 + KD and not after:
                        act.wait_ge(s_wout, 16)
                        act.copy(w_out_hi[:, s - 4, :], w_out_in[:, s - 4, :]).then_inc(c_w_hi, 1)

            with act.Fori(0, CA.pairs - 1) as p:
                ca_pair(p, (CA, p + 1))
            ca_pair(CA.pairs - 1, None)
            act.wait_ge(CAS["o_read"], 2 + CA.pairs * CA.results)

            def copy_mT(i, j):
                act.wait_ge(c_tp, i * 2 + (j + 1))
                act.wait_ge(c_acc, i * 4 + (2 * j + 2))
                act.copy(mT_hi[j % 2][:, :, :], banks(0, 2).rearrange("p (a b) -> p a b", a=KD)).then_inc(c_mT_act, 1)

            def square_sum(i, j):
                act.wait_ge(c_h2, i * 4 + (2 * j + 4))
                act.wait_ge(c_sq, i * 2 + (j + 1))
                act.activation(out_junk, h2[:, bass.ds(i * 2 + j, 1), :].rearrange("p a b -> p (a b)"), ACT.Square,
                               accum_out=ss[:, bass.ds(i * 2 + j, 1)]).then_inc(c_sq, 1)

            def store_f(i, j):
                act.wait_ge(c_f, i * 2 + (j + 1))
                act.wait_ge(c_fsaved, i * 32 + 16 * (j + 2))
                act.dma_start(f_rows[bass.ds(i * 2 * P + j * P, P), :], f_buf[:, j % 2, :]).then_inc(c_fsaved, 16)

            def copy_fT(i, j):
                act.wait_ge(c_ftp, i * 2 + (j + 1))
                act.copy(fT[:, 0:4, :], psum[:, 4, :].rearrange("p (a b) -> p a b", a=4)).then_inc(c_fT_act, 1)

            copy_mT(0, 0)
            copy_mT(0, 1)
            square_sum(0, 0)
            store_f(0, 0)
            with act.Fori(0, T // 2 - 1) as i:
                for j in (1, 2):
                    copy_mT(i, j + 1)
                    copy_fT(i, j - 1)
                    square_sum(i, j)
                    store_f(i, j)
            copy_fT(T // 2 - 1, 0)
            square_sum(T // 2 - 1, 1)
            store_f(T // 2 - 1, 1)
            copy_fT(T // 2 - 1, 1)

            act.wait_ge(r_gexp_in, 1)
            act.activation(g_exp[:, :, :], g_exp[:, :, :], ACT.Exp).then_inc(r_gexp, 1)
            act.wait_ge(r_esec_in, 1)
            act.activation(e_sec[:, :], e_gap[:, :], ACT.Exp).then_inc(r_esec, 1)

            def high_unit(u, times):
                landed, before = unit_landed[u]
                act.wait_ge(landed, times * 16 + before * 16)
                act.copy(unit_hi_w[u][:, :, :], unit_in[u]).then_inc(unit_hi, 1)

            def copy_xT(b):
                act.wait_ge(x_tp, b + 1)
                act.copy(xT_hi[:, :, :], banks(4, 2).rearrange("p (a b) -> p a b", a=KD)).then_inc(xT_act, 1)

            def silu_of(b):
                act.wait_ge(unit_used, b * UNITS + 2)
                act.activation(silu, psum[:, 0, :], ACT.Silu).then_inc(silu_ready, 1)

            def copy_hT(b):
                act.wait_ge(h_tp, b + 1)
                act.copy(hT_hi[:, :, :], psum[:, 6, :].rearrange("p (a b) -> p a b", a=KE)).then_inc(hT_high, 1)

            def copy_y(b, i, first=False):
                act.wait_ge(unit_used, i + 1)
                if not first:
                    act.wait_ge(y_stored, b * 16)
                act.copy(y_sb[:, 0:BANK], psum[:, 2, :]).then_inc(y_act, 1)

            def pass_of(b, first=False, final=False):
                copy_hT(b)
                high_unit(4, b + 1)
                high_unit(5, b + 1)
                silu_of(b + 1)
                if not final:
                    high_unit(0, b + 3)
                    high_unit(1, b + 3)
                copy_xT(b + 2)
                if not final:
                    high_unit(2, b + 3)
                copy_y(b, b * UNITS + (UNITS + 4), first)
                if not final:
                    high_unit(3, b + 3)

            for u in range(4):
                high_unit(u, 1)
            act.wait_ge(unit_hi, 4)
            act.sem_inc(unit_hi, 2)
            act.wait_ge(r_vals, 1)
            last_b = act.value_load(last_i[0:1, 0:1], min_val=NE - 1, max_val=NB - 2)
            before_last = act.value_load(last_i[0:1, 1:2], min_val=NE - 2, max_val=NB - 3)
            copy_xT(0)
            silu_of(0)
            high_unit(0, 2)
            high_unit(1, 2)
            copy_xT(1)
            high_unit(2, 2)
            high_unit(3, 2)
            pass_of(0, first=True)
            with act.Fori(1, before_last) as b:
                pass_of(b)
            pass_of(before_last, final=True)
            copy_hT(last_b)
            for u in (4, 5):
                high_unit(u, last_b + 1)
            copy_y(last_b, last_b * UNITS + UNITS)

        @block.vector
        def _(dve):
            dve.sem_inc(n_aT_lo, 2)
            dve.sem_inc(acc_dve, T // 2)
            for a in (SB, DF, CA):
                dve.sem_inc(a.s["pt_sb1"], 1)
                dve.sem_inc(a.s["z_read"], 2)
            for a in (DF, CA):
                dve.sem_inc(a.s["o_read"], 2)
                dve.sem_inc(a.s["qk_ms_ready"], 2)
            dve.sem_inc(c_mT_dve, 1)
            dve.sem_inc(c_h2, 2)
            dve.sem_inc(c_logits, 1)
            dve.sem_inc(y_dve, 1)
            dve.memset(ones[:, :], 1.0)
            dve.memset(mhalf[:, :], -0.5).then_inc(s_dve_const, 1)

            def low_aT(t):
                high = aT_hi[:, :, t * P:(t + 1) * P]
                dve.wait_ge(n_aT_hi, 2 + t + 1)
                dve.tensor_tensor(aT_lo[:, :, t * P:(t + 1) * P],
                                  banks(2 * (t % 2), 2).rearrange("p (a b) -> p a b", a=KD), high.bitcast(F32), ALU.subtract) \
                    .then_inc(n_aT_lo, 1)

            def low_w_in(c, h):
                dve.wait_ge(w_hi, c * 2 + (h + 1))
                dve.tensor_tensor(w_in_lo[h][:, :, :], w_in_ring[:, h, :, :], w_in_hi[h][:, :, :].bitcast(F32),
                                  ALU.subtract).then_inc(w_lo, 1)

            def copy_proj(c, t):
                dve.wait_ge(acc_ready, c * T + (t + 1))
                dve.tensor_copy(proj[:, t, bass.ds(c * BANK, BANK)], psum[:, t, :]).then_inc(acc_dve, 1)

            dve.wait_ge(s_gain, 16)
            for t in range(T + 2):
                if t < T:
                    for n in ((0, 1) if t == 0 else (t + 1,) if t + 1 < T else ()):
                        dve.wait_ge(n_sq, n + 2)
                        dve.tensor_scalar(ms[:, n:n + 1], ss[:, n:n + 1], 1.0 / D, EPS, ALU.mult, ALU.add).then_inc(n_ms, 1)
                    dve.wait_ge(n_rstd, t + 1)
                    if t >= 2:
                        dve.wait_ge(n_tp, t - 1)
                    dve.scalar_tensor_tensor(a_buf[:, t % 2, :], x_all[:, t, :], rstd[:, t:t + 1], attn_gain[:, :],
                                             ALU.mult, ALU.mult).then_inc(n_a, 1)
                if t >= 2:
                    low_aT(t - 2)
                if t == T:
                    low_w_in(0, 0)
            low_w_in(0, 1)
            dve.wait_ge(s_const, 16 * 10)
            for n in range(2):
                if n:
                    dve.wait_ge(s_lam_sum, n)
                dve.tensor_tensor_reduce(out=lam_junk[:, :], in0=lam_in[:, 2 * n * HEAD:(2 * n + 1) * HEAD],
                                         in1=lam_in[:, (2 * n + 1) * HEAD:(2 * n + 2) * HEAD], scale=1.0, scalar=0.0,
                                         op0=ALU.mult, op1=ALU.add, accum_out=lam_sum[:, n:n + 1]).then_inc(s_lam_sum, 1)
            dve.wait_ge(s_lam_exp, 1)
            dve.tensor_tensor(neg_lam[:, :], lam_exp[:, 1:2], lam_exp[:, 0:1], ALU.subtract).then_inc(s_lam, 1)
            dve.wait_ge(s_lam, 1)
            dve.tensor_scalar(neg_lam[:, :], neg_lam[:, :], LAM_INIT, None, ALU.subtract).then_inc(s_lam, 1)
            for c in (0, 2):
                dve.tensor_scalar(qk_gain[:, c:c + 1], qk_gain[:, c:c + 1], SCALE, None, ALU.mult).then_inc(s_lam, 1)
            dve.tensor_scalar(subln[:, :], subln[:, :], 1.0 - LAM_INIT, None, ALU.mult).then_inc(s_lam, 1)
            dve.wait_ge(s_lines_out, 32)
            with dve.Fori(0, CH - 1) as c:
                copy_proj(c, 1)
                low_w_in(c + 1, 0)
                for t in range(3, T, 2):
                    copy_proj(c, t)
                low_w_in(c + 1, 1)
            for t in range(1, T, 2):
                copy_proj(CH - 1, t)
            dve.wait_ge(s_lam, 5)

            def low_qk(a, p):
                q_gain, k_gain = qk_gains(a)
                for name, bank, gain, high, low_part in (("q", 0, q_gain, qT_hi, qT_lo), ("k", 2, k_gain, kT_hi, kT_lo)):
                    dve.wait_ge(a.s[f"{name}T_ready"], p * 2 + 1)
                    dve.scalar_tensor_tensor(low_part[:, :], banks(bank, 2), gain, high[:, :].bitcast(F32), ALU.mult,
                                             ALU.subtract).then_inc(a.s[f"{name}T_ready"], 1)

            def copy_pt1(a, p, r):
                if len(a.groups(r)) < 2:
                    return
                before, per = a.group_no(1, r)
                w = len(a.groups(r)[1]) * P
                dve.wait_ge(a.s["pt1"], p * per + (before + 1 + per))
                dve.tensor_copy(pt_sb[:, 1, 0:w], psum[:, 5, 0:w]).then_inc(a.s["pt_sb1"], 1)

            def mean_squares(a, p):
                dve.wait_ge(a.s["squared"], p * 2 + 2)
                dve.tensor_reduce(qk_ss[:, :, :].rearrange("p n g -> p (n g)"),
                                  squares.rearrange("p n t (h d) -> p (n t h) d", h=2), AX.X, ALU.add) \
                    .then_inc(a.s["qk_ms_ready"], 1)
                dve.wait_ge(a.s["qk_ms_ready"], p * 2 + 3)
                dve.tensor_scalar(qk_ms[:, :, :], qk_ss[:, :, :], 1.0 / HEAD, EPS, ALU.mult, ALU.add) \
                    .then_inc(a.s["qk_ms_ready"], 1)

            def biased(a, p, u, slot, stat, m, tile):
                t = u // 2
                first, n = a.keys(t)
                w = n * P
                wait_alone(dve, a.s["z_ready"], p * a.units + (u + 1))
                dve.tensor_tensor_reduce(out=work[:, slot, 0:w], in0=banks(2 * (u % 2), 2)[:, 0:w],
                                         in1=tile[:, 0:w][:, ::-1], scale=-1.0, scalar=-LOWEST,
                                         op0=ALU.add, op1=ALU.min, accum_out=low[:, stat, m:m + 1]) \
                    .then_inc(a.s["z_read"], 1)

            def mask_bias(a, p, tiles):
                dve.wait_ge(a.s["bias_landed"], p * 16 * len(tiles) + 16 * len(tiles))
                for tile in tiles:
                    last = dve.memset(tile[0:HEAD, 0:HEAD], MASKED)
                    if a.kind == "ca":
                        last = dve.memset(tile[HEAD:P, CA_W - HEAD:CA_W], MASKED)
                last.then_inc(a.s["bias_ready"], 1)

            def sb_softplus(p, u):
                w, buf = SB.keys(u // 2)[1] * P, u % 2
                dve.wait_ge(SBS["lp_ready"], p * SB.units + (u + 1))
                dve.scalar_tensor_tensor(work[:, 2 + buf, 0:w], banks(2 * buf, 2)[:, 0:w], 0.0, work[:, 2 + buf, 0:w],
                                         ALU.max, ALU.add).then_inc(SBS["sp_ready"], 1)

            def sb_exponent(p, u):
                w, buf = SB.keys(u // 2)[1] * P, u % 2
                dve.wait_ge(SBS["sp_masked"], p * SB.units + (u + 1))
                dve.tensor_tensor_scan(work[:, 4 + buf, 0:w][:, ::-1], ones[:, 0:1].to_broadcast([P, w]),
                                       work[:, 2 + buf, 0:w][:, ::-1], 0.0, ALU.mult, ALU.add).then_inc(SBS["scanned"], 1)
                dve.wait_ge(SBS["scanned"], p * SB.units + (u + 1))
                dve.tensor_tensor(work[:, 4 + buf, 0:w], banks(2 * buf, 2)[:, 0:w], work[:, 4 + buf, 0:w],
                                  ALU.subtract).then_inc(SBS["z_read"], 1)

            dve.wait_ge(acc_act, (CH + 1) * T // 2)
            dve.wait_ge(acc_dve, (CH + 1) * T // 2)
            for first, stage in ((SB.q, q_stage), (SB.k, k_stage)):
                dve.tensor_copy(stage, proj[:, :, first:first + P]).then_inc(SBS["staged"], 1)

            low_qk(SB, 0)

            def sb_pair(p, after):
                for s in range(SB.units + 3):
                    if s >= 3:
                        copy_pt1(SB, p, s - 3)
                    if 1 <= s <= SB.units:
                        sb_exponent(p, s - 1)
                    if s < SB.units:
                        sb_softplus(p, s)
                    if s == SB.units + 2:
                        low_qk(*after)
                    if s == 8 and after[0] is DF:
                        mean_squares(*after)

            with dve.Fori(0, SB.pairs - 1) as p:
                sb_pair(p, (SB, p + 1))
            sb_pair(SB.pairs - 1, (DF, 0))

            def df_mix(p, t):
                st = t % 4
                dve.wait_ge(DFS["summed"], p * DF.units + (2 * t + 2))
                dve.reciprocal(inv[:, st, :], total[:, st, :]).then_inc(DFS["inverse"], 1)
                dve.wait_ge(DFS["inverse"], p * 2 * T + (2 * t + 1))
                dve.tensor_scalar(mix[:, st:st + 1], inv[:, st, 1:2], total[:, st, 0:1], neg_lam[:, :], ALU.mult,
                                  ALU.mult).then_inc(DFS["inverse"], 1)
                w, buf = (t + 1) * P, 2 * (t % 3)
                dve.wait_ge(DFS["inverse"], p * 2 * T + (2 * t + 2))
                dve.scalar_tensor_tensor(work[:, buf, 0:w], work[:, buf + 1, 0:w], mix[:, st:st + 1], work[:, buf, 0:w],
                                         ALU.mult, ALU.add).then_inc(DFS["p_ready"], 1)

            def df_result(p, t):
                dve.wait_ge(DFS["o_ready"], p * T + (t + 1))
                dve.tensor_scalar(yd[:, t % 2, :], psum[:, 6 + t % 2, 0:P], inv[:, t % 4, 0:1], None, ALU.mult) \
                    .then_inc(DFS["o_read"], 1)
                dve.wait_ge(DFS["o_read"], p * T + (t + 3))
                dve.tensor_tensor_reduce(out=yd_junk[:, :], in0=yd[:, t % 2, :], in1=yd[:, t % 2, :], scale=1.0,
                                         scalar=0.0, op0=ALU.mult, op1=ALU.add,
                                         accum_out=yd_ss[:, t % 2:t % 2 + 1]).then_inc(DFS["yd_ss_ready"], 1)
                dve.wait_ge(DFS["yd_ss_ready"], p * T + (t + 1))
                dve.tensor_scalar(yd_ms[:, t % 2:t % 2 + 1], yd_ss[:, t % 2:t % 2 + 1], 1.0 / P, EPS, ALU.mult,
                                  ALU.add).then_inc(DFS["yd_ms_ready"], 1)

            def df_merge(p, t):
                dve.wait_ge(DFS["yd_rstd_ready"], p * T + (t + 1))
                dve.scalar_tensor_tensor(merged[:, t, cols(DF_O, p)], yd[:, t % 2, :], yd_rstd[:, t % 2:t % 2 + 1],
                                         subln[:, :], ALU.mult, ALU.mult).then_inc(DFS["merged_ready"], 1)

            dve.wait_ge(SBS["o_read"], 2 + SB.pairs * SB.results)
            def df_pair(p, after):
                mask_bias(DF, p, [df_bias])
                dve.wait_ge(DFS["bias_ready"], p + 1)
                for s in range(T + 4):
                    if 2 <= s < T + 2:
                        copy_pt1(DF, p, s - 2)
                    if 1 <= s <= T:
                        df_mix(p, s - 1)
                    if s < T:
                        wait_slot(dve, DF, p, s, 3)
                        for m in range(2):
                            biased(DF, p, 2 * s + m, 2 * (s % 3) + m, s % 4, m, df_bias)
                    if s == 3:
                        mean_squares(*after)
                    if s >= 4:
                        df_merge(p, s - 4)
                    if 3 <= s < T + 3:
                        df_result(p, s - 3)
                    if s == T + 1:
                        low_qk(*after)

            with dve.Fori(0, DF.pairs - 1) as p:
                df_pair(p, (DF, p + 1))
            df_pair(DF.pairs - 1, (CA, 0))

            dve.wait_ge(DFS["merged_ready"], DF.pairs * DF.results)
            def ca_pair(p, after):
                mask_bias(CA, p, ca_bias)
                dve.wait_ge(CAS["bias_ready"], p + 1)
                for s in range(CA.units + 3):
                    if 2 <= s < CA.units + 2:
                        copy_pt1(CA, p, s - 2)
                    if s < CA.units:
                        wait_slot(dve, CA, p, s, 4)
                        biased(CA, p, s, s % 4, s % 8 // 2, s % 2, ca_bias[s % 2])
                    if 1 <= s <= CA.units:
                        dve.wait_ge(CAS["p_ready"], p * CA.units + s)
                        st, m = (s - 1) % 8 // 2, (s - 1) % 2
                        dve.reciprocal(inv[:, st, m:m + 1], total[:, st, m:m + 1]).then_inc(CAS["inverse"], 1)
                    if s == CA.units + 1 and after:
                        low_qk(*after)
                    if s == 5 and after:
                        mean_squares(*after)
                    if 5 <= s < 5 + KD and not after:
                        k = s - 5
                        dve.wait_ge(c_w_hi, k + 1)
                        dve.tensor_tensor(w_out_lo[:, k, :], w_out_in[:, k, :], w_out_hi[:, k, :].bitcast(F32),
                                          ALU.subtract).then_inc(c_w_lo, 1)
                    if s >= 3:
                        r = s - 3
                        dve.wait_ge(CAS["o_ready"], p * CA.results + (r + 1))
                        dve.wait_ge(CAS["inverse"], p * CA.results + (r + 1))
                        dve.tensor_scalar(merged[:, r // 2, cols(CA_O + HEAD * (r % 2), p, HEAD)],
                                          psum[:, 6 + r % 2, 0:HEAD], inv[:, r % 8 // 2, r % 2:r % 2 + 1], None,
                                          ALU.mult) \
                            .then_inc(CAS["o_read"], 1)

            with dve.Fori(0, CA.pairs - 1) as p:
                ca_pair(p, (CA, p + 1))
            ca_pair(CA.pairs - 1, None)

            def row(tensor, i, j):
                return tensor[:, bass.ds(i * 2 + j, 1), :].rearrange("p a b -> p (a b)")

            dve.wait_ge(CAS["o_read"], 2 + CA.pairs * CA.results)
            dve.wait_ge(s_pool_const, 1)
            dve.wait_ge(s_gain, 32)
            def copy_mT(i, j):
                dve.wait_ge(c_tp, i * 2 + (j + 1))
                dve.wait_ge(c_acc, i * 4 + (2 * j + 2))
                dve.wait_ge(c_mT_act, i * 2 + (j + 2))
                dve.tensor_tensor(mT_lo[j % 2][:, :, :], banks(0, 2).rearrange("p (a b) -> p a b", a=KD),
                                  mT_hi[j % 2][:, :, :].bitcast(F32), ALU.subtract).then_inc(c_mT_dve, 1)

            def residual(i, j, halves=(0, 1)):
                for n in halves:
                    half = h2[:, bass.ds(i * 2 + j, 1), n * BANK:(n + 1) * BANK].rearrange("p a b -> p (a b)")
                    dve.wait_ge(c_acc, i * 4 + (2 * j + n + 5))
                    dve.tensor_tensor(half, psum[:, 2 + n, :], half, ALU.add).then_inc(c_h2, 1)

            def copy_fT(i, j):
                dve.wait_ge(c_ftp, i * 2 + (j + 1))
                dve.tensor_copy(fT[:, 4:8, :], psum[:, 5, :].rearrange("p (a b) -> p a b", a=4)).then_inc(c_fT_dve, 1)

            def second_norm(i, j):
                dve.wait_ge(c_sq, i * 2 + (j + 2))
                dve.tensor_scalar(ms[:, bass.ds(i * 2 + j, 1)], ss[:, bass.ds(i * 2 + j, 1)], 1.0 / D, EPS, ALU.mult,
                                  ALU.add).then_inc(c_ms, 1)
                dve.wait_ge(c_rstd, i * 2 + (j + 1))
                dve.wait_ge(c_fsaved, i * 32 + 16 * (j + 1))
                dve.scalar_tensor_tensor(f_buf[:, j % 2, :], row(h2, i, j), rstd[:, bass.ds(i * 2 + j, 1)],
                                         attn_gain[:, :], ALU.mult, ALU.mult).then_inc(c_f, 1)

            def router_logits(i, j):
                dve.wait_ge(c_lg, i * 2 + (j + 1))
                dve.tensor_tensor(row(logits, i, j), psum[:, 6, 0:NR], b_r[:, :], ALU.add).then_inc(c_logits, 1)

            copy_mT(0, 0)
            copy_mT(0, 1)
            dve.wait_ge(s_x_again[0], 16)
            residual(0, 0)
            second_norm(0, 0)
            dve.wait_ge(s_x_again[1], 16)
            with dve.Fori(0, T // 2 - 1) as i:
                for j in (1, 2):
                    copy_mT(i, j + 1)
                    residual(i, j, (0,))
                    copy_fT(i, j - 1)
                    residual(i, j, (1,))
                    second_norm(i, j)
                    router_logits(i, j - 1)
            residual(T // 2 - 1, 1, (0,))
            copy_fT(T // 2 - 1, 0)
            residual(T // 2 - 1, 1, (1,))
            second_norm(T // 2 - 1, 1)
            router_logits(T // 2 - 1, 0)
            copy_fT(T // 2 - 1, 1)
            router_logits(T // 2 - 1, 1)

            steps = [0]

            def step(ins, told=None):
                if told is not None:
                    ins.then_inc(told, 1)
                    dve.wait_ge(told, 1)
                else:
                    steps[0] += 1
                    ins.then_inc(r_dve, 1)
                    dve.wait_ge(r_dve, steps[0])

            def over(ap, axis, n):
                dims = [list(d) for d in ap.ap]
                return bass.AP(ap.tensor, ap.offset, dims[:1 + axis] + [[0, n]] + dims[1 + axis:])

            def low_unit(u, i):
                dve.wait_ge(unit_hi, i + 1)
                dve.tensor_tensor(unit_lo_w[u][:, :, :], unit_in[u], unit_hi_w[u][:, :, :].bitcast(F32), ALU.subtract) \
                    .then_inc(unit_lo, 1)

            dve.wait_ge(c_logits, T + 1)
            step(dve.memset(g8[:, :, :], LOWEST))
            step(dve.tensor_copy(g8[:, :, 0:NG], logits[:, :, 0:NG]))
            for t in range(T):
                last = dve.max(g_top[:, t, :], g8[:, t, :])
            step(last)
            for t in range(T):
                last = dve.max_index(g_idx[:, t, :], g_top[:, t, :], g8[:, t, :])
            step(last)
            step(dve.tensor_tensor(g_exp[:, :, :], logits[:, :, 0:NG], over(g_top[:, :, 0], 1, NG), ALU.subtract), r_gexp_in)
            step(dve.tensor_copy(g_sel[:, :], g_idx[:, :, 0]))
            step(dve.tensor_tensor(g_hot[:, :, :], over(iota_f[:, 0:NG], 0, T), over(g_sel[:, :], 1, NG), ALU.is_equal))
            step(dve.tensor_tensor(e_all[:, :, :, :], logits[:, :, NG:NR].rearrange("p t (g e) -> p t g e", g=NG),
                                   over(g_hot[:, :, :], 2, EG), ALU.mult))
            step(dve.tensor_reduce(e8[:, :, :], e_all[:, :, :, :].rearrange("p t g e -> p t e g"), AX.X, ALU.add))
            for t in range(T):
                last = dve.max(e_top[:, t, :], e8[:, t, :])
            step(last)
            for t in range(T):
                last = dve.max_index(e_idx[:, t, :], e_top[:, t, :], e8[:, t, :])
            step(last)
            step(dve.tensor_tensor(e_gap[:, :], e_top[:, :, 1], e_top[:, :, 0], ALU.subtract), r_esec_in)
            step(dve.tensor_copy(e_idf[:, :, :], e_idx[:, :, 0:TOP]))
            step(dve.scalar_tensor_tensor(eid[:, :, :], over(g_sel[:, :], 1, TOP), float(EG), e_idf[:, :, :], ALU.mult,
                                          ALU.add))
            for c in range(TOP):
                step(dve.tensor_tensor(hot[:, c, :, :], over(iota_f[:, 0:NE], 0, T), over(eid[:, :, c], 1, NE),
                                       ALU.is_equal))
            step(dve.tensor_tensor(hot_sum[:, :, :], hot[:, 0, :, :], hot[:, 1, :, :], ALU.add), r_hot)
            dve.wait_ge(r_gexp, 1)
            step(dve.tensor_reduce(g_sum[:, :], g_exp[:, :, :], AX.X, ALU.add))
            step(dve.reciprocal(g_w[:, :], g_sum[:, :]))
            dve.wait_ge(r_esec, 1)
            step(dve.tensor_scalar(e_den[:, :], e_sec[:, :], 1.0, None, ALU.add))
            step(dve.reciprocal(e_inv[:, :], e_den[:, :]))
            step(dve.tensor_tensor(gates[:, :, 0], g_w[:, :], e_inv[:, :], ALU.mult))
            step(dve.tensor_tensor(gates[:, :, 1], gates[:, :, 0], e_sec[:, :], ALU.mult))
            dve.wait_ge(r_counted, 1)
            step(dve.tensor_scalar(cnt_i[:, :], psum[:, 1, 0:NE], float(P - 1), None, ALU.add))
            step(dve.tensor_scalar(cnt_i[:, :], cnt_i[:, :], 7, None, ALU.arith_shift_right))
            step(dve.tensor_scalar(nblk[:, :], cnt_i[:, :], 1.0, None, ALU.max))
            step(dve.tensor_tensor_scan(blk_end[:, :], ones[:, 0:1].to_broadcast([P, NE]), nblk[:, :], 0.0, ALU.mult,
                                        ALU.add))
            step(dve.tensor_tensor(blk_start[:, :], blk_end[:, :], nblk[:, :], ALU.subtract))
            ranks = psum[:, 0, 0:T * NE].rearrange("p (t e) -> p t e", t=T)
            for c in range(TOP):
                step(dve.tensor_tensor(picked[:, c, :, :], ranks, hot[:, c, :, :], ALU.mult))
            step(dve.tensor_reduce(rank[:, :, :], picked[:, :, :, :], AX.X, ALU.add))
            for c in range(TOP):
                step(dve.tensor_tensor(picked[:, c, :, :], over(blk_start[:, :], 0, T), hot[:, c, :, :], ALU.mult))
            step(dve.tensor_reduce(first_blk[:, :, :], picked[:, :, :, :], AX.X, ALU.add))
            step(dve.tensor_copy(rank_i[:, :, :], rank[:, :, :]))
            step(dve.tensor_scalar(hi_i[:, :, :], rank_i[:, :, :], 7, None, ALU.arith_shift_right))
            step(dve.tensor_scalar(lo_i[:, :, :], rank_i[:, :, :], P - 1, None, ALU.bitwise_and))
            step(dve.tensor_copy(hi_f[:, :, :], hi_i[:, :, :]))
            step(dve.tensor_copy(lo_f[:, :, :], lo_i[:, :, :]))
            step(dve.tensor_tensor(blk[:, :, :], first_blk[:, :, :], hi_f[:, :, :], ALU.add))
            for c in range(TOP):
                step(dve.tensor_tensor(pos_hot[:, c, :, :], over(iota_f[:, :], 0, T), over(lo_f[:, c, :], 1, P),
                                       ALU.is_equal))
                step(dve.tensor_tensor(blk_hot[:, c, :, :], over(iota_f[:, 0:NB], 0, T), over(blk[:, c, :], 1, NB),
                                       ALU.is_equal))
                step(dve.tensor_scalar(blk_vals[:, c, :, 0, :], blk_hot[:, c, :, :], part_id[:, 0:1], None, ALU.mult))
                step(dve.tensor_tensor(blk_vals[:, c, :, 1, :], blk_hot[:, c, :, :], over(tile_id[:, :], 1, NB), ALU.mult))
                step(dve.tensor_scalar(blk_vals[:, c, :, 2, :], blk_hot[:, c, :, :], float(c), None, ALU.mult))
            for n in range(2):
                last = dve.tensor_scalar(last_i[0:1, n:n + 1], blk_end[0:1, NE - 1:NE], float(n + 1), None, ALU.subtract)
            step(last, r_vals)
            low_unit(0, 0)
            dve.wait_ge(r_rows, 1)
            told = psum[:, 2, 0:3 * NB].rearrange("p (a b) -> p a b", a=3)
            step(dve.tensor_scalar(empty[:, :], told[:, 0, :], 0.0, 65536.0, ALU.is_equal, ALU.mult))
            step(dve.scalar_tensor_tensor(empty[:, :], told[:, 0, :], 1.0, empty[:, :], ALU.subtract, ALU.add))
            step(dve.scalar_tensor_tensor(row_f[:, 0, :], told[:, 1, :], float(P), empty[:, :], ALU.mult, ALU.add))
            step(dve.scalar_tensor_tensor(row_f[:, 1, :], told[:, 1, :], float(P), row_f[:, 0, :], ALU.mult, ALU.add))
            step(dve.scalar_tensor_tensor(row_f[:, 1, :], told[:, 2, :], float(P), row_f[:, 1, :], ALU.mult, ALU.add))
            step(dve.tensor_copy(row_i[:, :, :], row_f[:, :, :]), r_table)
            def low_xT(b):
                dve.wait_ge(xT_act, b + 1)
                dve.tensor_tensor(xT_lo[:, :, :], banks(4, 2).rearrange("p (a b) -> p a b", a=KD),
                                  xT_hi[:, :, :].bitcast(F32), ALU.subtract).then_inc(xT_dve, 1)

            def low_hT(b):
                dve.wait_ge(hT_high, b + 1)
                dve.tensor_tensor(hT_lo[:, :, :], psum[:, 6, :].rearrange("p (a b) -> p a b", a=KE),
                                  hT_hi[:, :, :].bitcast(F32), ALU.subtract).then_inc(hT_ready, 1)

            def hidden(b):
                dve.wait_ge(unit_used, b * UNITS + 4)
                dve.wait_ge(silu_ready, b + 1)
                dve.tensor_tensor(hid, silu, psum[:, 1, :], ALU.mult).then_inc(h_ready, 1)

            def copy_y(b, i, first=False):
                dve.wait_ge(unit_used, i + 1)
                if not first:
                    dve.wait_ge(y_stored, b * 16)
                dve.tensor_copy(y_sb[:, BANK:2 * BANK], psum[:, 3, :]).then_inc(y_dve, 1)

            def pass_of(b, first=False, final=False):
                low_hT(b)
                low_unit(4, b * UNITS + (UNITS + 4))
                low_unit(5, b * UNITS + (UNITS + 5))
                if not final:
                    low_unit(0, b * UNITS + 2 * UNITS)
                hidden(b + 1)
                if not final:
                    low_unit(1, b * UNITS + (2 * UNITS + 1))
                low_xT(b + 2)
                if not final:
                    low_unit(2, b * UNITS + (2 * UNITS + 2))
                copy_y(b, b * UNITS + (UNITS + 5), first)
                if not final:
                    low_unit(3, b * UNITS + (2 * UNITS + 3))

            low_unit(1, 1)
            step(dve.tensor_tensor(be_cmp[:, :, :], over(blk_end[0:1, :], 0, NB), over(iota_f[0:1, 0:NB], 1, NE), ALU.is_le))
            step(dve.tensor_reduce(be_f[:, :], be_cmp[:, :, :], AX.X, ALU.add))
            step(dve.tensor_scalar(be_i[:, :], be_f[:, :], float(NE - 1), None, ALU.min), r_idx)
            last_b = dve.value_load(last_i[0:1, 0:1], min_val=NE - 1, max_val=NB - 2)
            before_last = dve.value_load(last_i[0:1, 1:2], min_val=NE - 2, max_val=NB - 3)
            low_xT(0)
            low_unit(2, 2)
            low_unit(3, 3)
            dve.wait_ge(unit_lo, 4)
            dve.sem_inc(unit_lo, 2)
            low_unit(0, UNITS)
            hidden(0)
            low_unit(1, UNITS + 1)
            low_xT(1)
            low_unit(2, UNITS + 2)
            low_unit(3, UNITS + 3)
            pass_of(0, first=True)
            with dve.Fori(1, before_last) as b:
                pass_of(b)
            pass_of(before_last, final=True)
            low_hT(last_b)
            for n in range(2):
                low_unit(4 + n, last_b * UNITS + (UNITS + n))
            copy_y(last_b, last_b * UNITS + (UNITS + 1))

            for t in range(T):
                dve.wait_ge(s_y[t % 4], 16 * (t // 4 + 3))
                dve.scalar_tensor_tensor(h2[:, t, :], y_tiles[:, t, 0, :], gates[:, t, 0:1], h2[:, t, :], ALU.mult,
                                         ALU.add).then_inc(f_part, 1)
                dve.wait_ge(f_part, t + 1)
                dve.scalar_tensor_tensor(h2[:, t, :], y_tiles[:, t, 1, :], gates[:, t, 1:2], h2[:, t, :], ALU.mult,
                                         ALU.add).then_inc(f_out, 1)

        @block.gpsimd
        def _(pool):
            pool.sem_inc(c_fsaved, 32)
            pool.memset(ident[:, :], 0.0).then_inc(s_ident, 1)
            pool.wait_ge(s_ident, 1)
            pool.affine_select(out=ident[:, :], in_=ident[:, :], compare_op=ALU.not_equal, fill=1.0, base=0,
                               pattern=[[-1, P]], channel_multiplier=1).then_inc(s_ident, 1)
            pool.wait_ge(s_dve_const, 1)
            for t in range(T):
                pool.wait_ge(n_ms, t + 1)
                pool.tensor_tensor(rstd[:, t:t + 1], ms[:, t:t + 1], mhalf[:, 0:1], ALU.pow).then_inc(n_rstd, 1)
            pool.wait_ge(s_lines_in, 32)
            pool.memset(t5_sb[:, :], 0.0)
            pool.memset(ca_sb[:, :], 0.0).then_inc(s_ident, 1)
            pool.wait_ge(s_ident, 3)
            for lo, hi, bucket in t5_runs(-(S - 1), P):
                run = t5_sb[:, P - hi:P - lo]
                last = pool.tensor_scalar(run, run, lines_in[:, bucket:bucket + 1], None, ALU.add)
            last.then_inc(s_lines, 1)
            near = P + CLIP
            pool.tensor_scalar(ca_sb[:, near:CA_LINE], ca_sb[:, near:CA_LINE], lines_in[:, T5_BUCKETS:T5_BUCKETS + 1],
                               None, ALU.add)
            pool.tensor_copy(ca_sb[:, 0:near], lines_in[:, T5_BUCKETS:T5_BUCKETS + near][:, ::-1]) \
                .then_inc(s_lines, 1)
            pool.iota(iota_f[:, :], [[1, P]], base=0, channel_multiplier=0, allow_small_or_imprecise_dtypes=True)
            pool.iota(part_id[:, :], [[1, 1]], base=1, channel_multiplier=1, allow_small_or_imprecise_dtypes=True)
            pool.iota(tile_id[:, :], [[1, T]], base=0, channel_multiplier=0, allow_small_or_imprecise_dtypes=True)
            pool.memset(ones_b[:, :], 1.0).then_inc(s_ident, 1)
            pool.wait_ge(s_ident, 4)
            pool.affine_select(out=tri[:, :], in_=ones_b[:, :], compare_op=ALU.is_gt, fill=0.0, base=0,
                               pattern=[[1, P]], channel_multiplier=-1).then_inc(s_pool_const, 1)

            def stage_plain(a, p, n):
                first, stage = ((a.q, q_stage), (a.k, k_stage))[n]
                pool.tensor_copy(stage, proj[:, :, cols(first, p)]).then_inc(a.s["staged"], 1)

            def root_mean_squares(a, p):
                pool.wait_ge(a.s["qk_ms_ready"], p * 2 + 4)
                pool.tensor_tensor(qk_rstd[:, :, :], qk_ms[:, :, :], mhalf[:, :].rearrange("p (a b) -> p a b", a=2),
                                   ALU.pow).then_inc(a.s["qk_rstd_ready"], 1)

            def stage_normed(a, p, part_no):
                n, h = part_no // 2, part_no % 2
                first, stage = ((a.q, q_stage), (a.k, k_stage))[n]
                if part_no == 0:
                    pool.wait_ge(a.s["qk_rstd_ready"], p + 1)
                r = qk_rstd[:, n, h:2 * T:2]
                last = pool.tensor_tensor(stage[:, :, h * HEAD:(h + 1) * HEAD], proj[:, :, cols(first + h * HEAD, p, HEAD)],
                                          bass.AP(r.tensor, r.offset, [*[list(d) for d in r.ap], [0, HEAD]]), ALU.mult)
                if h == 1:
                    last.then_inc(a.s["staged"], 1)

            def keep_earlier(buf, t, wait, done, value):
                diag = work[:, buf, t * P:(t + 1) * P]
                wait_alone(pool, wait, value)
                pool.affine_select(out=diag, in_=diag, compare_op=ALU.is_gt, fill=0.0, base=0, pattern=[[-1, P]],
                                   channel_multiplier=1).then_inc(done, 1)

            pool.wait_ge(acc_act, (CH + 1) * T // 2)
            pool.wait_ge(acc_dve, (CH + 1) * T // 2)
            def sb_pair(p, after):
                for s in range(SB.units + 1):
                    if s < SB.units:
                        keep_earlier(2 + s % 2, s // 2, SBS["sp_ready"], SBS["sp_masked"], p * SB.units + (s + 1))
                    if s >= 1:
                        keep_earlier((s - 1) % 2, (s - 1) // 2, SBS["w_exp"], SBS["p_ready"], p * SB.units + s)
                    if s == 4:
                        pool.wait_ge(SBS["k_tp"], p + 1)
                    if after[0] is SB and s in (4, 6):
                        stage_plain(*after, s // 2 - 2)
                    if after[0] is DF and s == 9:
                        root_mean_squares(*after)
                    if after[0] is DF and 10 <= s < 14:
                        stage_normed(*after, s - 10)

            with pool.Fori(0, SB.pairs - 1) as p:
                sb_pair(p, (SB, p + 1))
            sb_pair(SB.pairs - 1, (DF, 0))

            pool.wait_ge(SBS["o_read"], 2 + SB.pairs * SB.results)
            def df_pair(p, after):
                for s in range(T + 4):
                    if 3 <= s < T + 3:
                        t = s - 3
                        pool.wait_ge(DFS["yd_ms_ready"], p * T + (t + 1))
                        pool.tensor_tensor(yd_rstd[:, t % 2:t % 2 + 1], yd_ms[:, t % 2:t % 2 + 1], mhalf[:, 0:1],
                                           ALU.pow).then_inc(DFS["yd_rstd_ready"], 1)
                    if s == 3:
                        pool.wait_ge(DFS["k_tp"], p + 1)
                        root_mean_squares(*after)
                    if 4 <= s < 8:
                        stage_normed(*after, s - 4)

            with pool.Fori(0, DF.pairs - 1) as p:
                df_pair(p, (DF, p + 1))
            df_pair(DF.pairs - 1, (CA, 0))
            pool.wait_ge(DFS["merged_ready"], DF.pairs * DF.results)
            with pool.Fori(0, CA.pairs - 1) as p:
                pool.wait_ge(CAS["k_tp"], p + 1)
                root_mean_squares(CA, p + 1)
                for n in range(4):
                    stage_normed(CA, p + 1, n)

            pool.wait_ge(CAS["o_read"], 2 + CA.pairs * CA.results)

            def stage_merged(i, j):
                pool.wait_ge(c_tp, i * 2 + (j - 1))
                pool.tensor_copy(m_stage[j % 2], merged[:, bass.ds(i * 2 + j, 1), :].rearrange("p a b -> p (a b)")) \
                    .then_inc(c_stage, 1)

            def inverse_root(i, j):
                pool.wait_ge(c_ms, i * 2 + (j + 1))
                pool.tensor_tensor(rstd[:, bass.ds(i * 2 + j, 1)], ms[:, bass.ds(i * 2 + j, 1)], mhalf[:, 0:1],
                                   ALU.pow).then_inc(c_rstd, 1)

            with pool.Fori(0, T // 2 - 1) as i:
                for j in range(2):
                    stage_merged(i, j + 2)
                    inverse_root(i, j)
            for j in range(2):
                inverse_root(T // 2 - 1, j)

            pool.wait_ge(c_h2, 2 * T + 2)
            pool.memset(xg, 0.0).then_inc(xg_zero, 1)
            pool.wait_ge(r_table, 1)
            pool.wait_ge(xg_zero, 1)
            pool.wait_ge(c_fsaved, 16 * T + 32)

            def gather(b):
                pool.tensor_copy(tok_col[:, :], row_i[:, 0, bass.ds(b, 1)]).then_inc(tok_ready, 1)
                wait_alone(pool, tok_ready, b + 1)
                pool.indirect_dma_start(out=xg, out_offset=None, in_=f_rows,
                                        in_offset=bass.IndirectOffsetOnAxis(ap=tok_col[:, 0:1], axis=0),
                                        bounds_check=S - 1, oob_is_err=False).then_inc(xg_landed, 16)

            def scatter(b):
                pool.wait_ge(y_act, b + 2)
                pool.wait_ge(y_dve, b + 2)
                pool.tensor_copy(row_col[:, :], row_i[:, 1, bass.ds(b, 1)]).then_inc(row_ready, 1)
                wait_alone(pool, row_ready, b + 1)
                pool.indirect_dma_start(out=y_rows, out_offset=bass.IndirectOffsetOnAxis(ap=row_col[:, 0:1], axis=0),
                                        in_=y_sb, in_offset=None, bounds_check=TOP * S - 1,
                                        oob_is_err=False).then_inc(y_stored, 16)

            last_b = pool.value_load(last_i[0:1, 0:1], min_val=NE - 1, max_val=NB - 2)
            gather(0)
            pool.wait_ge(x_tp, 1)
            gather(1)
            with pool.Fori(1, last_b + 1) as b:
                pool.wait_ge(x_tp, b + 1)
                gather(b + 1)
                scatter(b - 1)
            scatter(last_b)


_INS = ['x', 't5_bias', 'attn_norm', 'w_in', 'diff_qk_norm', 'diff_lambda', 'diff_subln', 'ca_qk_norm',
        'ca_rel_bias', 'w_out', 'ffn_norm', 'router_group_w', 'router_group_b', 'router_expert_w',
        'router_expert_b', 'expert_w_gate', 'expert_w_up', 'expert_w_down']
_OUTS = [((1, 1024, 1024), 'float32')]


def kernel(**inputs):
    import numpy as _np
    import concourse.bacc as _bacc
    from concourse import mybir as _mybir
    from concourse.bass_utils import run_bass_kernel_spmd as _run

    nc = _bacc.Bacc("TRN2", target_bir_lowering=False, num_devices=1)
    arrays, args = {}, []
    for name in _INS:
        a = _np.ascontiguousarray(inputs[name])
        arrays[f"in_{name}_dram"] = a
        args.append(nc.dram_tensor(f"in_{name}_dram", a.shape, _mybir.dt.from_np(a.dtype), kind="ExternalInput").ap())
    for i, (shape, dtype) in enumerate(_OUTS):
        dt = _mybir.dt.from_np(_np.dtype(dtype))
        args.append(nc.dram_tensor(f"out_{i}_dram", shape, dt, kind="ExternalOutput").ap())
    hybrid_block(nc, *args)
    r = _run(nc, [arrays], core_ids=[0])
    got = tuple(r.results[0][f"out_{i}_dram"] for i in range(len(_OUTS)))
    return got[0]
```
